# Optimizing a Trainium2 kernel written in Bass

```python
import math
import jax, jax.numpy as jnp
from jax import lax
import numpy as np

D_MODEL = 1024
BATCH = 1
SEQ = 128
DEPTH = 2
DEC_BATCH = 1
DEC_SEQ = 256
PAST_LEN = 128

GRID_W = 64
ROPE_THETA = 10000.0
NORM_EPS = 1e-6
BLOCK = 128
N_BRANCH = 4
BRANCH_W = D_MODEL // N_BRANCH
HEAD_DIM = 64
A_HEADS = BRANCH_W // HEAD_DIM
A_KV = A_HEADS // 2
B_HEADS = BRANCH_W // HEAD_DIM
B_KV = B_HEADS // 2
WINDOW = 128
SSM_INNER = BRANCH_W
SSM_HEAD_DIM = 64
SSM_HEADS = SSM_INNER // SSM_HEAD_DIM
SSM_GROUPS = 2
SSM_STATE = 64
SSM_CONV = 5
SSM_CHUNK = 128
CONV_CH = SSM_INNER + 2 * SSM_GROUPS * SSM_STATE
DIFF_HEADS = BRANCH_W // HEAD_DIM
DIFF_V_DIM = HEAD_DIM
DIFF_QK_DIM = HEAD_DIM // 2
N_EXPERTS = 16
EXPERT_FF = D_MODEL
EC_FACTOR = 2
PROJ_SIZES = (A_HEADS * HEAD_DIM, A_KV * HEAD_DIM, A_KV * HEAD_DIM,
              B_HEADS * HEAD_DIM, B_KV * HEAD_DIM, B_KV * HEAD_DIM,
              SSM_INNER, CONV_CH, 2 * SSM_HEADS,
              DIFF_HEADS * 2 * DIFF_QK_DIM, DIFF_HEADS * 2 * DIFF_QK_DIM, DIFF_HEADS * DIFF_V_DIM,
              N_BRANCH * D_MODEL)
N_IN = sum(PROJ_SIZES)

kernel_name = 'hybrid_diffusion_prefix_trunk_step'

F32 = jnp.float32

def rmsnorm(x, g):
    xf = x.astype(F32)
    y = xf * lax.rsqrt(jnp.mean(xf * xf, axis=-1, keepdims=True) + NORM_EPS)
    return (y * g.astype(F32)).astype(x.dtype)

def split_proj(p):
    idx = [int(i) for i in np.cumsum(PROJ_SIZES)[:-1]]
    return jnp.split(p, idx, axis=-1)

def axial_rope(x):
    S, d = x.shape[1], x.shape[-1]
    n = d // 4
    t = jnp.arange(S)
    rows = (t // GRID_W).astype(F32)
    cols = (t % GRID_W).astype(F32)
    inv = ROPE_THETA ** (-jnp.arange(n, dtype=F32) / n)
    ang = jnp.stack([rows[:, None] * inv, cols[:, None] * inv], axis=1)
    bshape = (1, S) + (1,) * (x.ndim - 3) + (2, n)
    cos = jnp.cos(ang).reshape(bshape)
    sin = jnp.sin(ang).reshape(bshape)
    xr = x.astype(F32).reshape(x.shape[:-1] + (2, 2, n))
    x1, x2 = xr[..., 0, :], xr[..., 1, :]
    out = jnp.stack([x1 * cos - x2 * sin, x2 * cos + x1 * sin], axis=-2)
    return out.reshape(x.shape).astype(x.dtype)

def dense_attention(q, k, v, sink=None):
    Bz, S, H, d = q.shape
    Hk = k.shape[2]
    G = H // Hk
    dv = v.shape[-1]
    nb = S // BLOCK
    scale = 1.0 / math.sqrt(d)
    qb = jnp.moveaxis(q.reshape(Bz, nb, BLOCK, Hk, G, d), 1, 0)

    def one(qblk):
        s = jnp.einsum('bqkgd,bskd->bkgqs', qblk, k).astype(F32) * scale
        if sink is not None:
            sk = jnp.broadcast_to(sink.astype(F32).reshape(1, Hk, G, 1, 1), s.shape[:-1] + (1,))
            s = jnp.concatenate([s, sk], axis=-1)
        p = jax.nn.softmax(s, axis=-1)
        if sink is not None:
            p = p[..., :-1]
        return jnp.einsum('bkgqs,bskd->bqkgd', p.astype(v.dtype), v)

    o = lax.map(one, qb)
    return jnp.moveaxis(o, 0, 1).reshape(Bz, S, H, dv)

def window_attention(q, k, v, kc, vc, sink):
    Bz, S, H, d = q.shape
    Hk = k.shape[2]
    G = H // Hk
    dv = v.shape[-1]
    nb = S // BLOCK
    W = 3 * BLOCK
    Lc = kc.shape[1]
    scale = 1.0 / math.sqrt(d)
    pad = ((0, 0), (BLOCK, BLOCK), (0, 0), (0, 0))
    kp = jnp.pad(k, pad).reshape(Bz, nb + 2, BLOCK, Hk, d)
    vp = jnp.pad(v, pad).reshape(Bz, nb + 2, BLOCK, Hk, dv)
    kw = jnp.concatenate([kp[:, :-2], kp[:, 1:-1], kp[:, 2:]], axis=2)
    vw = jnp.concatenate([vp[:, :-2], vp[:, 1:-1], vp[:, 2:]], axis=2)
    qb = q.reshape(Bz, nb, BLOCK, Hk, G, d)
    xs = (jnp.moveaxis(qb, 1, 0), jnp.moveaxis(kw, 1, 0), jnp.moveaxis(vw, 1, 0), jnp.arange(nb))

    def one(args):
        qblk, kblk, vblk, n = args
        qpos = n * BLOCK + jnp.arange(BLOCK)[:, None]
        kpos = (n - 1) * BLOCK + jnp.arange(W)[None, :]
        ok = (kpos >= 0) & (kpos < S) & (jnp.abs(qpos - kpos) <= WINDOW)
        s_loc = jnp.einsum('bqkgd,bskd->bkgqs', qblk, kblk).astype(F32) * scale
        s_loc = jnp.where(ok, s_loc, -jnp.inf)
        s_ctx = jnp.einsum('bqkgd,bskd->bkgqs', qblk, kc).astype(F32) * scale
        sk = jnp.broadcast_to(sink.astype(F32).reshape(1, Hk, G, 1, 1), s_loc.shape[:-1] + (1,))
        p = jax.nn.softmax(jnp.concatenate([s_loc, s_ctx, sk], axis=-1), axis=-1)
        o = jnp.einsum('bkgqs,bskd->bqkgd', p[..., :W].astype(v.dtype), vblk)
        return o + jnp.einsum('bkgqs,bskd->bqkgd', p[..., W:W + Lc].astype(v.dtype), vc)

    o = lax.map(one, xs)
    return jnp.moveaxis(o, 0, 1).reshape(Bz, S, H, dv)

def diff_attention(q, k, v, lam):
    Bz, S, H, _, dk = q.shape
    nb = S // BLOCK
    scale = 1.0 / math.sqrt(dk)
    qb = jnp.moveaxis(q.reshape(Bz, nb, BLOCK, H, 2, dk), 1, 0)

    def one(qblk):
        s = jnp.einsum('bqhmd,bshmd->bhmqs', qblk, k).astype(F32) * scale
        p = jax.nn.softmax(s, axis=-1)
        w = p[:, :, 0] - lam * p[:, :, 1]
        return jnp.einsum('bhqs,bshd->bqhd', w.astype(v.dtype), v)

    o = lax.map(one, qb)
    return jnp.moveaxis(o, 0, 1).reshape(Bz, S, H, v.shape[-1])

def dwconv_centred(u, w, b):
    C = u.shape[-1]
    K = w.shape[0]
    out = lax.conv_general_dilated(u, w[:, None, :].astype(u.dtype), window_strides=(1,),
                                   padding=[(K // 2, K // 2)],
                                   dimension_numbers=('NWC', 'WIO', 'NWC'),
                                   feature_group_count=C)
    return out + b.astype(u.dtype)

def ssd_chunked(x, la, Bm, Cm, h0):
    Bz, S, H, P = x.shape
    N = Bm.shape[-1]
    Q = SSM_CHUNK
    nc = S // Q
    xc = x.reshape(Bz, nc, Q, H, P)
    Bc = Bm.reshape(Bz, nc, Q, H, N)
    Cc = Cm.reshape(Bz, nc, Q, H, N)
    acs = jnp.cumsum(la.reshape(Bz, nc, Q, H), axis=2)
    causal = jnp.tril(jnp.ones((Q, Q), dtype=bool))
    seg = acs[:, :, :, None, :] - acs[:, :, None, :, :]
    decay = jnp.exp(jnp.where(causal[:, :, None], seg, -jnp.inf))
    scores = jnp.einsum('bclhn,bcshn->bclsh', Cc, Bc) * decay
    y_diag = jnp.einsum('bclsh,bcshp->bclhp', scores, xc)
    to_end = jnp.exp(acs[:, :, -1:, :] - acs)
    states = jnp.einsum('bclhn,bclh,bclhp->bchpn', Bc, to_end, xc)
    chunk_decay = jnp.exp(acs[:, :, -1, :])

    def step(hs, inp):
        s, dcy = inp
        return hs * dcy[:, :, None, None] + s, hs

    h_fin, h_in = lax.scan(step, h0.astype(F32),
                           (jnp.moveaxis(states, 1, 0), jnp.moveaxis(chunk_decay, 1, 0)))
    h_in = jnp.moveaxis(h_in, 0, 1)
    y_off = jnp.einsum('bclhn,bchpn->bclhp', Cc, h_in) * jnp.exp(acs)[..., None]
    return (y_diag + y_off).reshape(Bz, S, H, P), h_fin

def ssd_mixer(z, xbc, dt_raw, h0, lp):
    Bz, S, _ = xbc.shape
    u = jax.nn.silu(dwconv_centred(xbc, lp['conv_w'], lp['conv_b']))
    xs, Bm, Cm = jnp.split(u, [SSM_INNER, SSM_INNER + SSM_GROUPS * SSM_STATE], axis=-1)
    rep = SSM_HEADS // SSM_GROUPS
    xs = xs.reshape(Bz, S, SSM_HEADS, SSM_HEAD_DIM).astype(F32)
    Bm = jnp.repeat(Bm.reshape(Bz, S, SSM_GROUPS, SSM_STATE), rep, axis=2).astype(F32)
    Cm = jnp.repeat(Cm.reshape(Bz, S, SSM_GROUPS, SSM_STATE), rep, axis=2).astype(F32)
    dt = jax.nn.softplus(dt_raw.reshape(Bz, S, 2, SSM_HEADS).astype(F32) + lp['dt_bias'].astype(F32))
    A = -jnp.exp(lp['a_log'].astype(F32))
    xdt = xs[:, :, None] * dt[..., None]
    la = dt * A
    fl = lambda t: jnp.flip(t, axis=1)
    y_f, h_f = ssd_chunked(xdt[:, :, 0], la[:, :, 0], Bm, Cm, h0[:, 0])
    y_b, h_b = ssd_chunked(fl(xdt[:, :, 1]), fl(la[:, :, 1]), fl(Bm), fl(Cm), h0[:, 1])
    y = y_f + fl(y_b) + xs * lp['d_skip'].astype(F32)[:, None]
    y = y.reshape(Bz, S, SSM_INNER) * jax.nn.silu(z.astype(F32))
    return rmsnorm(y, lp['g_ssm']).astype(z.dtype), jnp.stack([h_f, h_b], axis=1)

def token_mixers(h, lp, li, ctx):
    Bz, S, _ = h.shape
    latent = ctx is not None
    proj = jnp.einsum('bsd,dn->bsn', h, lp['w_in'])
    (a_q, a_k, a_v, b_q, b_k, b_v, c_z, c_xbc, c_dt, d_q, d_k, d_v, gate) = split_proj(proj)
    qa = rmsnorm(a_q.reshape(Bz, S, A_HEADS, HEAD_DIM), lp['g_qa'])
    ka = rmsnorm(a_k.reshape(Bz, S, A_KV, HEAD_DIM), lp['g_ka'])
    va = a_v.reshape(Bz, S, A_KV, HEAD_DIM)
    qb = rmsnorm(b_q.reshape(Bz, S, B_HEADS, HEAD_DIM), lp['g_qb'])
    kb = rmsnorm(b_k.reshape(Bz, S, B_KV, HEAD_DIM), lp['g_kb'])
    vb = b_v.reshape(Bz, S, B_KV, HEAD_DIM)
    qd = rmsnorm(d_q.reshape(Bz, S, DIFF_HEADS, 2, DIFF_QK_DIM), lp['g_qd'])
    kd = rmsnorm(d_k.reshape(Bz, S, DIFF_HEADS, 2, DIFF_QK_DIM), lp['g_kd'])
    vd = d_v.reshape(Bz, S, DIFF_HEADS, DIFF_V_DIM)
    if latent:
        qa, ka, qb, kb, qd, kd = [axial_rope(t) for t in (qa, ka, qb, kb, qd, kd)]
        ya = dense_attention(qa, jnp.concatenate([ka, ctx['a_k'].astype(ka.dtype)], axis=1),
                             jnp.concatenate([va, ctx['a_v'].astype(va.dtype)], axis=1))
        yb = window_attention(qb, kb, vb, ctx['b_k'].astype(kb.dtype), ctx['b_v'].astype(vb.dtype),
                              lp['sink_b'])
        kd_all = jnp.concatenate([kd, ctx['d_k'].astype(kd.dtype)], axis=1)
        vd_all = jnp.concatenate([vd, ctx['d_v'].astype(vd.dtype)], axis=1)
        h0 = ctx['ssm']
    else:
        ya = dense_attention(qa, ka, va)
        yb = dense_attention(qb, kb, vb, sink=lp['sink_b'])
        kd_all, vd_all = kd, vd
        h0 = jnp.zeros((Bz, 2, SSM_HEADS, SSM_HEAD_DIM, SSM_STATE), F32)
    lam_init = 0.8 - 0.6 * math.exp(-0.3 * li)
    lam = (jnp.exp(jnp.sum(lp['lam_q1'].astype(F32) * lp['lam_k1'].astype(F32)))
           - jnp.exp(jnp.sum(lp['lam_q2'].astype(F32) * lp['lam_k2'].astype(F32))) + lam_init)
    yd = diff_attention(qd, kd_all, vd_all, lam)
    yd = rmsnorm(yd, lp['g_dout']) * (1.0 - lam_init)
    yc, h_fin = ssd_mixer(c_z, c_xbc, c_dt, h0, lp)
    branches = jnp.stack([ya.reshape(Bz, S, BRANCH_W), yb.reshape(Bz, S, BRANCH_W),
                          yc, yd.reshape(Bz, S, BRANCH_W)], axis=2)
    up = jnp.einsum('bsnw,nwd->bsnd', branches, lp['w_br'])
    g = jax.nn.sigmoid(gate.reshape(Bz, S, N_BRANCH, D_MODEL))
    out = jnp.einsum('bsd,de->bse', jnp.sum(g * up, axis=2), lp['w_out'])
    new_ctx = None if latent else dict(a_k=ka, a_v=va, b_k=kb, b_v=vb, ssm=h_fin, d_k=kd, d_v=vd)
    return out, new_ctx

def expert_choice_ffn(x, w_router, w1, w3, w2):
    Bz, T, D = x.shape
    cap = EC_FACTOR * T // N_EXPERTS
    aff = jax.nn.softmax(jnp.einsum('btd,de->bte', x, w_router).astype(F32), axis=-1)
    gval, idx = lax.top_k(jnp.swapaxes(aff, 1, 2), cap)
    xs = jax.vmap(lambda xb, ib: xb[ib])(x, idx)
    hid = jax.nn.silu(jnp.einsum('becd,edf->becf', xs, w1)) * jnp.einsum('becd,edf->becf', xs, w3)
    yo = jnp.einsum('becf,efd->becd', hid, w2) * gval[..., None].astype(x.dtype)
    return jax.vmap(lambda ib, yb: jnp.zeros((T, D), yb.dtype).at[ib.reshape(-1)].add(yb.reshape(-1, D)))(idx, yo)

def adaln(cvec, w, b):
    m = jnp.einsum('bd,dn->bn', jax.nn.silu(cvec), w) + b
    return m.reshape(m.shape[0], 6, D_MODEL)

def trunk_layer(x, mod, lp, li, ctx):
    shift1, scale1, gate1, shift2, scale2, gate2 = [mod[:, i, None, :] for i in range(6)]
    h = rmsnorm(x, lp['g_norm1']) * (1 + scale1) + shift1
    mix, new_ctx = token_mixers(h, lp, li, ctx)
    x = x + gate1 * mix
    h2 = rmsnorm(x, lp['g_norm2']) * (1 + scale2) + shift2
    x = x + gate2 * expert_choice_ffn(h2, lp['w_router'], lp['w_e1'], lp['w_e3'], lp['w_e2'])
    return x, new_ctx

def setup_inputs(seed: int = 0) -> dict:
    key = jax.random.key(seed)
    ks = iter(jax.random.split(key, 64))
    nrm = lambda shape, s: jax.random.normal(next(ks), shape, F32) * s
    gain = lambda shape: 1.0 + 0.02 * jax.random.normal(next(ks), shape, F32)
    inp = {}
    inp['x_prompt'] = nrm((BATCH, SEQ, D_MODEL), 1.0)
    inp['x_sample'] = nrm((DEC_BATCH, DEC_SEQ, D_MODEL), 1.0)
    inp['c'] = nrm((DEC_BATCH, D_MODEL), 1.0)
    inp['cache_a_k'] = nrm((DEC_BATCH, DEPTH, PAST_LEN, A_KV, HEAD_DIM), 1.0)
    inp['cache_a_v'] = nrm((DEC_BATCH, DEPTH, PAST_LEN, A_KV, HEAD_DIM), 1.0)
    inp['cache_b_k'] = nrm((DEC_BATCH, DEPTH, PAST_LEN, B_KV, HEAD_DIM), 1.0)
    inp['cache_b_v'] = nrm((DEC_BATCH, DEPTH, PAST_LEN, B_KV, HEAD_DIM), 1.0)
    inp['state_ssm'] = nrm((DEC_BATCH, DEPTH, 2, SSM_HEADS, SSM_HEAD_DIM, SSM_STATE), 0.1)
    inp['cache_d_k'] = nrm((DEC_BATCH, DEPTH, PAST_LEN, DIFF_HEADS, 2, DIFF_QK_DIM), 1.0)
    inp['cache_d_v'] = nrm((DEC_BATCH, DEPTH, PAST_LEN, DIFF_HEADS, DIFF_V_DIM), 1.0)
    inp['c_ctx'] = nrm((D_MODEL,), 1.0)
    inp['w_ada'] = nrm((DEPTH, D_MODEL, 6 * D_MODEL), 0.5 * D_MODEL ** -0.5)
    inp['b_ada'] = nrm((DEPTH, 6 * D_MODEL), 0.02)
    inp['g_norm1'] = gain((DEPTH, D_MODEL))
    inp['g_norm2'] = gain((DEPTH, D_MODEL))
    inp['w_in'] = nrm((DEPTH, D_MODEL, N_IN), D_MODEL ** -0.5)
    inp['g_qa'] = gain((DEPTH, HEAD_DIM))
    inp['g_ka'] = gain((DEPTH, HEAD_DIM))
    inp['g_qb'] = gain((DEPTH, HEAD_DIM))
    inp['g_kb'] = gain((DEPTH, HEAD_DIM))
    inp['sink_b'] = nrm((DEPTH, B_HEADS), 0.5)
    inp['conv_w'] = nrm((DEPTH, SSM_CONV, CONV_CH), SSM_CONV ** -0.5)
    inp['conv_b'] = nrm((DEPTH, CONV_CH), 0.02)
    dt0 = jnp.exp(jax.random.uniform(next(ks), (DEPTH, 2, SSM_HEADS), F32,
                                     minval=math.log(1e-3), maxval=math.log(1e-1)))
    inp['dt_bias'] = dt0 + jnp.log(-jnp.expm1(-dt0))
    inp['a_log'] = jnp.log(jax.random.uniform(next(ks), (DEPTH, 2, SSM_HEADS), F32, minval=1.0, maxval=16.0))
    inp['d_skip'] = 1.0 + 0.1 * jax.random.normal(next(ks), (DEPTH, SSM_HEADS), F32)
    inp['g_ssm'] = gain((DEPTH, SSM_INNER))
    inp['g_qd'] = gain((DEPTH, DIFF_QK_DIM))
    inp['g_kd'] = gain((DEPTH, DIFF_QK_DIM))
    inp['lam_q1'] = nrm((DEPTH, DIFF_QK_DIM), 0.1)
    inp['lam_k1'] = nrm((DEPTH, DIFF_QK_DIM), 0.1)
    inp['lam_q2'] = nrm((DEPTH, DIFF_QK_DIM), 0.1)
    inp['lam_k2'] = nrm((DEPTH, DIFF_QK_DIM), 0.1)
    inp['g_dout'] = gain((DEPTH, DIFF_V_DIM))
    inp['w_br'] = nrm((DEPTH, N_BRANCH, BRANCH_W, D_MODEL), BRANCH_W ** -0.5)
    inp['w_out'] = nrm((DEPTH, D_MODEL, D_MODEL), D_MODEL ** -0.5)
    inp['w_router'] = nrm((DEPTH, D_MODEL, N_EXPERTS), D_MODEL ** -0.5)
    inp['w_e1'] = nrm((DEPTH, N_EXPERTS, D_MODEL, EXPERT_FF), D_MODEL ** -0.5)
    inp['w_e3'] = nrm((DEPTH, N_EXPERTS, D_MODEL, EXPERT_FF), D_MODEL ** -0.5)
    inp['w_e2'] = nrm((DEPTH, N_EXPERTS, EXPERT_FF, D_MODEL), EXPERT_FF ** -0.5)
    return inp

def reference(x_prompt, x_sample, c, cache_a_k, cache_a_v, cache_b_k, cache_b_v, state_ssm,
              cache_d_k, cache_d_v, c_ctx, w_ada, b_ada, g_norm1, g_norm2, w_in, g_qa, g_ka,
              g_qb, g_kb, sink_b, conv_w, conv_b, dt_bias, a_log, d_skip, g_ssm, g_qd, g_kd,
              lam_q1, lam_k1, lam_q2, lam_k2, g_dout, w_br, w_out, w_router, w_e1, w_e3, w_e2):
    xp = x_prompt
    xl = x_sample
    new_a_k, new_a_v, new_b_k, new_b_v, new_ssm, new_d_k, new_d_v = [], [], [], [], [], [], []
    for li in range(DEPTH):
        lp = dict(g_norm1=g_norm1[li], g_norm2=g_norm2[li], w_in=w_in[li], g_qa=g_qa[li],
                  g_ka=g_ka[li], g_qb=g_qb[li], g_kb=g_kb[li], sink_b=sink_b[li],
                  conv_w=conv_w[li], conv_b=conv_b[li], dt_bias=dt_bias[li], a_log=a_log[li],
                  d_skip=d_skip[li], g_ssm=g_ssm[li], g_qd=g_qd[li], g_kd=g_kd[li],
                  lam_q1=lam_q1[li], lam_k1=lam_k1[li], lam_q2=lam_q2[li], lam_k2=lam_k2[li],
                  g_dout=g_dout[li], w_br=w_br[li], w_out=w_out[li], w_router=w_router[li],
                  w_e1=w_e1[li], w_e3=w_e3[li], w_e2=w_e2[li])
        mod_ctx = adaln(c_ctx[None, :], w_ada[li], b_ada[li])
        mod_lat = adaln(c, w_ada[li], b_ada[li])
        xp, ctx_new = trunk_layer(xp, mod_ctx, lp, li, None)
        new_a_k.append(ctx_new['a_k'])
        new_a_v.append(ctx_new['a_v'])
        new_b_k.append(ctx_new['b_k'])
        new_b_v.append(ctx_new['b_v'])
        new_ssm.append(ctx_new['ssm'])
        new_d_k.append(ctx_new['d_k'])
        new_d_v.append(ctx_new['d_v'])
        ctx_cached = dict(a_k=cache_a_k[:, li], a_v=cache_a_v[:, li], b_k=cache_b_k[:, li],
                          b_v=cache_b_v[:, li], ssm=state_ssm[:, li], d_k=cache_d_k[:, li],
                          d_v=cache_d_v[:, li])
        xl, _ = trunk_layer(xl, mod_lat, lp, li, ctx_cached)
    out_a_k = jnp.stack(new_a_k, axis=1)
    out_a_v = jnp.stack(new_a_v, axis=1)
    out_b_k = jnp.stack(new_b_k, axis=1)
    out_b_v = jnp.stack(new_b_v, axis=1)
    out_ssm = jnp.stack(new_ssm, axis=1)
    out_d_k = jnp.stack(new_d_k, axis=1)
    out_d_v = jnp.stack(new_d_v, axis=1)
    return (xp, xl, out_a_k, out_a_v, out_b_k, out_b_v, out_ssm, out_d_k, out_d_v)


_drawn_inputs = setup_inputs


def setup_inputs(seed=0):
    import zlib

    import numpy as np

    out = dict(_drawn_inputs(seed))
    spreads = {}
    factors = {'cache_a_k': 5.061,
     'cache_a_v': 4.556,
     'cache_b_k': 4.658,
     'cache_b_v': 3.833,
     'g_norm2': 5.992,
     'g_qa': 8.0,
     'g_ka': 2.849,
     'g_qb': 8.0,
     'g_kb': 2.872,
     'sink_b': 8.0,
     'd_skip': 2.895,
     'g_ssm': 8.0,
     'g_qd': 8.0,
     'g_kd': 2.678,
     'lam_q1': 6.672,
     'lam_k1': 7.086,
     'lam_q2': 7.541,
     'lam_k2': 7.153,
     'g_dout': 8.0,
     'cache_d_k': 8.0,
     'cache_d_v': 8.0}
    for name, (base, spread) in spreads.items():
        noise = np.random.default_rng([zlib.crc32(name.encode()), seed]).standard_normal(out[name].shape)
        drawn = base * np.exp(spread * noise) if base else spread * noise
        out[name] = __import__('jax').numpy.asarray(drawn.astype(out[name].dtype))
    for name, factor in factors.items():
        out[name] = (out[name] * factor).astype(out[name].dtype)
    return out
```

```python
from contextlib import ExitStack

import concourse.bass as bass
from concourse import mybir

P = 128
D = 1024
KD = D // P
NT = 3
T = NT * P
DEPTH = 2
HD = 64
NE = 16
CAP = (16, 32)
CE = CAP[0] + CAP[1]
EPS = 1e-6
HALF = 512
SLOTS = 4
LOADS0 = 32
LOADS = LOADS0 + NE * 6
PER_SLOT = LOADS // SLOTS
BRANCH = (0, 1, 3, 2)
COL_A, COL_B, COL_C, COL_D, COL_G = 0, 512, 1024, 1800, 2568
NC_ = 776
ND_ = 768
PADW = 392
NU_CONV = PADW - 4
LAT0 = 132

F32 = mybir.dt.float32
ACT = mybir.ActivationFunctionType
ALU = mybir.AluOpType
AX = mybir.AxisListType

ROW = {}
_at = 0
for _name, _n in (("gq", 128), ("gk", 128), ("gqd", 32), ("gkd", 32), ("gdout", 64), ("lamq", 64), ("lamk", 64),
                  ("sink", 4), ("alog", 8), ("dtb", 8), ("dskip", 4), ("gssm", 256), ("laminit", 1), ("onemlam", 1)):
    ROW[_name] = (_at, _at + _n)
    _at += _n
NROW = _at
COLS = {"gn1": (0, 8), "gn2": (8, 16), "convw": (16, 36), "convb": (36, 40)}
NCOL = 40
CACHE = {"ak": (0, 128), "bk": (128, 256), "av": (256, 384), "bv": (384, 512), "dk": (512, 768), "dv": (768, 1024),
         "ssm": (1024, 1280)}
NCACHE = 1280
CST = {}
_at = 0
for _name, _n in (("ident", 128), ("upto", 128), ("from", 128), ("negbelow", 128), ("negabove", 128), ("ones", 128),
                  ("sel", 2), ("selb", 256), ("iota", 128), ("bias1", 32), ("cos", 128), ("sin", 128),
                  ("cosd", 64), ("sind", 64), ("zero", 128)):
    CST[_name] = (_at, _at + _n)
    _at += _n
NCST = _at


def big_results():
    out = []
    for v in range(6):
        out += [(("row", v, h), "act") for h in range(2)]
        if v >= 1 and v - 1 in (0, 1, 3, 4):
            out.append((("col", v - 1), "dve"))
    out += [(("hT", k), "dve" if k % 2 else "act") for k in range(KD)]
    out += [(("ab", t, b), "act") for b in range(2) for t in range(NT)]
    for t in range(NT):
        out += [(("dqk", t), "act"), (("dv", t), "act")]
    out += [(("zdt", t), "act") for t in range(NT)]
    out += [(("xbc", g), "act") for g in range(4)]
    out += [(("g", 0, t, h), "act") for t in range(NT) for h in range(2)]
    out += [(("qkT", t, b), "act") for t in range(NT) for b in range(2)] + [(("ckT",), "act")]
    out += [(("dT", t), "act") for t in range(NT)] + [(("cdT",), "act")]
    for i in range(4):
        if i < 3:
            for s in range(6):
                out.append((("g", i + 1, s // 2, s % 2), "act"))
        else:
            out += [(("uT", t), "act") for t in range(NT)]
            out += [(("cum",), "dve"), (("h0T",), "act")]
            for t in range(NT):
                out += [(("dec", t, 0), "act"), (("dec", t, 1), "act"), (("GT", t, 0), "dve"), (("GT", t, 1), "dve")]
                out += [(("st", t), "dve" if t else "act"), (("y", t), "dve")]
            out += [(("yo", t, g), "dve") for t in (1, 2) for g in range(2)]
        out += [(("boT", i, k), "dve") for k in range(2)]
        out += [(("up", i, t, h), "dve") for t in range(NT) for h in range(2)]
    out += [(("mT", k), "dve" if k % 2 else "act") for k in range(KD)]
    out += [(("gb", g, h), "act") for g in range(2) for h in range(2)]
    out += [(("out", t, h), "dve") for t in range(NT) for h in range(2)]
    out += [(("h2T", k), "dve" if k % 2 else "act") for k in range(KD)]
    out += [(("lg",), "dve"), (("affT",), "act"), (("mk",), "act"), (("rank",), "dve")]
    for k in range(KD):
        out += [(("xc", k), "dve" if k % 2 else "act"), (("xl", k), "dve" if k % 2 else "act")]
    return out


BIG = big_results()
BIG_AT = {name: n for n, (name, _) in enumerate(BIG)}
BIG_BY = dict(BIG)


def taken_by(name):
    n = BIG_AT[name]
    by = BIG[n][1]
    return by, sum(1 for _, e in BIG[:n + 1] if e == by)


def trunk_kernel(nc, x_prompt, x_sample, cvecT, rowp, colp, caches, b_ada, w_ada, w_in, w_br, w_out, w_router,
                 w_e1, w_e3, w_e2, consts, y_prompt, y_sample, o_ak, o_av, o_bk, o_bv, o_ssm, o_dk, o_dv):
    with ExitStack() as ctx:
        def sb(name, shape):
            return ctx.enter_context(nc.sbuf_tensor(name, shape, F32))

        def sem(name):
            return ctx.enter_context(nc.semaphore(name))

        ring = sb("ring", [P, SLOTS, 4, D])
        x = sb("x", [P, NT, D])
        xn = sb("xn", [P, NT, D])
        hT = sb("hT", [P, KD, T])
        cst = sb("cst", [P, NCST])
        gaterow = sb("gaterow", [P, 2, D])
        rp = sb("rp", [P, NROW])
        cp = sb("cp", [P, NCOL])
        ca = sb("ca", [P, NCACHE])
        wr = sb("wr", [P, KD, NE])
        cs = sb("cs", [P, KD, 2])
        csw = sb("csw", [P, KD, 32])
        modc = sb("modc", [P, 4, KD, 2])
        gs = sb("gs", [P, 2, KD, 2])
        st = sb("st", [P, 6, 48])
        stw = sb("stw", [P, 48])
        dsm = sb("dsm", [P, 88])
        expa, lamd, lamx, nlam, nsink = dsm[:, 0:8], dsm[:, 8:10], dsm[:, 10:12], dsm[:, 12:13], dsm[:, 13:17]
        xmark = dsm[:, 17:18]
        lamt = dsm[:, 20:84]
        used = [0]
        SCR = 20520
        scr = sb("scr", [P, SCR])

        def at(off, n):
            assert off + n <= SCR
            return scr[:, off:off + n]

        def take(n):
            used[0] += n
            return at(used[0] - n, n)

        G = [take(NT * D).rearrange("p (t n) -> p t n", t=NT) for _ in range(2)]
        AB = take(2304).rearrange("p (t b n) -> p t b n", t=NT, b=2)
        qko = used[0]
        qT = take(2 * 2 * T).rearrange("p (b g t) -> p b g t", b=2, g=2)
        kT = take(2 * 512).rearrange("p (b t) -> p b t", b=2)
        dqT = take(2 * T).rearrange("p (c t) -> p c t", c=2)
        dkT = take(2 * 512).rearrange("p (c t) -> p c t", c=2)
        vab = take(NT * 256).rearrange("p (t b n) -> p t b n", t=NT, b=2)
        vd = take(NT * 256).rearrange("p (t n) -> p t n", t=NT)
        qkend = used[0]
        sz = take(NT * 256).rearrange("p (t n) -> p t n", t=NT)
        xbc = take(4 * PADW).rearrange("p (g n) -> p g n", g=4)
        uT = xbc[:, :, 0:T]
        bof = used[0]
        bo = take(NT * 256).rearrange("p (t n) -> p t n", t=NT)
        boT = take(2 * T).rearrange("p (c t) -> p c t", c=2)
        DQ = at(bof, NT * 512).rearrange("p (t n) -> p t n", t=NT)
        po = used[0]
        pr = take(2 * 768).rearrange("p (i n) -> p i n", i=2)
        pT = take(2 * T).rearrange("p (i n) -> p i n", i=2)
        tmp = at(po, 2 * 768).rearrange("p (i n) -> p i n", i=2)
        cacc = at(po, 4 * NU_CONV).rearrange("p (i n) -> p i n", i=4)
        so = [qko]

        def over(n):
            so[0] += n
            assert so[0] <= qkend
            return at(so[0] - n, n)

        xsB = over(NT * 384).rearrange("p (t n) -> p t n", t=NT)
        E = over(8 * P).rearrange("p (j l) -> p j l", j=8)
        Mt = over(8 * P).rearrange("p (j l) -> p j l", j=8)
        xdt = over(512).rearrange("p (d h n) -> p d h n", d=2, h=4)
        xde = over(512).rearrange("p (d h n) -> p d h n", d=2, h=4)
        hin = over(512).rearrange("p (i n) -> p i n", i=4)
        sst = over(256).rearrange("p (i n) -> p i n", i=4)
        sm = over(72).rearrange("p (i t j) -> p i t j", i=3, t=NT)
        ex = over(72).rearrange("p (i t j) -> p i t j", i=3, t=NT)
        nacs = over(24).rearrange("p (t j) -> p t j", t=NT)
        dtk = sb("dtk", [P, 5, 24])
        dtr, dt_, la = (dtk[:, i, :].rearrange("p (t j) -> p t j", t=NT) for i in range(3))
        dabs = dtk[:, 3, :].rearrange("p (t j) -> p t j", t=NT)
        dexp = dtk[:, 4, :].rearrange("p (t j) -> p t j", t=NT)
        brow = scr[0:1, 0:6 * D]
        rsb = at(6 * D, 2 * D).rearrange("p (i n) -> p i n", i=2)
        gbc = at(0, 2 * D).rearrange("p (g n) -> p g n", g=2)
        gtmp = at(2 * D, D).rearrange("p (i n) -> p i n", i=2)
        eo = [0]

        def exp_take(n):
            eo[0] += n
            return at(eo[0] - n, n)

        gbc2 = gbc
        eo[0] = 3 * D
        XT = exp_take(KD * 784).rearrange("p (k c) -> p k c", k=KD)
        Sc = exp_take(256).rearrange("p (e c) -> p e c", e=NE)
        Sl = exp_take(2 * 512).rearrange("p (i e c) -> p i e c", i=2, e=NE)
        xcur = exp_take(KD * 64).rearrange("p (k c) -> p k c", k=KD)
        sgs = exp_take(T).rearrange("p (t c) -> p t c", t=NT)
        sgT = exp_take(T).rearrange("p (t c) -> p t c", t=NT)
        hs = exp_take(HALF)
        hid = exp_take(HALF).rearrange("p (b n) -> p b n", b=4)
        hidT = exp_take(HALF).rearrange("p (b n) -> p b n", b=4)
        yo = exp_take(HALF)
        aff = exp_take(48).rearrange("p (t e) -> p t e", t=NT)
        pos = exp_take(48).rearrange("p (t e) -> p t e", t=NT)
        msk = exp_take(48).rearrange("p (t e) -> p t e", t=NT)
        affT = scr[0:NE, eo[0]:eo[0] + T]
        wrk = scr[0:NE, eo[0] + T:eo[0] + 2 * T]
        top8 = scr[0:NE, eo[0] + 2 * T:eo[0] + 2 * T + 8]
        maskT = scr[0:NE, eo[0] + 2 * T + 8:eo[0] + 3 * T + 8]
        assert eo[0] + 3 * T + 8 <= SCR

        banks = [ctx.enter_context(nc.psum_tensor(f"bank{i}", [P, 512], F32)) for i in range(8)]

        def c_(name):
            return cst[:, CST[name][0]:CST[name][1]]

        def r_(name):
            return rp[:, ROW[name][0]:ROW[name][1]]

        def ch(name):
            return ca[:, CACHE[name][0]:CACHE[name][1]]

        ident = c_("ident")
        gqc = r_("gq").rearrange("p (b n) -> p b n", b=2)
        gkc = r_("gk").rearrange("p (b n) -> p b n", b=2)

        def rep(ap, axis, n):
            a = ap.unsqueeze(axis)
            shape = list(a.shape)
            shape[axis] = n
            return a.broadcast_to(shape)

        loaded = [sem(f"loaded{i}") for i in range(SLOTS)]
        freed = [sem(f"freed{i}") for i in range(SLOTS)]
        in_x = sem("in_x")
        done_pe, done_act, done_dve, done_pool = (sem(f"done_{e}") for e in ("pe", "act", "dve", "pool"))
        layer_go = sem("layer_go")
        dummy, dummy_pe, dummy_act, dummy_dve, dummy_sp = (sem(f"passed_{e}") for e in ("pool", "pe", "act", "dve", "sp"))
        y_out = sem("y_out")
        params = sem("params")
        kv_out = sem("kv_out")
        ssm_out = sem("ssm_out")
        x_final = sem("x_final")
        layer_sems = []

        def lsem(name):
            layer_sems.append(sem(name))
            return layer_sems[-1]

        pads = lsem("pads")
        big = lsem("big_ready")
        big_act = lsem("big_taken_act")
        big_dve = lsem("big_taken_dve")
        big_of = {"act": big_act, "dve": big_dve}
        cond = lsem("cond_ready")
        mod1 = lsem("mod_ready")
        act_sq = lsem("squares_ready")
        sq_free = lsem("squares_used")
        var_ready = lsem("variance_ready")
        root_ready = lsem("root_ready")
        xn_ready = lsem("xn_ready")
        ab_ready = lsem("ab_ready")
        d_ready = lsem("d_ready")
        dt_abs = lsem("dt_abs")
        dt_log = lsem("dt_log")
        dt_done = lsem("dt_done")
        lam_dot = lsem("lam_dot")
        lam_exp = lsem("lam_exp")
        conv_sum = lsem("conv_sum")
        conv_out = lsem("conv_out")
        s_ready = lsem("scores_ready")
        m_ready = lsem("max_ready")
        aff_in = lsem("aff_in")
        aff_exp = lsem("aff_exp")
        w1hot = lsem("expert_hot")
        p_ready = lsem("probs_ready")
        w_ready = lsem("diffprobs_ready")
        pt_ready = lsem("probsT_ready")
        pts_ready = lsem("probsT_sbuf")
        pv_ready = lsem("pv_ready")
        o_ready = lsem("o_taken")
        bo_ready = lsem("branch_ready")
        merged = lsem("merged")
        ssd_small = lsem("ssd_small")
        ssd_exp = lsem("ssd_exp")
        mt_ready = lsem("mt_ready")
        h_in = lsem("h_in")
        x_ready = lsem("x_ready")
        aff_ready = lsem("aff_ready")
        mask_ready = lsem("mask_ready")
        mk_ready = lsem("mk_ready")
        hot_ready = lsem("hot_ready")
        xc_ready = lsem("xcur_ready")
        h3_ready = lsem("h3_ready")
        silu_ready = lsem("silu_ready")
        hid_ready = lsem("hid_ready")
        ht_ready = lsem("hidT_ready")
        hts_ready = lsem("hidT_sbuf")
        yp_ready = lsem("yo_psum")
        sg_ready = lsem("sgT_ready")
        sgs_ready = lsem("sgT_sbuf")
        yo_ready = lsem("yo_sbuf")
        gb2 = lsem("gate2_psum")
        gb2_sb = lsem("gate2_sbuf")
        act_step = lsem("act_step")
        dve_step = lsem("dve_step")
        numbers = sorted(s.num for s in layer_sems)
        assert numbers == list(range(numbers[0], numbers[0] + len(numbers)))

        def iters(i):
            return [(h, t) for h in range(4) for t in range(NT)]

        NIT = 12

        block = ctx.enter_context(nc.Block())

        @block.sync
        def _(sp):
            sp.dma_start(x[:, 0, :], x_prompt.rearrange("a s d -> (a s) d")).then_inc(in_x, 16)
            sp.dma_start(x[:, 1:3, :], x_sample.rearrange("a (t p) d -> p (a t) d", p=P)).then_inc(in_x, 16)
            sp.dma_start(cst[:, :], consts).then_inc(in_x, 16)
            sp.dma_start(cs[:, :, :], cvecT).then_inc(in_x, 16)

            def load(n, s, src, cols, chunks=4):
                sp.wait_ge(freed[s], n)
                sp.dma_start(ring[:, s, 0:chunks, 0:cols],
                             src.rearrange("(k p) n -> p k n", p=P)).then_inc(loaded[s], 16)

            with sp.Fori(0, DEPTH) as li:
                base = li * PER_SLOT
                plan = []
                for v in range(6):
                    plan += [(w_ada[li, h * HALF:(h + 1) * HALF, v * D:(v + 1) * D], D, 4) for h in range(2)]
                for c0, n in ((COL_A, D), (COL_D, ND_), (COL_C, NC_)):
                    plan += [(w_in[li, h * HALF:(h + 1) * HALF, c0:c0 + n], n, 4) for h in range(2)]
                for br in BRANCH:
                    c0 = COL_G + br * D
                    plan += [(w_in[li, h * HALF:(h + 1) * HALF, c0:c0 + D], D, 4) for h in range(2)]
                    plan.append((w_br[li, br, :, :], D, 2))
                plan += [(w_out[li, h * HALF:(h + 1) * HALF, :], D, 4) for h in range(2)]
                for j, (src, cols, chunks) in enumerate(plan):
                    load(base + j // SLOTS, j % SLOTS, src, cols, chunks)
                with sp.Fori(0, NE // 2) as ep:
                    for i in range(12):
                        w = (w_e1, w_e3, w_e2)[(i % 6) // 2]
                        h = i % 2
                        load(base + LOADS0 // SLOTS + ep * 3 + i // SLOTS, i % SLOTS,
                             w[li, ep * 2 + i // 6, h * HALF:(h + 1) * HALF, :], D)
                for s in (done_pe, done_act, done_dve, done_pool):
                    sp.wait_ge(s, li + 1)
                sp.sem_inc(dummy_sp, 1)
                sp.sem_clear(range(numbers[0], numbers[-1] + 1))
                sp.sem_inc(layer_go, 1)
            sp.wait_ge(x_final, 1)
            sp.dma_start(y_prompt.rearrange("a s d -> (a s) d"), x[:, 0, :]).then_inc(y_out, 16)
            sp.dma_start(y_sample.rearrange("a (t p) d -> p (a t) d", p=P), x[:, 1:3, :]).then_inc(y_out, 16)
            sp.wait_ge(y_out, 32)

        @block.gpsimd
        def _(pool):
            with pool.Fori(0, DEPTH) as li:
                pool.dma_start(rp[:, :], rowp[li, :].partition_broadcast(P)).then_inc(params, 16)
                pool.dma_start(cp[:, :], colp[li, :, :]).then_inc(params, 16)
                pool.dma_start(ca[:, :], caches[li, :, :]).then_inc(params, 16)
                pool.dma_start(brow, b_ada[li, :].unsqueeze(0)).then_inc(params, 16)
                pool.dma_start(wr[:, :, :], w_router[li, :, :].rearrange("(k p) e -> p k e", p=P)).then_inc(params, 16)
                pool.memset(csw[:, :, :], 0.0).then_inc(pads, 1)
                pool.wait_ge(big_act, taken_by(("row", 5, 1))[1])
                pool.memset(xbc[:, :, :], 0.0).then_inc(pads, 1)
                pool.wait_ge(ab_ready, 1)
                pool.dma_start(o_ak[0, li].rearrange("s h d -> s (h d)"), AB[:, 0, 0, 256:384]).then_inc(kv_out, 16)
                pool.dma_start(o_bk[0, li].rearrange("s h d -> s (h d)"), AB[:, 0, 1, 256:384]).then_inc(kv_out, 16)
                pool.wait_ge(big_act, taken_by(("ab", 0, 1))[1])
                pool.dma_start(o_av[0, li].rearrange("s h d -> s (h d)"), vab[:, 0, 0, :]).then_inc(kv_out, 16)
                pool.dma_start(o_bv[0, li].rearrange("s h d -> s (h d)"), vab[:, 0, 1, :]).then_inc(kv_out, 16)
                pool.wait_ge(d_ready, 1)
                pool.dma_start(o_dk[0, li].rearrange("s h m d -> s (h m d)"), DQ[:, 0, 256:512]).then_inc(kv_out, 16)
                pool.wait_ge(big_act, taken_by(("dv", 0))[1])
                pool.dma_start(o_dv[0, li].rearrange("s h d -> s (h d)"), vd[:, 0, :]).then_inc(kv_out, 16)
                pool.wait_ge(big_act, taken_by(("st", 0))[1])
                for d in range(2):
                    for g in range(2):
                        pool.dma_start(o_ssm[0, li, d, 2 * g:2 * g + 2].rearrange("h p n -> (h p) n"),
                                       sst[:, 2 * d + g, :]).then_inc(ssm_out, 16)
                pool.wait_ge(kv_out, (li + 1) * 96)
                pool.sem_inc(dummy, 1)
                pool.wait_ge(ssm_out, (li + 1) * 64)
                pool.sem_inc(dummy, 1)
                pool.drain().then_inc(done_pool, 1)
                pool.wait_ge(layer_go, li + 1)
                pool.sem_inc(dummy, 1)

        @block.tensor
        def _(pe):
            owed = []

            def mm(out, lhsT, rhs, start=True, stop=True, signal=None, **kw):
                ins = pe.matmul(out, lhsT, rhs, start=start, stop=stop, **kw)
                if signal is not None:
                    ins.then_inc(signal, 1)
                elif owed:
                    ins.then_inc(owed.pop(0), 1)
                return ins

            def turn(out, in_, signal=None):
                k = in_.shape[0]
                ins = pe.transpose(out, in_, ident[0:k, 0:k])
                if signal is not None:
                    ins.then_inc(signal, 1)
                elif owed:
                    ins.then_inc(owed.pop(0), 1)
                return ins

            count = [0]

            def bank(name):
                n = count[0]
                assert BIG[n][0] == name, (BIG[n], name)
                count[0] += 1
                if n >= 4:
                    by, value = taken_by(BIG[n - 4][0])
                    pe.wait_ge(big_of[by], value)
                return banks[n % 4]

            def taken(name):
                by, value = taken_by(name)
                pe.wait_ge(big_of[by], value)

            pe.wait_ge(in_x, 64)
            with pe.Fori(0, DEPTH) as li:
                count[0] = 0
                base = li * PER_SLOT

                def need(j):
                    pe.wait_ge(loaded[j % SLOTS], (base + (j // SLOTS + 1)) * 16)

                pe.wait_ge(cond, 1)
                pe.wait_ge(params, (li + 1) * 80)

                def columns(v):
                    taken(("row", v, 1))
                    b = bank(("col", v))
                    for k in range(KD):
                        mm(b[:, 2 * k:2 * k + 2], rsb[:, v % 2, k * P:(k + 1) * P], c_("sel"),
                           signal=big if k == KD - 1 else None)

                for v in range(6):
                    need(2 * v)
                    need(2 * v + 1)
                    for h in range(2):
                        b = bank(("row", v, h))
                        cols = slice(h * HALF, (h + 1) * HALF)
                        for k in range(KD):
                            q = 32 * (k % 4)
                            last = h == 1 and k == 3
                            mm(b[q:q + 32, :], csw[:, k, :], ring[:, (2 * v + k // 4) % SLOTS, k % 4, cols],
                               start=k < 4, stop=k >= 4 and q > 0, signal=freed[(2 * v) % SLOTS] if last else None)
                        mm(b[0:32, :], c_("bias1")[0:1, :], brow[0:1, v * D + h * HALF:v * D + (h + 1) * HALF],
                           start=False, stop=True, signal=big)
                    owed.append(freed[(2 * v + 1) % SLOTS])
                    if v >= 1 and v - 1 in (0, 1, 3, 4):
                        columns(v - 1)

                def widths(name):
                    for k in range(KD):
                        if k == 0:
                            pe.wait_ge(xn_ready, NT * (1 if name == "hT" else 2))
                        b = bank((name, k))
                        for t in range(NT):
                            turn(b[:, t * P:(t + 1) * P], xn[:, t, k * P:(k + 1) * P],
                                 signal=big if t == NT - 1 else None)

                def tokens(out, t, j, cols, signal=None, free=False):
                    for k in range(KD):
                        sig = None
                        if free and k == 3:
                            sig = freed[j % SLOTS]
                        if k == KD - 1:
                            sig = signal
                        mm(out, hT[:, k, t * P:(t + 1) * P], ring[:, (j + k // 4) % SLOTS, k % 4, cols],
                           start=k == 0, stop=k == KD - 1, signal=sig)
                    if free:
                        owed.append(freed[(j + 1) % SLOTS])

                widths("hT")
                taken(("hT", KD - 2))
                taken(("hT", KD - 1))
                need(12)
                need(13)
                for br in range(2):
                    for t in range(NT):
                        tokens(bank(("ab", t, br))[:, :], t, 12, slice(br * 512, br * 512 + 512), signal=big,
                               free=(br == 1 and t == NT - 1))
                need(14)
                need(15)
                for t in range(NT):
                    tokens(bank(("dqk", t))[:, :], t, 14, slice(0, 512), signal=big)
                    tokens(bank(("dv", t))[:, 0:256], t, 14, slice(512, 768), signal=big, free=t == NT - 1)
                need(16)
                need(17)
                for t in range(NT):
                    b = bank(("zdt", t))
                    tokens(b[:, 0:256], t, 16, slice(0, 256))
                    tokens(b[:, 256:264], t, 16, slice(768, 776), signal=big)
                for g in range(4):
                    b = bank(("xbc", g))
                    for k in range(KD):
                        sig = None
                        if g == 3 and k == 3:
                            sig = freed[16 % SLOTS]
                        if k == KD - 1:
                            sig = big
                        mm(b[:, 0:T], ring[:, (16 + k // 4) % SLOTS, k % 4, 256 + g * P:256 + (g + 1) * P], hT[:, k, :],
                           start=k == 0, stop=k == KD - 1, signal=sig)
                owed.append(freed[17 % SLOTS])

                def gate(i, s):
                    j = 18 + 3 * i
                    if s == 0:
                        need(j)
                        need(j + 1)
                    t, h = s // 2, s % 2
                    tokens(bank(("g", i, t, h))[:, :], t, j, slice(h * HALF, (h + 1) * HALF), signal=big, free=s == 5)

                for s in range(6):
                    gate(0, s)

                pe.wait_ge(ab_ready, 1)
                for t in range(NT):
                    for br in range(2):
                        b = bank(("qkT", t, br))
                        for g in range(2):
                            turn(b[:, g * P:(g + 1) * P], AB[:, t, br, g * P:(g + 1) * P])
                        turn(b[:, 256:384], AB[:, t, br, 256:384], signal=big)
                b = bank(("ckT",))
                turn(b[:, 0:P], ch("ak"))
                turn(b[:, P:2 * P], ch("bk"), signal=big)
                pe.wait_ge(d_ready, 1)
                for t in range(NT):
                    b = bank(("dT", t))
                    for c in range(4):
                        turn(b[:, c * P:(c + 1) * P], DQ[:, t, c * P:(c + 1) * P], signal=big if c == 3 else None)
                b = bank(("cdT",))
                turn(b[:, 0:P], ch("dk")[:, 0:P])
                turn(b[:, P:2 * P], ch("dk")[:, P:2 * P], signal=big)
                taken(("cdT",))

                def keys(t):
                    return (0, P) if t == 0 else (P, 512)

                def values(i, h, t):
                    cols = slice((h // 2) * HD, (h // 2) * HD + HD) if i < 2 else slice(h * HD, h * HD + HD)
                    own = [0] if t == 0 else [1, 2]
                    out = [vab[:, s, i, cols] if i < 2 else vd[:, s, cols] for s in own]
                    if t:
                        out.append(ch(("av", "bv", "dv")[i])[:, cols])
                    return out

                def scores(i, n):
                    h, t = iters(i)[n]
                    k0, k1 = keys(t)
                    step = i * NIT + n
                    if i < 2:
                        v, g = h // 2, h % 2
                        rows = slice(v * HD, (v + 1) * HD)
                        b = banks[4 + n % 2]
                        if n >= 2:
                            pe.wait_ge(p_ready, step - 1)
                        elif i:
                            pe.wait_ge(p_ready, i * NIT)
                        masked = i == 1 and t > 0
                        mm(b[:, 0:k1 - k0], qT[rows, i, g, t * P:(t + 1) * P], kT[rows, i, k0:k1], start=True,
                           stop=True, signal=None if masked else s_ready, skip_group_check=masked)
                        if masked:
                            other = slice(P, 2 * P) if t == 1 else slice(0, P)
                            mm(b[:, other], ident, c_("negabove") if t == 1 else c_("negbelow"), start=False, stop=True,
                               signal=s_ready, skip_group_check=True)
                    else:
                        if n:
                            pe.wait_ge(p_ready, 2 * NIT + n)
                        else:
                            pe.wait_ge(p_ready, 2 * NIT)
                        for m in range(2):
                            j = 2 * h + m
                            r = slice(32 * (j % 4), 32 * (j % 4) + 32)
                            mm(banks[4 + m][:, 0:k1 - k0], dqT[r, j // 4, t * P:(t + 1) * P], dkT[r, j // 4, k0:k1],
                               tile_position=(32 * (j % 4), 0), signal=s_ready if m else None)

                def weights(i, n):
                    h, t = iters(i)[n]
                    step = i * NIT + n
                    if i < 2:
                        pe.wait_ge(p_ready, step + 1)
                    else:
                        pe.wait_ge(w_ready, n + 1)
                    if step:
                        pe.wait_ge(pts_ready, step)
                    nb = len(values(i, h, t))
                    for k in range(nb):
                        turn(banks[6][:, k * P:(k + 1) * P], pr[:, n % 2, k * P:(k + 1) * P],
                             signal=pt_ready if k == nb - 1 else None)

                def weighted(i, n):
                    h, t = iters(i)[n]
                    step = i * NIT + n
                    pe.wait_ge(pts_ready, step + 1)
                    if step:
                        pe.wait_ge(o_ready, step)
                    vs = values(i, h, t)
                    for k, v in enumerate(vs):
                        mm(banks[7][:, 0:HD], pT[:, n % 2, k * P:(k + 1) * P], v, start=k == 0, stop=k == len(vs) - 1,
                           signal=pv_ready if k == len(vs) - 1 else None)

                def lift(i):
                    j = 20 + 3 * i
                    if i < 2:
                        pe.wait_ge(o_ready, (i + 1) * NIT)
                    else:
                        pe.wait_ge(bo_ready, i - 1)
                    for c in range(2):
                        b = bank(("boT", i, c))
                        for t in range(NT):
                            turn(b[:, t * P:(t + 1) * P], bo[:, t, c * P:(c + 1) * P], signal=big if t == NT - 1 else None)
                    taken(("boT", i, 1))
                    need(j)
                    for t in range(NT):
                        for h in range(2):
                            b = bank(("up", i, t, h))
                            for c in range(2):
                                mm(b[:, :], boT[:, c, t * P:(t + 1) * P], ring[:, j % SLOTS, c, h * HALF:(h + 1) * HALF],
                                   start=c == 0, stop=c == 1, signal=big if c == 1 else None)
                    owed.append(freed[j % SLOTS])

                for i in range(3):
                    for n in range(NIT + 2):
                        if n < NIT:
                            scores(i, n)
                        if 1 <= n <= NIT:
                            weights(i, n - 1)
                        if n >= 2:
                            weighted(i, n - 2)
                        if n % 2 == 1 and n < NIT:
                            gate(i + 1, n // 2)
                    lift(i)

                pe.wait_ge(conv_out, 4)
                for t in range(NT):
                    b = bank(("uT", t))
                    for g in range(3):
                        turn(b[:, g * P:(g + 1) * P], uT[:, g, t * P:(t + 1) * P], signal=big if g == 2 else None)
                pe.wait_ge(dt_done, 1)
                b = bank(("cum",))
                for t in range(NT):
                    o = t * 16
                    mm(b[:, o:o + 4], c_("upto"), la[:, t, 0:4])
                    mm(b[:, o + 4:o + 8], c_("from"), la[:, t, 4:8])
                    mm(b[:, o + 8:o + 16], c_("ones"), la[:, t, :], signal=big if t == NT - 1 else None)
                b = bank(("h0T",))
                for d in range(2):
                    turn(b[:, d * P:(d + 1) * P], ch("ssm")[:, d * P:(d + 1) * P], signal=big if d else None)

                def tri(d):
                    return c_("upto") if d == 0 else c_("from")

                pe.wait_ge(ssd_small, 1)
                taken(("uT", 2))
                for t in range(NT):
                    for d in range(2):
                        b = bank(("dec", t, d))
                        for h in range(4):
                            mm(b[:, h * P:(h + 1) * P], la[:, t, 4 * d + h:4 * d + h + 1].broadcast_to([P, P]), tri(d),
                               start=h == 0, stop=False, skip_group_check=True)
                        mm(b[:, :], ident, rep(c_("negbelow" if d == 0 else "negabove"), 1, 4), start=False, stop=True,
                           signal=big, skip_group_check=True)
                    for g in range(2):
                        b = bank(("GT", t, g))
                        r = slice(g * HD, (g + 1) * HD)
                        mm(b[:, 0:P], uT[r, 2, t * P:(t + 1) * P], uT[r, 3, t * P:(t + 1) * P], signal=big)
                    pe.wait_ge(mt_ready, t + 1)
                    b = bank(("st", t))
                    if t == 0:
                        for d in range(2):
                            for g in range(2):
                                o = (2 * d + g) * HD
                                mm(b[:, o:o + HD], xde[:, d, 2 * g:2 * g + 2, :], xsB[:, t, 256 + g * HD:256 + (g + 1) * HD],
                                   signal=big if d and g else None)
                    else:
                        for g in range(2):
                            mm(b[g * HD:(g + 1) * HD, 0:P], xsB[:, t, 256 + g * HD:256 + (g + 1) * HD],
                               xde[:, t - 1, 2 * g:2 * g + 2, :], signal=big if g else None)
                    b = bank(("y", t))
                    for h in range(4):
                        for d in range(2):
                            mm(b[:, h * HD:(h + 1) * HD], Mt[:, 4 * d + h, :], xdt[:, d, h, :], start=d == 0, stop=d == 1,
                               signal=big if (h == 3 and d == 1) else None)
                pe.wait_ge(h_in, 1)
                for t in (1, 2):
                    for g in range(2):
                        b = bank(("yo", t, g))
                        r = slice(g * HD, (g + 1) * HD)
                        for d in range(2):
                            i = (0, 3) if t == 1 else (1, 2)
                            mm(b[:, d * P:(d + 1) * P], uT[r, 3, t * P:(t + 1) * P], hin[r, i[d], :],
                               signal=big if d else None)
                lift(3)

                pe.wait_ge(merged, 18)
                for k in range(KD):
                    b = bank(("mT", k))
                    for t in range(NT):
                        turn(b[:, t * P:(t + 1) * P], xn[:, t, k * P:(k + 1) * P], signal=big if t == NT - 1 else None)

                def gate_rows(out, i, g, h, signal):
                    mm(out, c_("selb")[:, g * P:(g + 1) * P], gaterow[:, i, h * HALF:(h + 1) * HALF], signal=signal)

                for g in range(2):
                    for h in range(2):
                        gate_rows(bank(("gb", g, h))[:, :], 0, g, h, big)
                taken(("mT", KD - 2))
                taken(("mT", KD - 1))
                need(30)
                need(31)
                for t in range(NT):
                    for h in range(2):
                        tokens(bank(("out", t, h))[:, :], t, 30, slice(h * HALF, (h + 1) * HALF), signal=big,
                               free=t == NT - 1 and h == 1)

                widths("h2T")
                taken(("h2T", KD - 2))
                taken(("h2T", KD - 1))
                b = bank(("lg",))
                for t in range(NT):
                    for k in range(KD):
                        mm(b[:, t * NE:(t + 1) * NE], hT[:, k, t * P:(t + 1) * P], wr[:, k, :], start=k == 0,
                           stop=k == KD - 1, signal=big if t == NT - 1 and k == KD - 1 else None)
                pe.wait_ge(aff_ready, 1)
                b = bank(("affT",))
                for t in range(NT):
                    turn(b[0:NE, t * P:(t + 1) * P], aff[:, t, :], signal=big if t == NT - 1 else None)
                pe.wait_ge(mask_ready, 1)
                b = bank(("mk",))
                for t in range(NT):
                    turn(b[:, t * NE:(t + 1) * NE], maskT[:, t * P:(t + 1) * P], signal=big if t == NT - 1 else None)
                taken(("mk",))
                b = bank(("rank",))
                mm(b[:, 0:NE], c_("upto"), msk[:, 0, :])
                mm(b[:, NE:2 * NE], c_("upto"), msk[:, 1, :])
                mm(b[:, 2 * NE:3 * NE], c_("upto"), msk[:, 2, :], stop=False)
                mm(b[:, 2 * NE:3 * NE], c_("ones"), msk[:, 1, :], start=False, signal=big)
                pe.wait_ge(hot_ready, 1)
                for k in range(KD):
                    cols = slice(k * P, (k + 1) * P)
                    mm(bank(("xc", k))[:, 0:256], xn[:, 0, cols], Sc[:, :, :], signal=big)
                    b = bank(("xl", k))
                    mm(b[:, :], xn[:, 1, cols], Sl[:, 0, :, :], stop=False)
                    mm(b[:, :], xn[:, 2, cols], Sl[:, 1, :, :], start=False, signal=big)
                for n in range(len(BIG) - 4, len(BIG)):
                    taken(BIG[n][0])
                for i in range(6):
                    mm(banks[i][:, :], c_("zero"), cst[:, 0:512], stop=False, skip_group_check=True)

                with pe.Fori(0, NE // 2) as ep:
                    for u in range(2):
                        e = ep * 2 + u

                        def arrive(i):
                            i += 6 * u
                            pe.wait_ge(loaded[i % SLOTS], (base + (LOADS0 // SLOTS + i // SLOTS + 1) + ep * 3) * 16)

                        def up(out, i, last, free_last):
                            for k in range(KD):
                                s = (6 * u + i + k // 4) % SLOTS
                                if k % 4 == 0:
                                    arrive(i + k // 4)
                                for h in range(2):
                                    sig = None
                                    if h and k == 3:
                                        sig = freed[s]
                                    if h and k == KD - 1:
                                        sig = freed[s] if free_last else last
                                    mm(out[h * 64:(h + 1) * 64, :], xcur[:, k, :], ring[:, s, k % 4, h * HALF:(h + 1) * HALF],
                                       start=k == 0, stop=k == KD - 1, signal=sig)
                            if not free_last:
                                owed.append(freed[s])

                        pe.wait_ge(xc_ready, e + 1)
                        pe.wait_ge(sgs_ready, e)
                        up(banks[6], 0, None, True)
                        pe.wait_ge(yo_ready, e)
                        up(banks[7], 2, h3_ready, False)
                        pe.wait_ge(hid_ready, e + 1)
                        for b in range(4):
                            turn(banks[6][:, b * P:(b + 1) * P], hid[:, b, :], signal=ht_ready if b == 3 else None)
                        pe.wait_ge(hts_ready, e + 1)
                        for fh in range(2):
                            arrive(4 + fh)
                            s = (6 * u + 4 + fh) % SLOTS
                            for b in range(4):
                                for h in range(2):
                                    sig = None
                                    if b == 3 and h == 1:
                                        sig = yp_ready if fh else freed[s]
                                    mm(banks[7][h * 64:(h + 1) * 64, :], hidT[:, b, fh * 64:(fh + 1) * 64],
                                       ring[:, s, b, h * HALF:(h + 1) * HALF], start=fh == 0 and b == 0,
                                       stop=fh == 1 and b == 3, signal=sig)
                        owed.append(freed[s])
                        pe.wait_ge(w1hot, e + 1)
                        for t in range(NT):
                            turn(banks[6][:, t * P:(t + 1) * P], sgs[:, t, :], signal=sg_ready if t == NT - 1 else None)
                        pe.wait_ge(sgs_ready, e + 1)
                        pe.wait_ge(yo_ready, e + 1)
                        for t in range(NT):
                            for h in range(2):
                                r = slice(h * 64, (h + 1) * 64)
                                mm(banks[2 * t + h][:, :], sgT[r, t, :], yo[r, :], start=False, stop=False,
                                   skip_group_check=True)
                for i in range(6):
                    mm(banks[i][:, 0:32], c_("zero"), cst[:, 0:32], start=False, stop=True, skip_group_check=True)
                for g in range(2):
                    for h in range(2):
                        if g == 1:
                            pe.wait_ge(gb2_sb, h + 1)
                        gate_rows(banks[6 + h][:, :], 1, g, h, gb2)
                assert not owed
                pe.drain().then_inc(done_pe, 1)
                pe.wait_ge(layer_go, li + 1)
                pe.sem_inc(dummy_pe, 1)

        @block.scalar
        def _(act):
            A = nc.scalar.activation
            nbig = [0]
            own = [0]

            def step(ins):
                ins.then_inc(act_step, 1)
                own[0] += 1

            def settle():
                act.wait_ge(act_step, own[0])

            def grab(name):
                assert BIG_BY[name] == "act"
                act.wait_ge(big, BIG_AT[name] + 1)
                return banks[BIG_AT[name] % 4]

            def gave(name, ins):
                nbig[0] += 1
                assert taken_by(name) == ("act", nbig[0]), name
                ins.then_inc(big_act, 1)

            def taken_dve(name):
                act.wait_ge(big_dve, taken_by(name)[1])

            roots = [0]

            def root(n):
                roots[0] += 1
                act.wait_ge(var_ready, roots[0])
                A(st[:, 1, 0:n], st[:, 0, 0:n], ACT.Sqrt).then_inc(root_ready, 1)

            def modulated(name, k, out_c, in_c, out_l, in_l, which):
                A(out_c, in_c, ACT.Identity, bias=modc[:, 2 * which, k, 0:1], scale=gs[:, which, k, 0:1])
                gave((name, k), A(out_l, in_l, ACT.Identity, bias=modc[:, 2 * which, k, 1:2], scale=gs[:, which, k, 1:2]))

            act.wait_ge(in_x, 64)
            with act.Fori(0, DEPTH) as li:
                nbig[0] = own[0] = roots[0] = 0
                act.wait_ge(pads, 1)
                A(csw[:, :, 0:2], cs[:, :, :], ACT.Silu).then_inc(cond, 1)
                for t in range(NT):
                    A(xn[:, t, :], x[:, t, :], ACT.Square, accum_out=st[:, 4, t:t + 1]).then_inc(act_sq, 1)
                root(NT)
                for v in range(6):
                    for h in range(2):
                        b = grab(("row", v, h))
                        out = gaterow[:, v // 3, :] if v in (2, 5) else rsb[:, v % 2, :]
                        gave(("row", v, h), A(out[:, h * HALF:(h + 1) * HALF], b[:, :], ACT.Copy))
                act.wait_ge(mod1, 1)

                def modulate(name, which):
                    for k in range(0, KD, 2):
                        b = grab((name, k))
                        modulated(name, k, hT[:, k, 0:P], b[:, 0:P], hT[:, k, P:T], b[:, P:T], which)

                modulate("hT", 0)
                for br in range(2):
                    for t in range(NT):
                        b = grab(("ab", t, br))
                        A(AB[:, t, br, 0:256].rearrange("p (g v d) -> p v g d", v=2, g=2),
                          b[:, 0:256].rearrange("p (v g d) -> p v g d", v=2, g=2), ACT.Copy)
                        A(AB[:, t, br, 256:384], b[:, 256:384], ACT.Copy)
                        gave(("ab", t, br), A(vab[:, t, br, :], b[:, 384:512], ACT.Copy))
                for t in range(NT):
                    act.wait_ge(big_act, taken_by(("ab", t, 1))[1])
                    if t >= 2:
                        act.wait_ge(sq_free, t - 1)
                    A(tmp[:, t % 2, :], AB[:, t, :, :].rearrange("p b n -> p (b n)"), ACT.Square).then_inc(act_sq, 1)
                for t in range(NT):
                    b = grab(("dqk", t))
                    gave(("dqk", t), A(DQ[:, t, :], b[:, :], ACT.Copy))
                    b = grab(("dv", t))
                    gave(("dv", t), A(vd[:, t, :], b[:, 0:256], ACT.Copy))
                root(36)
                for t in range(NT):
                    b = grab(("zdt", t))
                    A(sz[:, t, :], b[:, 0:256], ACT.Silu)
                    gave(("zdt", t), A(dtr[:, t, :], b[:, 256:264], ACT.Copy))
                act.wait_ge(pads, 2)
                for g in range(4):
                    b = grab(("xbc", g))
                    A(xbc[:, g, 2:2 + P], b[:, 0:P], ACT.Copy)
                    gave(("xbc", g), A(xbc[:, g, LAT0 + 2:LAT0 + 2 + 256], b[:, P:T], ACT.Copy))
                act.wait_ge(ab_ready, 1)
                for t in range(NT):
                    if t >= 2:
                        act.wait_ge(sq_free, NT + t - 1)
                    A(tmp[:, t % 2, 0:512], DQ[:, t, :], ACT.Square).then_inc(act_sq, 1)
                root(48)
                act.wait_ge(dt_abs, 1)
                step(A(dexp, dabs, ACT.Exp))
                settle()
                A(dexp, dexp, ACT.Ln, bias=1.0)
                A(expa, r_("alog"), ACT.Exp).then_inc(dt_log, 1)
                act.wait_ge(lam_dot, 1)
                A(lamx, lamd, ACT.Exp).then_inc(lam_exp, 1)

                def gate(i, s):
                    t, h = s // 2, s % 2
                    if s == 0 and i == 2:
                        taken_dve(("up", 0, NT - 1, 1))
                    elif s == 0 and i == 3:
                        act.wait_ge(merged, 6)
                    b = grab(("g", i, t, h))
                    gave(("g", i, t, h), A(G[i % 2][:, t, h * HALF:(h + 1) * HALF], b[:, :], ACT.Tanh, scale=0.5))

                for s in range(6):
                    gate(0, s)
                for g in range(4):
                    act.wait_ge(conv_sum, g + 1)
                    bias = cp[:, COLS["convb"][0] + g:COLS["convb"][0] + g + 1]
                    A(uT[:, g, 0:P], cacc[:, g, 0:P], ACT.Silu, bias=bias)
                    A(uT[:, g, P:T], cacc[:, g, LAT0:LAT0 + 256], ACT.Silu, bias=bias).then_inc(conv_out, 1)
                for t in range(NT):
                    for br in range(2):
                        b = grab(("qkT", t, br))
                        A(qT[:, br, :, t * P:(t + 1) * P], b[:, 0:256].rearrange("p (g t) -> p g t", g=2), ACT.Copy)
                        gave(("qkT", t, br), A(kT[:, br, t * P:(t + 1) * P], b[:, 256:384], ACT.Copy))
                b = grab(("ckT",))
                gave(("ckT",), A(kT[:, :, T:512], b[:, 0:256].rearrange("p (g t) -> p g t", g=2), ACT.Copy))
                for t in range(NT):
                    b = grab(("dT", t))
                    A(dqT[:, :, t * P:(t + 1) * P], b[:, 0:256].rearrange("p (g t) -> p g t", g=2), ACT.Copy)
                    gave(("dT", t), A(dkT[:, :, t * P:(t + 1) * P], b[:, 256:512].rearrange("p (g t) -> p g t", g=2), ACT.Copy))
                b = grab(("cdT",))
                gave(("cdT",), A(dkT[:, :, T:512], b[:, 0:256].rearrange("p (g t) -> p g t", g=2), ACT.Copy))

                for i in range(3):
                    its = iters(i)
                    for n in range(NIT + 1):
                        if n < NIT:
                            h, t = its[n]
                            nk = P if t == 0 else T
                            step_ = i * NIT + n
                            act.wait_ge(m_ready, step_ + 1)
                            q = 2 * (n % 4)
                            if i < 2:
                                ins = A(pr[:, n % 2, 0:nk], banks[4 + n % 2][:, 0:nk], ACT.Exp, bias=st[:, 1, q:q + 1],
                                        scale=HD ** -0.5, accum_out=st[:, 2, q:q + 1])
                                if i == 1:
                                    ins = A(st[:, 4, q:q + 1], r_("sink")[:, h:h + 1], ACT.Exp, bias=st[:, 1, q:q + 1])
                            else:
                                for m in range(2):
                                    ins = A(pr[:, n % 2, m * T:m * T + nk], banks[4 + m][:, 0:nk], ACT.Exp,
                                            bias=st[:, 1, q + m:q + m + 1], scale=32 ** -0.5,
                                            accum_out=st[:, 2, q + m:q + m + 1])
                            ins.then_inc(p_ready, 1)
                        if n >= 1:
                            h, t = its[n - 1]
                            nk = P if t == 0 else T
                            step_ = i * NIT + n - 1
                            act.wait_ge(pt_ready, step_ + 1)
                            if step_ >= 2:
                                act.wait_ge(pv_ready, step_ - 1)
                            A(pT[:, (n - 1) % 2, 0:nk], banks[6][:, 0:nk], ACT.Copy).then_inc(pts_ready, 1)
                        if n % 2 == 1 and n < NIT:
                            gate(i + 1, n // 2)
                    if i == 2:
                        root(12)
                for t in range(NT):
                    b = grab(("uT", t))
                    gave(("uT", t), A(xsB[:, t, :], b[:, 0:384], ACT.Copy))
                b = grab(("h0T",))
                A(hin[:, 0, :], b[:, 0:P], ACT.Copy)
                gave(("h0T",), A(hin[:, 2, :], b[:, P:2 * P], ACT.Copy))
                act.wait_ge(ssd_small, 1)
                A(ex[:, :, :, :], sm[:, :, :, :], ACT.Exp).then_inc(ssd_exp, 1)
                for t in range(NT):
                    if t:
                        act.wait_ge(mt_ready, t)
                    for d in range(2):
                        b = grab(("dec", t, d))
                        for h in range(4):
                            ins = A(E[:, 4 * d + h, :], b[:, h * P:(h + 1) * P], ACT.Exp, bias=nacs[:, t, 4 * d + h:4 * d + h + 1])
                        gave(("dec", t, d), ins)
                    if t == 0:
                        b = grab(("st", 0))
                        gave(("st", 0), A(sst[:, :, :], b[:, 0:256].rearrange("p (i n) -> p i n", i=4), ACT.Copy))
                root(NT)
                for k in range(0, KD, 2):
                    b = grab(("mT", k))
                    gave(("mT", k), A(hT[:, k, :], b[:, 0:T], ACT.Copy, scale=0.5))
                for g in range(2):
                    for h in range(2):
                        b = grab(("gb", g, h))
                        gave(("gb", g, h), A(gbc[:, g, h * HALF:(h + 1) * HALF], b[:, :], ACT.Copy))
                for t in range(NT):
                    act.wait_ge(x_ready, t + 1)
                    A(xn[:, t, :], x[:, t, :], ACT.Square, accum_out=st[:, 4, t:t + 1]).then_inc(act_sq, 1)
                root(NT)
                modulate("h2T", 1)
                act.wait_ge(ssm_out, (li + 1) * 64)
                act.wait_ge(aff_in, 1)
                A(aff[:, :, :], aff[:, :, :], ACT.Exp).then_inc(aff_exp, 1)
                b = grab(("affT",))
                gave(("affT",), A(affT, b[0:NE, 0:T], ACT.Copy))
                b = grab(("mk",))
                gave(("mk",), A(msk[:, :, :], b[:, 0:48].rearrange("p (t e) -> p t e", t=NT), ACT.Copy))
                XTe = XT[:, :, 0:NE * CE].rearrange("p k (e c) -> p k e c", c=CE)
                for k in range(0, KD, 2):
                    b = grab(("xc", k))
                    gave(("xc", k), A(XTe[:, k, :, 0:CAP[0]], b[:, 0:256].rearrange("p (e c) -> p e c", e=NE), ACT.Identity,
                                      bias=modc[:, 2, k, 0:1], scale=gs[:, 1, k, 0:1]))
                    b = grab(("xl", k))
                    gave(("xl", k), A(XTe[:, k, :, CAP[0]:CE], b[:, :].rearrange("p (e c) -> p e c", e=NE), ACT.Identity,
                                      bias=modc[:, 2, k, 1:2], scale=gs[:, 1, k, 1:2]))
                with act.Fori(0, NE) as e:
                    act.wait_ge(h3_ready, e + 1)
                    A(hs, banks[6][:, :], ACT.Silu).then_inc(silu_ready, 1)
                    act.wait_ge(ht_ready, e + 1)
                    A(hidT[:, :, :], banks[6][:, :].rearrange("p (b n) -> p b n", b=4), ACT.Copy).then_inc(hts_ready, 1)
                    act.wait_ge(yp_ready, e + 1)
                    A(yo, banks[7][:, :], ACT.Copy).then_inc(yo_ready, 1)
                for g in range(2):
                    for h in range(2):
                        act.wait_ge(gb2, 2 * g + h + 1)
                        A(gbc[:, g, h * HALF:(h + 1) * HALF], banks[6 + h][:, :], ACT.Copy).then_inc(gb2_sb, 1)
                act.drain().then_inc(done_act, 1)
                act.wait_ge(layer_go, li + 1)
                act.sem_inc(dummy_act, 1)

        @block.vector
        def _(dve):
            V = nc.vector
            nbig = [0]
            own = [0]
            norms = [0]
            sqs = [0]

            def step(ins):
                ins.then_inc(dve_step, 1)
                own[0] += 1

            def settle():
                dve.wait_ge(dve_step, own[0])

            def link(ins):
                step(ins)
                settle()

            def grab(name):
                assert BIG_BY[name] == "dve"
                dve.wait_ge(big, BIG_AT[name] + 1)
                return banks[BIG_AT[name] % 4]

            def gave(name, ins):
                nbig[0] += 1
                assert taken_by(name) == ("dve", nbig[0]), name
                ins.then_inc(big_dve, 1)

            def rsqrt(ssq, n, width):
                var, root, y, c = (st[:, i, 0:n] for i in range(4))
                V.tensor_scalar(var, ssq, 1.0 / width, EPS, ALU.mult, ALU.add).then_inc(var_ready, 1)
                norms[0] += 1
                dve.wait_ge(root_ready, norms[0])
                dve.wait_ge(var_ready, norms[0])
                link(V.reciprocal(y, root))
                link(V.tensor_tensor(c, var, y, ALU.mult))
                link(V.tensor_tensor(c, c, y, ALU.mult))
                link(V.tensor_scalar(c, c, -0.5, 1.5, ALU.mult, ALU.add))
                link(V.tensor_tensor(y, y, c, ALU.mult))
                return y

            def norm_rows():
                sqs[0] += NT
                dve.wait_ge(act_sq, sqs[0])
                y = rsqrt(st[:, 4, 0:NT], NT, D)
                for t in range(NT):
                    V.tensor_scalar(xn[:, t, :], x[:, t, :], y[:, t:t + 1], None, ALU.mult).then_inc(xn_ready, 1)

            def modulate(name, which):
                for k in range(1, KD, 2):
                    b = grab((name, k))
                    V.tensor_scalar(hT[:, k, 0:P], b[:, 0:P], gs[:, which, k, 0:1], modc[:, 2 * which, k, 0:1],
                                    ALU.mult, ALU.add)
                    gave((name, k), V.tensor_scalar(hT[:, k, P:T], b[:, P:T], gs[:, which, k, 1:2],
                                                    modc[:, 2 * which, k, 1:2], ALU.mult, ALU.add))

            def head_norm(buf, heads, width, per_tile, gq_mul, ready, rotary):
                n = NT * heads
                for t in range(NT):
                    sqs[0] += 1
                    dve.wait_ge(act_sq, sqs[0])
                    V.tensor_reduce(st[:, 5, t * heads:(t + 1) * heads] if n <= 36 else stw[:, t * heads:(t + 1) * heads],
                                    tmp[:, t % 2, 0:heads * width].rearrange("p (h n) -> p h n", h=heads), AX.X, ALU.add)\
                        .then_inc(sq_free, 1)
                    per_tile[0] += 1
                dve.wait_ge(sq_free, per_tile[0])
                y = rsqrt(st[:, 5, 0:n] if n <= 36 else stw[:, 0:n], n, width)
                for t in range(NT):
                    step(V.tensor_tensor(buf(t), buf(t), rep(y[:, t * heads:(t + 1) * heads], 2, width), ALU.mult))
                settle()
                for t in range(NT):
                    for ins in gq_mul(t):
                        step(ins)
                settle()
                for t in (1, 2):
                    rotary(t)
                return None

            taken_sq = [0]
            dve.wait_ge(in_x, 64)
            with dve.Fori(0, DEPTH) as li:
                nbig[0] = own[0] = norms[0] = sqs[0] = taken_sq[0] = 0
                norm_rows()
                for n, v in enumerate((0, 1, 3, 4)):
                    b = grab(("col", v))
                    gave(("col", v), V.tensor_copy(modc[:, n, :, :], b[:, 0:16].rearrange("p (k g) -> p k g", g=2)))
                dve.wait_ge(big_dve, 4)
                dve.wait_ge(params, (li + 1) * 80)
                for i in range(2):
                    gain = cp[:, 8 * i:8 * i + 8]
                    ins = V.scalar_tensor_tensor(gs[:, i, :, :], modc[:, 2 * i + 1, :, :], 1.0, rep(gain, 2, 2),
                                                 ALU.add, ALU.mult)
                    if i == 0:
                        step(ins)
                ins.then_inc(mod1, 1)
                settle()
                dve.wait_ge(mod1, 1)
                link(V.tensor_tensor(lamt, r_("lamq"), r_("lamk"), ALU.mult))
                step(V.tensor_scalar(nsink, r_("sink"), -1.0, None, ALU.mult))
                V.tensor_reduce(lamd, lamt.rearrange("p (i n) -> p i n", i=2), AX.X, ALU.add).then_inc(lam_dot, 1)
                modulate("hT", 0)

                def ab_gain(t):
                    q = AB[:, t, :, 0:256].rearrange("p b (h d) -> p b h d", h=4)
                    k = AB[:, t, :, 256:384].rearrange("p b (h d) -> p b h d", h=2)
                    return [V.tensor_tensor(q, q, rep(gqc, 2, 4), ALU.mult), V.tensor_tensor(k, k, rep(gkc, 2, 2), ALU.mult)]

                def turner(buf, heads, width, cosn, sinn, last, sem_):
                    def rotary(t):
                        n = width // 4
                        v = buf(t)
                        cs_ = c_(cosn)[:, (t - 1) * width:t * width]
                        sn_ = c_(sinn)[:, (t - 1) * width:t * width].rearrange("p (a h n) -> p a h n", a=2, h=2)
                        v5 = v.rearrange("p h (a c n) -> p h a c n", a=2, c=2)
                        o5 = tmp[:, 1, 0:heads * width].rearrange("p (h a c n) -> p h a c n", h=heads, a=2, c=2)
                        for c in range(2):
                            step(V.tensor_tensor(o5[:, :, :, c, :], v5[:, :, :, 1 - c, :], rep(sn_[:, :, c, :], 1, heads), ALU.mult))
                        settle()
                        link(V.tensor_tensor(v, v, rep(cs_, 1, heads), ALU.mult))
                        ins = V.tensor_tensor(v, v, tmp[:, 1, 0:heads * width].rearrange("p (h n) -> p h n", h=heads), ALU.add)
                        if t == last:
                            ins.then_inc(sem_, 1)
                            dve.wait_ge(sem_, 1)
                        else:
                            link(ins)
                    return rotary

                abuf = lambda t: AB[:, t, :, :].rearrange("p b (h d) -> p (b h) d", d=HD)
                head_norm(abuf, 12, HD, taken_sq, ab_gain, ab_ready, turner(abuf, 12, HD, "cos", "sin", 2, ab_ready))

                dve.wait_ge(big_act, taken_by(("zdt", 2))[1])
                link(V.tensor_tensor(dtr, dtr, rep(r_("dtb"), 1, NT), ALU.add))
                V.scalar_tensor_tensor(dabs, dtr, -1.0, dtr, ALU.mult, ALU.min).then_inc(dt_abs, 1)

                def d_gain(t):
                    q = DQ[:, t, 0:256].rearrange("p (h d) -> p h d", h=8)
                    k = DQ[:, t, 256:512].rearrange("p (h d) -> p h d", h=8)
                    return [V.tensor_tensor(q, q, rep(r_("gqd"), 1, 8), ALU.mult), V.tensor_tensor(k, k, rep(r_("gkd"), 1, 8), ALU.mult)]

                dbuf = lambda t: DQ[:, t, :].rearrange("p (h d) -> p h d", h=16)
                head_norm(dbuf, 16, 32, taken_sq, d_gain, d_ready, turner(dbuf, 16, 32, "cosd", "sind", 2, d_ready))

                dve.wait_ge(dt_log, 1)
                link(V.scalar_tensor_tensor(dt_, dtr, 0.0, dexp, ALU.max, ALU.add))
                V.scalar_tensor_tensor(la, dt_, -1.0, rep(expa, 1, NT), ALU.mult, ALU.mult).then_inc(dt_done, 1)
                dve.wait_ge(lam_exp, 1)
                link(V.tensor_tensor(nlam, lamx[:, 1:2], lamx[:, 0:1], ALU.subtract))
                link(V.tensor_tensor(nlam, nlam, r_("laminit"), ALU.subtract))

                dve.wait_ge(big_act, taken_by(("xbc", 3))[1])
                cw = cp[:, COLS["convw"][0]:COLS["convw"][1]].rearrange("p (g k) -> p g k", g=4)
                for k in range(5):
                    for g in range(4):
                        if k == 0:
                            step(V.tensor_scalar(cacc[:, g, :], xbc[:, g, 0:NU_CONV], cw[:, g, 0:1], None, ALU.mult))
                        else:
                            ins = V.scalar_tensor_tensor(cacc[:, g, :], xbc[:, g, k:k + NU_CONV], cw[:, g, k:k + 1],
                                                         cacc[:, g, :], ALU.mult, ALU.add)
                            if k == 4:
                                ins.then_inc(conv_sum, 1)
                            else:
                                step(ins)
                    if k < 4:
                        settle()

                def lift(i):
                    for c in range(2):
                        b = grab(("boT", i, c))
                        gave(("boT", i, c), V.tensor_copy(boT[:, c, :], b[:, 0:T]))
                    for t in range(NT):
                        for h in range(2):
                            b = grab(("up", i, t, h))
                            g = G[i % 2][:, t, h * HALF:(h + 1) * HALF]
                            m = xn[:, t, h * HALF:(h + 1) * HALF]
                            if i == 0:
                                dve.wait_ge(big_act, taken_by(("g", 0, t, h))[1])
                                gave(("up", i, t, h), V.scalar_tensor_tensor(m, g, 1.0, b[:, :], ALU.add, ALU.mult))
                            else:
                                dve.wait_ge(big_act, taken_by(("g", i, t, h))[1])
                                gave(("up", i, t, h), V.scalar_tensor_tensor(g, g, 1.0, b[:, :], ALU.add, ALU.mult))
                                dve.wait_ge(big_dve, nbig[0])
                                V.tensor_tensor(m, m, g, ALU.add).then_inc(merged, 1)

                for i in range(3):
                    its = iters(i)
                    for n in range(NIT + 2):
                        if n < NIT:
                            h, t = its[n]
                            nk = P if t == 0 else T
                            q = 2 * (n % 4)
                            dve.wait_ge(s_ready, i * NIT + n + 1)
                            mx, nb = st[:, 0, q:q + 2], st[:, 1, q:q + 2]
                            if i < 2:
                                link(V.tensor_reduce(mx[:, 0:1], banks[4 + n % 2][:, 0:nk], AX.X, ALU.max))
                            else:
                                for m in range(2):
                                    step(V.tensor_reduce(mx[:, m:m + 1], banks[4 + m][:, 0:nk], AX.X, ALU.max))
                                settle()
                            if i == 0:
                                ins = V.tensor_scalar(nb[:, 0:1], mx[:, 0:1], -(HD ** -0.5), None, ALU.mult)
                            elif i == 1:
                                ins = V.tensor_scalar(nb[:, 0:1], mx[:, 0:1], -(HD ** -0.5), nsink[:, h:h + 1], ALU.mult, ALU.min)
                            else:
                                ins = V.tensor_scalar(nb, mx, -(32 ** -0.5), None, ALU.mult)
                            ins.then_inc(m_ready, 1)
                        if 1 <= n <= NIT:
                            h, t = its[n - 1]
                            nk = P if t == 0 else T
                            q = 2 * ((n - 1) % 4)
                            dve.wait_ge(p_ready, i * NIT + n)
                            sums, rs = st[:, 2, q:q + 2], st[:, 3, q:q + 2]
                            if i == 1:
                                link(V.tensor_tensor(sums[:, 0:1], sums[:, 0:1], st[:, 4, q:q + 1], ALU.add))
                            if i < 2:
                                step(V.reciprocal(rs[:, 0:1], sums[:, 0:1]))
                            else:
                                link(V.reciprocal(rs, sums))
                                link(V.tensor_tensor(rs[:, 1:2], rs[:, 1:2], nlam, ALU.mult))
                                p0, p1 = pr[:, (n - 1) % 2, 0:nk], pr[:, (n - 1) % 2, T:T + nk]
                                link(V.tensor_scalar(p1, p1, rs[:, 1:2], None, ALU.mult))
                                V.scalar_tensor_tensor(p0, p0, rs[:, 0:1], p1, ALU.mult, ALU.add).then_inc(w_ready, 1)
                        if n >= 2:
                            h, t = its[n - 2]
                            q = 2 * ((n - 2) % 4)
                            settle()
                            dve.wait_ge(pv_ready, i * NIT + n - 1)
                            if i == 0 and n == 2:
                                dve.wait_ge(kv_out, (li + 1) * 96)
                            out = bo[:, t, h * HD:(h + 1) * HD]
                            if i < 2:
                                V.tensor_scalar(out, banks[7][:, 0:HD], st[:, 3, q:q + 1], None, ALU.mult).then_inc(o_ready, 1)
                            else:
                                V.tensor_copy(out, banks[7][:, 0:HD]).then_inc(o_ready, 1)
                    if i == 2:
                        dve.wait_ge(o_ready, 3 * NIT)
                        sq = at(po, NT * 256).rearrange("p (t n) -> p t n", t=NT)
                        link(V.tensor_tensor(sq, bo[:, :, :], bo[:, :, :], ALU.mult))
                        link(V.tensor_reduce(st[:, 5, 0:12], sq.rearrange("p t (h n) -> p (t h) n", n=HD), AX.X, ALU.add))
                        y = rsqrt(st[:, 5, 0:12], 12, HD)
                        link(V.tensor_scalar(y, y, r_("onemlam"), None, ALU.mult))
                        b4 = bo[:, :, :].rearrange("p t (h n) -> p (t h) n", n=HD)
                        link(V.tensor_tensor(b4, b4, rep(y, 2, HD), ALU.mult))
                        V.tensor_tensor(b4, b4, rep(r_("gdout"), 1, 12), ALU.mult).then_inc(bo_ready, 1)
                    lift(i)

                b = grab(("cum",))
                cum = b[:, 0:48].rearrange("p (t i j) -> p i t j", t=NT, i=2)
                step(V.tensor_copy(sm[:, 0, :, :], cum[:, 0, :, :]))
                step(V.tensor_copy(sm[:, 2, :, :], cum[:, 1, :, :]))
                gave(("cum",), V.tensor_scalar(nacs, cum[:, 0, :, :], -1.0, None, ALU.mult))
                settle()
                V.tensor_tensor(sm[:, 1, :, :], sm[:, 2, :, :], sm[:, 0, :, :], ALU.subtract).then_inc(ssd_small, 1)
                dve.wait_ge(ssd_exp, 1)
                dve.wait_ge(big_dve, nbig[0])
                ea, te, dcy = ex[:, 0, :, :], ex[:, 1, :, :], ex[:, 2, :, :]
                for t in range(NT):
                    xs = xsB[:, t, 0:256].rearrange("p (h n) -> p h n", h=4)
                    dve.wait_ge(big_act, taken_by(("uT", 2))[1])
                    for d in range(2):
                        step(V.tensor_tensor(xdt[:, d, :, :], xs, rep(dt_[:, t, 4 * d:4 * d + 4], 2, HD), ALU.mult))
                    settle()
                    step(V.tensor_tensor(xde.rearrange("p d h n -> p (d h) n"), xdt.rearrange("p d h n -> p (d h) n"),
                                         rep(te[:, t, :], 2, HD), ALU.mult))
                    step(V.tensor_tensor(bo[:, t, :].rearrange("p (h n) -> p h n", h=4), xs, rep(r_("dskip"), 2, HD), ALU.mult))
                    dve.wait_ge(big_act, taken_by(("dec", t, 1))[1])
                    E4 = E.rearrange("p (d h) l -> p d h l", d=2)
                    M4 = Mt.rearrange("p (d h) l -> p d h l", d=2)
                    for g in range(2):
                        b = grab(("GT", t, g))
                        for d in range(2):
                            ins = V.tensor_tensor(M4[:, d, 2 * g:2 * g + 2, :], E4[:, d, 2 * g:2 * g + 2, :],
                                                  rep(b[:, 0:P], 1, 2), ALU.mult)
                            if d:
                                gave(("GT", t, g), ins)
                            else:
                                step(ins)
                    settle()
                    dve.wait_ge(big_dve, nbig[0])
                    V.tensor_copy(xmark, dt_[:, 0, 0:1]).then_inc(mt_ready, 1)
                    if t:
                        b = grab(("st", t))
                        d, src, dst = t - 1, 2 * (t - 1), 2 * (t - 1) + 1
                        for g in range(2):
                            r = slice(g * HD, (g + 1) * HD)
                            hh = hin[r, dst, :].rearrange("p (h n) -> p h n", h=2)
                            step(V.tensor_tensor(hh, hin[r, src, :].rearrange("p (h n) -> p h n", h=2),
                                                 rep(dcy[r, t, 4 * d + 2 * g:4 * d + 2 * g + 2], 2, HD), ALU.mult))
                        settle()
                        gave(("st", t), V.tensor_tensor(hin[:, dst, :], hin[:, dst, :], b[:, 0:P], ALU.add))
                    b = grab(("y", t))
                    gave(("y", t), V.tensor_tensor(bo[:, t, :], bo[:, t, :], b[:, 0:256], ALU.add))
                    dve.wait_ge(big_dve, nbig[0])
                V.tensor_copy(xmark, dt_[:, 0, 0:1]).then_inc(h_in, 1)
                for t in (1, 2):
                    for g in range(2):
                        b = grab(("yo", t, g))
                        yt = at(po, 256).rearrange("p (d h n) -> p d h n", d=2, h=2)
                        for d in range(2):
                            ins = V.tensor_tensor(yt[:, d, :, :], b[:, d * P:(d + 1) * P].rearrange("p (h n) -> p h n", h=2),
                                                  rep(ea[:, t, 4 * d + 2 * g:4 * d + 2 * g + 2], 2, HD), ALU.mult)
                            if d:
                                gave(("yo", t, g), ins)
                            else:
                                step(ins)
                        settle()
                        dve.wait_ge(big_dve, nbig[0])
                        o = bo[:, t, g * P:(g + 1) * P].rearrange("p (h n) -> p h n", h=2)
                        for d in range(2):
                            link(V.tensor_tensor(o, o, yt[:, d, :, :], ALU.add))
                link(V.tensor_tensor(bo[:, :, :], bo[:, :, :], sz[:, :, :], ALU.mult))
                sq = at(po, NT * 256).rearrange("p (t n) -> p t n", t=NT)
                link(V.tensor_tensor(sq, bo[:, :, :], bo[:, :, :], ALU.mult))
                link(V.tensor_reduce(st[:, 5, 0:NT], sq, AX.X, ALU.add))
                y = rsqrt(st[:, 5, 0:NT], NT, 256)
                for t in range(NT):
                    ins = V.scalar_tensor_tensor(bo[:, t, :], bo[:, t, :], y[:, t:t + 1], r_("gssm"), ALU.mult, ALU.mult)
                    if t == NT - 1:
                        ins.then_inc(bo_ready, 1)
                    else:
                        step(ins)
                settle()
                lift(3)

                for k in range(1, KD, 2):
                    b = grab(("mT", k))
                    gave(("mT", k), V.tensor_scalar(hT[:, k, :], b[:, 0:T], 0.5, None, ALU.mult))
                dve.wait_ge(big_act, taken_by(("gb", 1, 1))[1])
                for t in range(NT):
                    for h in range(2):
                        b = grab(("out", t, h))
                        cols = slice(h * HALF, (h + 1) * HALF)
                        gave(("out", t, h), V.tensor_tensor(gtmp[:, h, :], b[:, :], gbc[:, min(t, 1), cols], ALU.mult))
                        dve.wait_ge(big_dve, nbig[0])
                        ins = V.tensor_tensor(x[:, t, cols], x[:, t, cols], gtmp[:, h, :], ALU.add)
                        if h:
                            ins.then_inc(x_ready, 1)
                        else:
                            step(ins)
                    settle()
                norm_rows()
                modulate("h2T", 1)
                dve.wait_ge(ssm_out, (li + 1) * 64)
                b = grab(("lg",))
                lg = b[:, 0:48].rearrange("p (t e) -> p t e", t=NT)
                link(V.tensor_reduce(st[:, 0, 0:NT], lg, AX.X, ALU.max))
                gave(("lg",), V.tensor_tensor(aff[:, :, :], lg, rep(st[:, 0, 0:NT], 2, NE), ALU.subtract))
                dve.wait_ge(big_dve, nbig[0])
                V.tensor_copy(xmark, dt_[:, 0, 0:1]).then_inc(aff_in, 1)
                dve.wait_ge(aff_exp, 1)
                link(V.tensor_reduce(st[:, 1, 0:NT], aff[:, :, :], AX.X, ALU.add))
                link(V.reciprocal(st[:, 2, 0:NT], st[:, 1, 0:NT]))
                V.tensor_tensor(aff[:, :, :], aff[:, :, :], rep(st[:, 2, 0:NT], 2, NE), ALU.mult).then_inc(aff_ready, 1)
                dve.wait_ge(big_act, taken_by(("affT",))[1])
                for c0, c1, rounds in ((0, P, CAP[0] // 8), (P, T, CAP[1] // 8)):
                    src = affT[:, c0:c1]
                    for _ in range(rounds):
                        link(V.max(top8, src))
                        link(V.match_replace(wrk[:, c0:c1], top8, src, -1.0))
                        src = wrk[:, c0:c1]
                V.tensor_scalar(maskT, wrk, 0.0, None, ALU.is_lt).then_inc(mask_ready, 1)
                b = grab(("rank",))
                rk = b[:, 0:48].rearrange("p (t e) -> p t e", t=NT)
                step(V.tensor_tensor(pos[:, 0, :], rk[:, 0, :], msk[:, 0, :], ALU.mult))
                gave(("rank",), V.scalar_tensor_tensor(pos[:, 1:3, :], rk[:, 1:3, :], float(CAP[0]), msk[:, 1:3, :],
                                                       ALU.add, ALU.mult))
                settle()
                dve.wait_ge(big_dve, nbig[0])
                link(V.tensor_scalar(pos[:, :, :], pos[:, :, :], -1.0, None, ALU.add))
                iota = c_("iota")
                step(V.tensor_tensor(Sc[:, :, :], rep(iota[:, 0:CAP[0]], 1, NE), rep(pos[:, 0, :], 2, CAP[0]), ALU.is_equal))
                step(V.tensor_tensor(Sl[:, 0, :, :], rep(iota[:, CAP[0]:CE], 1, NE), rep(pos[:, 1, :], 2, CAP[1]), ALU.is_equal))
                step(V.tensor_tensor(Sl[:, 1, :, :], rep(iota[:, CAP[0]:CE], 1, NE), rep(pos[:, 2, :], 2, CAP[1]), ALU.is_equal))
                settle()
                V.memset(XT[:, :, NE * CE:784], 0.0).then_inc(hot_ready, 1)
                XTe = XT[:, :, 0:NE * CE].rearrange("p k (e c) -> p k e c", c=CE)
                for k in range(1, KD, 2):
                    b = grab(("xc", k))
                    gave(("xc", k), V.tensor_scalar(XTe[:, k, :, 0:CAP[0]], b[:, 0:256].rearrange("p (e c) -> p e c", e=NE),
                                                    gs[:, 1, k, 0:1], modc[:, 2, k, 0:1], ALU.mult, ALU.add))
                    b = grab(("xl", k))
                    gave(("xl", k), V.tensor_scalar(XTe[:, k, :, CAP[0]:CE], b[:, :].rearrange("p (e c) -> p e c", e=NE),
                                                    gs[:, 1, k, 1:2], modc[:, 2, k, 1:2], ALU.mult, ALU.add))
                dve.wait_ge(big_dve, nbig[0])
                dve.wait_ge(big_act, taken_by(("xl", KD - 2))[1])
                dve.wait_ge(hot_ready, 1)

                with dve.Fori(0, NE) as e:
                    dve.wait_ge(h3_ready, e)
                    V.tensor_copy(xcur[:, :, :], XT[:, :, bass.ds(e * CE, 64)]).then_inc(xc_ready, 1)
                    dve.wait_ge(sg_ready, e)
                    for t in range(NT):
                        ins = V.tensor_scalar(sgs[:, t, :], iota, pos[:, t, bass.ds(e, 1)], aff[:, t, bass.ds(e, 1)],
                                              ALU.is_equal, ALU.mult)
                    ins.then_inc(w1hot, 1)
                    dve.wait_ge(silu_ready, e + 1)
                    V.tensor_tensor(hid.rearrange("p b n -> p (b n)"), hs, banks[7][:, :], ALU.mult).then_inc(hid_ready, 1)
                    dve.wait_ge(sg_ready, e + 1)
                    V.tensor_copy(sgT.rearrange("p t c -> p (t c)"), banks[6][:, 0:T]).then_inc(sgs_ready, 1)
                for t in range(NT):
                    if t < 2:
                        dve.wait_ge(gb2_sb, 2 * t + 2)
                    for h in range(2):
                        cols = slice(h * HALF, (h + 1) * HALF)
                        link(V.tensor_tensor(gtmp[:, h, :], banks[2 * t + h][:, :], gbc[:, min(t, 1), cols], ALU.mult))
                        step(V.tensor_tensor(x[:, t, cols], x[:, t, cols], gtmp[:, h, :], ALU.add))
                    settle()
                dve.drain().then_inc(done_dve, 1)
                dve.wait_ge(layer_go, li + 1)
                dve.sem_inc(dummy_dve, 1)
            dve.drain().then_inc(x_final, 1)


_OUTS = [((1, 128, 1024), "float32"), ((1, 256, 1024), "float32"),
         ((1, 2, 128, 2, 64), "float32"), ((1, 2, 128, 2, 64), "float32"),
         ((1, 2, 128, 2, 64), "float32"), ((1, 2, 128, 2, 64), "float32"),
         ((1, 2, 2, 4, 64, 64), "float32"),
         ((1, 2, 128, 4, 2, 32), "float32"), ((1, 2, 128, 4, 64), "float32")]


def constants():
    import numpy as np
    c = np.zeros((P, NCST), np.float32)

    def put(name, a):
        c[:, CST[name][0]:CST[name][1]] = a

    i = np.arange(P)
    put("ident", np.eye(P))
    put("upto", i[:, None] <= i[None, :])
    put("from", i[:, None] >= i[None, :])
    put("negbelow", np.where(i[None, :] < i[:, None], -1e30, 0.0))
    put("negabove", np.where(i[None, :] > i[:, None], -1e30, 0.0))
    put("ones", 1.0)
    put("sel", (i[:, None] % 32) == np.arange(2)[None, :])
    put("selb", np.repeat((i[:, None] % 32) == np.arange(2)[None, :], P, axis=1))
    put("iota", np.tile(np.arange(64), 2)[None, :])
    put("bias1", (np.arange(32) < 2)[None, :])
    for width, cn, sn in ((64, "cos", "sin"), (32, "cosd", "sind")):
        n = width // 4
        inv = np.float32(10000.0) ** (-np.arange(n, dtype=np.float32) / np.float32(n))
        inv = inv.astype(np.float32)
        tok = np.arange(256)
        ang = np.stack([(tok // 64)[:, None].astype(np.float32) * inv, (tok % 64)[:, None].astype(np.float32) * inv], 1)
        cos, sin = np.cos(ang), np.sin(ang)
        full_c = np.stack([cos, cos], 2).reshape(2, P, width)
        full_s = np.stack([-sin, sin], 2).reshape(2, P, width)
        put(cn, full_c.transpose(1, 0, 2).reshape(P, 2 * width))
        put(sn, full_s.transpose(1, 0, 2).reshape(P, 2 * width))
    return c


def kernel(**inputs):
    import math

    import numpy as _np
    import concourse.bacc as _bacc
    from concourse.bass_utils import run_bass_kernel_spmd as _run

    n = {k: _np.asarray(v) for k, v in inputs.items()}
    f32 = _np.float32
    init = [0.8 - 0.6 * math.exp(-0.3 * i) for i in range(DEPTH)]
    rows = [n["g_qa"], n["g_qb"], n["g_ka"], n["g_kb"], n["g_qd"], n["g_kd"], n["g_dout"], n["lam_q1"], n["lam_q2"],
            n["lam_k1"], n["lam_k2"], n["sink_b"], n["a_log"].reshape(DEPTH, 8), n["dt_bias"].reshape(DEPTH, 8),
            n["d_skip"], n["g_ssm"], _np.array(init, f32)[:, None], (1 - _np.array(init))[:, None].astype(f32)]
    cols = [n["g_norm1"].reshape(DEPTH, KD, P).transpose(0, 2, 1), n["g_norm2"].reshape(DEPTH, KD, P).transpose(0, 2, 1),
            n["conv_w"].reshape(DEPTH, 5, 4, P).transpose(0, 3, 2, 1).reshape(DEPTH, P, 20),
            n["conv_b"].reshape(DEPTH, 4, P).transpose(0, 2, 1)]
    ssm = n["state_ssm"][0].reshape(DEPTH, 2, 2, 2, 64, 64).transpose(0, 3, 4, 1, 2, 5).reshape(DEPTH, P, 256)
    cache = [n["cache_" + k][0].reshape(DEPTH, P, -1) for k in ("a_k", "b_k", "a_v", "b_v", "d_k", "d_v")] + [ssm]
    cvec = _np.stack([n["c_ctx"], n["c"][0]], axis=-1).reshape(KD, P, 2).transpose(1, 0, 2)
    arrays = {
        "x_prompt": n["x_prompt"], "x_sample": n["x_sample"], "cvecT": cvec, "rowp": _np.concatenate(rows, axis=1),
        "colp": _np.concatenate(cols, axis=2), "caches": _np.concatenate(cache, axis=2), "b_ada": n["b_ada"],
        "w_ada": n["w_ada"], "w_in": n["w_in"], "w_br": n["w_br"], "w_out": n["w_out"], "w_router": n["w_router"],
        "w_e1": n["w_e1"], "w_e3": n["w_e3"], "w_e2": n["w_e2"], "consts": constants(),
    }
    nc = _bacc.Bacc("TRN2", target_bir_lowering=False, num_devices=1)
    sent, args = {}, []
    for name, a in arrays.items():
        sent[f"in_{name}"] = _np.ascontiguousarray(a)
        args.append(nc.dram_tensor(f"in_{name}", a.shape, mybir.dt.from_np(a.dtype), kind="ExternalInput").ap())
    for i, (shape, dtype) in enumerate(_OUTS):
        args.append(nc.dram_tensor(f"out_{i}", shape, mybir.dt.from_np(_np.dtype(dtype)), kind="ExternalOutput").ap())
    trunk_kernel(nc, *args)
    r = _run(nc, [sent], core_ids=[0])
    return tuple(r.results[0][f"out_{i}"] for i in range(len(_OUTS)))
```

```python
from contextlib import ExitStack

import concourse.bass as bass
from concourse import mybir

P = 128
D = 1024
KD = D // P
NT = 3
T = NT * P
DEPTH = 2
HD = 64
NE = 16
CAP = (16, 32)
CE = CAP[0] + CAP[1]
EPS = 1e-6
HALF = 512
SLOTS = 4
AT_ADA = (0, 2, 20, 22, 25, 30)
AT_AB, AT_D, AT_C, AT_OUT = 4, 6, 8, 28
AT_GATE = (10, 12, 15, 18)
AT_LIFT = (14, 17, 24, 27)
LOADS0 = 32
LOADS = LOADS0 + NE * 6
PER_SLOT = LOADS // SLOTS
BRANCH = (0, 1, 3, 2)
COL_A, COL_B, COL_C, COL_D, COL_G = 0, 512, 1024, 1800, 2568
NC_ = 776
ND_ = 768
PADW = 392
NU_CONV = PADW - 4
LAT0 = 132

F32 = mybir.dt.float32
ACT = mybir.ActivationFunctionType
ALU = mybir.AluOpType
AX = mybir.AxisListType

ROW = {}
_at = 0
for _name, _n in (("gq", 128), ("gk", 128), ("gqd", 32), ("gkd", 32), ("gdout", 64), ("lamq", 64), ("lamk", 64),
                  ("sink", 4), ("alog", 8), ("dtb", 8), ("dskip", 4), ("gssm", 256), ("laminit", 1), ("onemlam", 1)):
    ROW[_name] = (_at, _at + _n)
    _at += _n
NROW = _at
COLS = {"gn1": (0, 8), "gn2": (8, 16), "convw": (16, 36), "convb": (36, 40), "bada": (40, 72)}
NCOL = 72
CACHE = {"ak": (0, 128), "bk": (128, 256), "av": (256, 384), "bv": (384, 512), "dk": (512, 768), "dv": (768, 1024),
         "ssm": (1024, 1280)}
NCACHE = 1280
CST = {}
_at = 0
for _name, _n in (("ident", 128), ("upto", 128), ("from", 128), ("negbelow", 128), ("negabove", 128), ("ones", 128),
                  ("sel", 2), ("selb", 256), ("iota", 128), ("cos", 128), ("sin", 128),
                  ("cosd", 64), ("sind", 64), ("zero", 128)):
    CST[_name] = (_at, _at + _n)
    _at += _n
NCST = _at




def big_results():
    out = []
    for v in range(2):
        out += [(("row", v, h), "act") for h in range(2)]
    out += [(("col", v), "dve") for v in range(2)]
    out += [(("hT", k), "dve" if k % 2 else "act") for k in range(KD)]
    out += [(("ab", t, b), "act") for b in range(2) for t in range(NT)]
    for t in range(NT):
        out += [(("dqk", t), "act"), (("dv", t), "act")]
    out += [(("zdt", t), "act") for t in range(NT)]
    out += [(("xbc", g), "act") for g in range(4)]
    out += [(("g", 0, t, h), "act") for t in range(NT) for h in range(2)]
    out += [(("qkT", t, b), "act") for t in range(NT) for b in range(2)] + [(("ckT",), "act")]
    out += [(("dT", t), "act") for t in range(NT)] + [(("cdT",), "act")]
    for i in range(4):
        if i < 3:
            out += [(("g", i + 1, t, h), "act") for t in range(NT) for h in range(2)]
        if i == 2:
            out += [(("row", 2, h), "act") for h in range(2)]
            out += [(("uT", t), "act") for t in range(NT)]
            out += [(("cum",), "dve"), (("h0T",), "act")]
            out += [(("row", 3, h), "act") for h in range(2)]
            out += [(("dec", 0, d), "act") for d in range(2)]
        if i == 3:
            for t in range(NT):
                out += [(("GT", t, 0), "dve"), (("GT", t, 1), "dve")]
                if t + 1 < NT:
                    out += [(("dec", t + 1, d), "act") for d in range(2)]
            out.append((("row", 4, 0), "act"))
            out += [(("yo", t, g), "dve") for t in (1, 2) for g in range(2)]
            out += [(("row", 4, 1), "act"), (("col", 3), "dve")]
        out += [(("boT", i, k), "dve") for k in range(2)]
        out += [(("up", i, t, h), "dve") for t in range(NT) for h in range(2)]
    out.append((("col", 4), "dve"))
    out += [(("mT", k), "dve" if k % 2 else "act") for k in range(KD)]
    out += [(("gb", g, h), "act") for g in range(2) for h in range(2)]
    out += [(("out", t, h), "dve") for t in range(NT) for h in range(2)]
    out.append((("row", 5, 0), "act"))
    out += [(("h2T", k), "dve" if k % 2 else "act") for k in range(KD)]
    out += [(("lg",), "dve"), (("affT",), "act"), (("row", 5, 1), "act"), (("mk",), "act"), (("rank",), "dve")]
    out += [(("gb2", g, h), "act") for g in range(2) for h in range(2)]
    for k in range(KD):
        out += [(("xc", k), "dve" if k % 2 else "act"), (("xl", k), "dve" if k % 2 else "act")]
    return out


BIG = big_results()
BIG_AT = {name: n for n, (name, _) in enumerate(BIG)}
BIG_BY = dict(BIG)


def taken_by(name):
    n = BIG_AT[name]
    by = BIG[n][1]
    return by, sum(1 for _, e in BIG[:n + 1] if e == by)


def trunk_kernel(nc, x_prompt, x_sample, cvecT, rowp, colp, caches, b_ada, w_ada, w_in, w_br, w_out, w_router,
                 w_e1, w_e3, w_e2, consts, y_prompt, y_sample, o_ak, o_av, o_bk, o_bv, o_ssm, o_dk, o_dv):
    with ExitStack() as ctx:
        def sb(name, shape):
            return ctx.enter_context(nc.sbuf_tensor(name, shape, F32))

        def sem(name):
            return ctx.enter_context(nc.semaphore(name))

        ring = sb("ring", [P, SLOTS, 4, D])
        x = sb("x", [P, NT, D])
        xn = sb("xn", [P, NT, D])
        hT = sb("hT", [P, KD, T])
        cst = sb("cst", [P, NCST])
        gaterow = sb("gaterow", [P, 2, D])
        rp = sb("rp", [P, NROW])
        cp = sb("cp", [P, NCOL])
        ca = sb("ca", [P, NCACHE])
        wr = sb("wr", [P, KD, NE])
        cs = sb("cs", [P, KD, 2])
        csw = sb("csw", [P, KD, 32])
        modc = sb("modc", [P, 4, KD, 2])
        gs = sb("gs", [P, 2, KD, 2])
        st = sb("st", [P, 6, 48])
        stw = sb("stw", [P, 48])
        dsm = sb("dsm", [P, 88])
        expa, lamd, lamx, nlam, nsink = dsm[:, 0:8], dsm[:, 8:10], dsm[:, 10:12], dsm[:, 12:13], dsm[:, 13:17]
        xmark = dsm[:, 17:18]
        lamt = dsm[:, 20:84]
        used = [0]
        SCR = 20520
        scr = sb("scr", [P, SCR])

        def at(off, n):
            assert off + n <= SCR
            return scr[:, off:off + n]

        def take(n):
            used[0] += n
            return at(used[0] - n, n)

        G = [take(NT * D).rearrange("p (t n) -> p t n", t=NT) for _ in range(2)]
        abo = used[0]
        AB = take(2304).rearrange("p (t b n) -> p t b n", t=NT, b=2)
        qko = used[0]
        qT = take(2 * 2 * T).rearrange("p (b g t) -> p b g t", b=2, g=2)
        kT = take(2 * 512).rearrange("p (b t) -> p b t", b=2)
        dqT = take(2 * T).rearrange("p (c t) -> p c t", c=2)
        dkT = take(2 * 512).rearrange("p (c t) -> p c t", c=2)
        vab = take(NT * 256).rearrange("p (t b n) -> p t b n", t=NT, b=2)
        vd = take(NT * 256).rearrange("p (t n) -> p t n", t=NT)
        qkend = used[0]
        sz = take(NT * 256).rearrange("p (t n) -> p t n", t=NT)
        xbc = take(4 * PADW).rearrange("p (g n) -> p g n", g=4)
        uT = xbc[:, :, 0:T]
        bof = used[0]
        bo = take(NT * 256).rearrange("p (t n) -> p t n", t=NT)
        boT = take(2 * T).rearrange("p (c t) -> p c t", c=2)
        DQ = at(bof, NT * 512).rearrange("p (t n) -> p t n", t=NT)
        po = used[0]
        pr = take(2 * 768).rearrange("p (i n) -> p i n", i=2)
        pT = take(2 * T).rearrange("p (i n) -> p i n", i=2)
        tmp = at(po, 2 * 768).rearrange("p (i n) -> p i n", i=2)
        cacc = at(po, 4 * NU_CONV).rearrange("p (i n) -> p i n", i=4)
        so = [qko]

        def over(n):
            so[0] += n
            assert so[0] <= qkend
            return at(so[0] - n, n)

        xsB = over(NT * 384).rearrange("p (t n) -> p t n", t=NT)
        E = over(8 * P).rearrange("p (j l) -> p j l", j=8)
        Mt = over(8 * P).rearrange("p (j l) -> p j l", j=8)
        xdt = over(512).rearrange("p (d h n) -> p d h n", d=2, h=4)
        xde = over(512).rearrange("p (d h n) -> p d h n", d=2, h=4)
        hin = over(512).rearrange("p (i n) -> p i n", i=4)
        sst = over(256).rearrange("p (i n) -> p i n", i=4)
        sm = over(72).rearrange("p (i t j) -> p i t j", i=3, t=NT)
        ex = over(72).rearrange("p (i t j) -> p i t j", i=3, t=NT)
        nacs = over(24).rearrange("p (t j) -> p t j", t=NT)
        dtk = sb("dtk", [P, 5, 24])
        dtr, dt_, la = (dtk[:, i, :].rearrange("p (t j) -> p t j", t=NT) for i in range(3))
        dabs = dtk[:, 3, :].rearrange("p (t j) -> p t j", t=NT)
        dexp = dtk[:, 4, :].rearrange("p (t j) -> p t j", t=NT)
        rsb = at(abo, 2 * D).rearrange("p (i n) -> p i n", i=2)
        gbc = at(0, 2 * D).rearrange("p (g n) -> p g n", g=2)
        gtmp = at(2 * D, D).rearrange("p (i n) -> p i n", i=2)
        eo = [0]

        def exp_take(n):
            eo[0] += n
            return at(eo[0] - n, n)

        eo[0] = 3 * D
        XT = exp_take(KD * 784).rearrange("p (k c) -> p k c", k=KD)
        Sc = exp_take(256).rearrange("p (e c) -> p e c", e=NE)
        Sl = exp_take(2 * 512).rearrange("p (i e c) -> p i e c", i=2, e=NE)
        xcur = exp_take(KD * 64).rearrange("p (k c) -> p k c", k=KD)
        sgs = exp_take(T).rearrange("p (t c) -> p t c", t=NT)
        sgT = exp_take(T).rearrange("p (t c) -> p t c", t=NT)
        hs = exp_take(HALF)
        hid = exp_take(HALF).rearrange("p (b n) -> p b n", b=4)
        hidT = exp_take(HALF).rearrange("p (b n) -> p b n", b=4)
        yo = exp_take(HALF)
        aff = exp_take(48).rearrange("p (t e) -> p t e", t=NT)
        pos = exp_take(48).rearrange("p (t e) -> p t e", t=NT)
        msk = exp_take(48).rearrange("p (t e) -> p t e", t=NT)
        affT = scr[0:NE, eo[0]:eo[0] + T]
        wrk = scr[0:NE, eo[0] + T:eo[0] + 2 * T]
        top8 = scr[0:NE, eo[0] + 2 * T:eo[0] + 2 * T + 8]
        maskT = scr[0:NE, eo[0] + 2 * T + 8:eo[0] + 3 * T + 8]
        assert eo[0] + 3 * T + 8 <= SCR

        banks = [ctx.enter_context(nc.psum_tensor(f"bank{i}", [P, 512], F32)) for i in range(8)]

        def c_(name):
            return cst[:, CST[name][0]:CST[name][1]]

        def r_(name):
            return rp[:, ROW[name][0]:ROW[name][1]]

        def ch(name):
            return ca[:, CACHE[name][0]:CACHE[name][1]]

        ident = c_("ident")
        gqc = r_("gq").rearrange("p (b n) -> p b n", b=2)
        gkc = r_("gk").rearrange("p (b n) -> p b n", b=2)

        def rep(ap, axis, n):
            a = ap.unsqueeze(axis)
            shape = list(a.shape)
            shape[axis] = n
            return a.broadcast_to(shape)

        loaded = [sem(f"loaded{i}") for i in range(SLOTS)]
        freed = [sem(f"freed{i}") for i in range(SLOTS)]
        in_x = sem("in_x")
        in_cst = sem("in_cst")
        in_cond = sem("in_cond")
        cond0 = sem("cond_zero")
        cond = sem("cond_ready")
        done_pe, done_act, done_dve, done_pool = (sem(f"done_{e}") for e in ("pe", "act", "dve", "pool"))
        layer_go = sem("layer_go")
        dummy, dummy_pe, dummy_act, dummy_dve, dummy_sp = (sem(f"passed_{e}") for e in ("pool", "pe", "act", "dve", "sp"))
        y_out = sem("y_out")
        params = sem("params")
        kv_out = sem("kv_out")
        ssm_out = sem("ssm_out")
        bias_row1, bias_row2 = sem("bias_row1"), sem("bias_row2")
        x_final = sem("x_final")
        layer_sems = []

        def lsem(name):
            layer_sems.append(sem(name))
            return layer_sems[-1]

        pads = lsem("pads")
        big = lsem("big_ready")
        big_act = lsem("big_taken_act")
        big_dve = lsem("big_taken_dve")
        big_of = {"act": big_act, "dve": big_dve}
        mod1 = lsem("mod_ready")
        act_sq = lsem("squares_ready")
        sq_free = lsem("squares_used")
        var_ready = lsem("variance_ready")
        root_ready = lsem("root_ready")
        xn_ready = lsem("xn_ready")
        ab_ready = lsem("ab_ready")
        d_ready = lsem("d_ready")
        dt_abs = lsem("dt_abs")
        dt_log = lsem("dt_log")
        dt_done = lsem("dt_done")
        lam_dot = lsem("lam_dot")
        lam_exp = lsem("lam_exp")
        conv_sum = lsem("conv_sum")
        conv_out = lsem("conv_out")
        s_ready = lsem("scores_ready")
        m_ready = lsem("max_ready")
        aff_in = lsem("aff_in")
        aff_exp = lsem("aff_exp")
        w1hot = lsem("expert_hot")
        p_ready = lsem("probs_ready")
        w_ready = lsem("diffprobs_ready")
        pt_ready = lsem("probsT_ready")
        pts_ready = lsem("probsT_sbuf")
        pv_ready = lsem("pv_ready")
        o_ready = lsem("o_taken")
        bo_ready = lsem("branch_ready")
        merged = lsem("merged")
        ssd_small = lsem("ssd_small")
        ssd_exp = lsem("ssd_exp")
        mt_ready = lsem("mt_ready")
        h_in = lsem("h_in")
        x_ready = lsem("x_ready")
        aff_ready = lsem("aff_ready")
        mask_ready = lsem("mask_ready")
        mk_ready = lsem("mk_ready")
        hot_ready = lsem("hot_ready")
        xc_ready = lsem("xcur_ready")
        h3_ready = lsem("h3_ready")
        silu_ready = lsem("silu_ready")
        hid_ready = lsem("hid_ready")
        ht_ready = lsem("hidT_ready")
        hts_ready = lsem("hidT_sbuf")
        yp_ready = lsem("yo_psum")
        sg_ready = lsem("sgT_ready")
        sgs_ready = lsem("sgT_sbuf")
        yo_ready = lsem("yo_sbuf")
        sty_ready = lsem("tile_products")
        st0_taken = lsem("states_taken")
        y_taken = lsem("tile_taken")
        closed = lsem("sums_closed")
        act_step = lsem("act_step")
        dve_step = lsem("dve_step")
        numbers = sorted(s.num for s in layer_sems)
        assert numbers == list(range(numbers[0], numbers[0] + len(numbers)))

        def iters(i):
            return [(h, t) for h in range(4) for t in range(NT)]

        NIT = 12

        block = ctx.enter_context(nc.Block())

        @block.sync
        def _(sp):
            sp.dma_start(cs[:, :, :], cvecT).then_inc(in_cond, 16)

            def load(n, s, src, cols, chunks=4):
                sp.wait_ge(freed[s], n)
                sp.dma_start(ring[:, s, 0:chunks, 0:cols],
                             src.rearrange("(k p) n -> p k n", p=P)).then_inc(loaded[s], 16)

            def mixer_weights(li, first, last):
                plan = {}
                for h in range(2):
                    rows = slice(h * HALF, (h + 1) * HALF)
                    for v in range(6):
                        plan[AT_ADA[v] + h] = (w_ada[li, rows, v * D:(v + 1) * D], D, 4)
                    for j, c0, n in ((AT_AB, COL_A, D), (AT_D, COL_D, ND_), (AT_C, COL_C, NC_)):
                        plan[j + h] = (w_in[li, rows, c0:c0 + n], n, 4)
                    for i, br in enumerate(BRANCH):
                        plan[AT_GATE[i] + h] = (w_in[li, rows, COL_G + br * D:COL_G + (br + 1) * D], D, 4)
                    plan[AT_OUT + h] = (w_out[li, rows, :], D, 4)
                for i, br in enumerate(BRANCH):
                    plan[AT_LIFT[i]] = (w_br[li, br, :, :], D, 2)
                assert sorted(plan) == list(range(LOADS0))
                for j in range(first, last):
                    src, cols, chunks = plan[j]
                    load(li * PER_SLOT + j // SLOTS, j % SLOTS, src, cols, chunks)

            def expert_weights(li):
                base = li * PER_SLOT
                with sp.Fori(0, NE // 2) as ep:
                    for i in range(12):
                        w = (w_e1, w_e3, w_e2)[(i % 6) // 2]
                        h = i % 2
                        load(base + LOADS0 // SLOTS + ep * 3 + i // SLOTS, i % SLOTS,
                             w[li, ep * 2 + i // 6, h * HALF:(h + 1) * HALF, :], D)

            def layer_end(li):
                for s in (done_pe, done_act, done_dve, done_pool):
                    sp.wait_ge(s, li + 1)
                sp.sem_inc(dummy_sp, 1)
                sp.sem_clear(range(numbers[0], numbers[-1] + 1))
                sp.sem_inc(layer_go, 1)

            mixer_weights(0, 0, 2)
            sp.dma_start(x[:, 0, :], x_prompt.rearrange("a s d -> (a s) d")).then_inc(in_x, 16)
            sp.dma_start(x[:, 1:3, :], x_sample.rearrange("a (t p) d -> p (a t) d", p=P)).then_inc(in_x, 16)
            sp.dma_start(cst[:, :], consts).then_inc(in_cst, 16)
            mixer_weights(0, 2, SLOTS)
            with sp.Fori(0, DEPTH - 1) as li:
                mixer_weights(li, SLOTS, LOADS0)
                expert_weights(li)
                mixer_weights(li + 1, 0, SLOTS)
                layer_end(li)
            mixer_weights(DEPTH - 1, SLOTS, LOADS0)
            expert_weights(DEPTH - 1)
            layer_end(DEPTH - 1)
            sp.wait_ge(x_final, 1)
            sp.dma_start(y_prompt.rearrange("a s d -> (a s) d"), x[:, 0, :]).then_inc(y_out, 16)
            sp.dma_start(y_sample.rearrange("a (t p) d -> p (a t) d", p=P), x[:, 1:3, :]).then_inc(y_out, 16)
            sp.wait_ge(y_out, 32)

        @block.gpsimd
        def _(pool):
            def parameters(li):
                pool.dma_start(cp[:, :], colp[li, :, :]).then_inc(params, 16)
                pool.dma_start(rp[:, :], rowp[li, :].partition_broadcast(P)).then_inc(params, 16)
                pool.dma_start(ca[:, :], caches[li, :, :]).then_inc(params, 16)
                pool.dma_start(wr[:, :, :], w_router[li, :, :].rearrange("(k p) e -> p k e", p=P)).then_inc(params, 16)

            def mixers(li):
                pool.memset(xbc[:, :, :], 0.0).then_inc(pads, 1)
                pool.wait_ge(ab_ready, 1)
                pool.dma_start(o_ak[0, li].rearrange("s h d -> s (h d)"), AB[:, 0, 0, 256:384]).then_inc(kv_out, 16)
                pool.dma_start(o_bk[0, li].rearrange("s h d -> s (h d)"), AB[:, 0, 1, 256:384]).then_inc(kv_out, 16)
                pool.wait_ge(big_act, taken_by(("ab", 0, 1))[1])
                pool.dma_start(o_av[0, li].rearrange("s h d -> s (h d)"), vab[:, 0, 0, :]).then_inc(kv_out, 16)
                pool.dma_start(o_bv[0, li].rearrange("s h d -> s (h d)"), vab[:, 0, 1, :]).then_inc(kv_out, 16)
                pool.wait_ge(d_ready, 1)
                pool.dma_start(o_dk[0, li].rearrange("s h m d -> s (h m d)"), DQ[:, 0, 256:512]).then_inc(kv_out, 16)
                pool.wait_ge(big_act, taken_by(("dv", 0))[1])
                pool.dma_start(o_dv[0, li].rearrange("s h d -> s (h d)"), vd[:, 0, :]).then_inc(kv_out, 16)

                def bias_row(i, v):
                    pool.wait_ge(big_act, taken_by(("row", v, 1))[1])
                    pool.dma_start(gaterow[2:3, i, :], b_ada[li, v * D:(v + 1) * D].unsqueeze(0)).then_inc((bias_row1, bias_row2)[i], 16)

                bias_row(0, 2)
                pool.wait_ge(st0_taken, 1)
                for d in range(2):
                    for g in range(2):
                        pool.dma_start(o_ssm[0, li, d, 2 * g:2 * g + 2].rearrange("h p n -> (h p) n"),
                                       sst[:, 2 * d + g, :]).then_inc(ssm_out, 16)
                bias_row(1, 5)
                pool.wait_ge(kv_out, (li + 1) * 96)
                pool.sem_inc(dummy, 1)
                pool.wait_ge(ssm_out, (li + 1) * 64)
                pool.sem_inc(dummy, 1)
                pool.wait_ge(bias_row2, (li + 1) * 16)
                pool.sem_inc(dummy, 1)

            def layer_end(li):
                pool.drain().then_inc(done_pool, 1)
                pool.wait_ge(layer_go, li + 1)
                pool.sem_inc(dummy, 1)

            pool.memset(csw[:, :, :], 0.0).then_inc(cond0, 1)
            parameters(0)
            with pool.Fori(0, DEPTH - 1) as li:
                mixers(li)
                pool.wait_ge(big_dve, taken_by(("lg",))[1])
                parameters(li + 1)
                layer_end(li)
            mixers(DEPTH - 1)
            layer_end(DEPTH - 1)

        @block.tensor
        def _(pe):
            owed = []

            def mm(out, lhsT, rhs, start=True, stop=True, signal=None, **kw):
                ins = pe.matmul(out, lhsT, rhs, start=start, stop=stop, **kw)
                if signal is not None:
                    ins.then_inc(signal, 1)
                elif owed:
                    ins.then_inc(owed.pop(0), 1)
                return ins

            def turn(out, in_, signal=None):
                k = in_.shape[0]
                ins = pe.transpose(out, in_, ident[0:k, 0:k])
                if signal is not None:
                    ins.then_inc(signal, 1)
                elif owed:
                    ins.then_inc(owed.pop(0), 1)
                return ins

            count = [0]

            def bank(name):
                n = count[0]
                assert BIG[n][0] == name, (BIG[n], name)
                count[0] += 1
                if n >= 4:
                    by, value = taken_by(BIG[n - 4][0])
                    pe.wait_ge(big_of[by], value)
                return banks[n % 4]

            def taken(name):
                by, value = taken_by(name)
                pe.wait_ge(big_of[by], value)

            pe.wait_ge(cond, 1)
            with pe.Fori(0, DEPTH) as li:
                count[0] = 0
                base = li * PER_SLOT

                def need(j):
                    pe.wait_ge(loaded[j % SLOTS], (base + (j // SLOTS + 1)) * 16)

                def rows(v, h):
                    j = AT_ADA[v]
                    if h == 0:
                        need(j)
                        need(j + 1)
                    b = bank(("row", v, h))
                    cols = slice(h * HALF, (h + 1) * HALF)
                    for k in range(KD):
                        q = 32 * (k % 4)
                        sig = big if k == KD - 1 else freed[j % SLOTS] if h and k == 3 else None
                        mm(b[q:q + 32, :], csw[:, k, :], ring[:, (j + k // 4) % SLOTS, k % 4, cols],
                           start=k < 4, stop=k >= 4, signal=sig)
                    if h:
                        owed.append(freed[(j + 1) % SLOTS])

                def columns(v):
                    taken(("row", v, 1))
                    b = bank(("col", v))
                    for k in range(KD):
                        mm(b[:, 2 * k:2 * k + 2], rsb[:, v % 2, k * P:(k + 1) * P], c_("sel"),
                           signal=big if k == KD - 1 else None)

                for v in range(2):
                    for h in range(2):
                        rows(v, h)
                pe.wait_ge(in_cst, 16)
                for v in range(2):
                    columns(v)

                def widths(name):
                    for k in range(KD):
                        if k == 0:
                            pe.wait_ge(xn_ready, NT * (1 if name == "hT" else 2))
                        b = bank((name, k))
                        for t in range(NT):
                            turn(b[:, t * P:(t + 1) * P], xn[:, t, k * P:(k + 1) * P],
                                 signal=big if t == NT - 1 else None)

                def tokens(out, t, j, cols, signal=None, free=False, ks=range(KD)):
                    for k in ks:
                        sig = None
                        if free and k == 3:
                            sig = freed[j % SLOTS]
                        if k == KD - 1:
                            sig = signal
                        mm(out, hT[:, k, t * P:(t + 1) * P], ring[:, (j + k // 4) % SLOTS, k % 4, cols],
                           start=k == 0, stop=k == KD - 1, signal=sig)
                    if free and KD - 1 in ks:
                        owed.append(freed[(j + 1) % SLOTS])

                widths("hT")
                taken(("hT", KD - 2))
                taken(("hT", KD - 1))
                need(AT_AB)
                need(AT_AB + 1)
                for br in range(2):
                    for t in range(NT):
                        tokens(bank(("ab", t, br))[:, :], t, AT_AB, slice(br * 512, br * 512 + 512), signal=big,
                               free=(br == 1 and t == NT - 1))
                need(AT_D)
                need(AT_D + 1)
                for t in range(NT):
                    tokens(bank(("dqk", t))[:, :], t, AT_D, slice(0, 512), signal=big)
                    tokens(bank(("dv", t))[:, 0:256], t, AT_D, slice(512, 768), signal=big, free=t == NT - 1)
                need(AT_C)
                need(AT_C + 1)
                for t in range(NT):
                    b = bank(("zdt", t))
                    tokens(b[:, 0:256], t, AT_C, slice(0, 256))
                    tokens(b[:, 256:264], t, AT_C, slice(768, 776), signal=big)
                for g in range(4):
                    b = bank(("xbc", g))
                    for k in range(KD):
                        sig = None
                        if g == 3 and k == 3:
                            sig = freed[AT_C % SLOTS]
                        if k == KD - 1:
                            sig = big
                        mm(b[:, 0:T], ring[:, (AT_C + k // 4) % SLOTS, k % 4, 256 + g * P:256 + (g + 1) * P], hT[:, k, :],
                           start=k == 0, stop=k == KD - 1, signal=sig)
                owed.append(freed[(AT_C + 1) % SLOTS])

                gate_bank = [None]

                def gate(i, s, part):
                    j = AT_GATE[i]
                    if s == 0:
                        need(j + part)
                    t, h = s // 2, s % 2
                    if part == 0:
                        gate_bank[0] = bank(("g", i, t, h))
                    tokens(gate_bank[0][:, :], t, j, slice(h * HALF, (h + 1) * HALF), signal=big, free=s == 5,
                           ks=range(4 * part, 4 * part + 4))

                for s in range(6):
                    for part in range(2):
                        gate(0, s, part)

                pe.wait_ge(ab_ready, 1)
                for t in range(NT):
                    for br in range(2):
                        b = bank(("qkT", t, br))
                        for g in range(2):
                            turn(b[:, g * P:(g + 1) * P], AB[:, t, br, g * P:(g + 1) * P])
                        turn(b[:, 256:384], AB[:, t, br, 256:384], signal=big)
                b = bank(("ckT",))
                turn(b[:, 0:P], ch("ak"))
                turn(b[:, P:2 * P], ch("bk"), signal=big)
                pe.wait_ge(d_ready, 1)
                for t in range(NT):
                    b = bank(("dT", t))
                    for c in range(4):
                        turn(b[:, c * P:(c + 1) * P], DQ[:, t, c * P:(c + 1) * P], signal=big if c == 3 else None)
                b = bank(("cdT",))
                turn(b[:, 0:P], ch("dk")[:, 0:P])
                turn(b[:, P:2 * P], ch("dk")[:, P:2 * P], signal=big)
                taken(("cdT",))

                def keys(t):
                    return (0, P) if t == 0 else (P, 512)

                def values(i, h, t):
                    cols = slice((h // 2) * HD, (h // 2) * HD + HD) if i < 2 else slice(h * HD, h * HD + HD)
                    own = [0] if t == 0 else [1, 2]
                    out = [vab[:, s, i, cols] if i < 2 else vd[:, s, cols] for s in own]
                    if t:
                        out.append(ch(("av", "bv", "dv")[i])[:, cols])
                    return out

                def scores(i, n):
                    h, t = iters(i)[n]
                    k0, k1 = keys(t)
                    step = i * NIT + n
                    if i < 2:
                        v, g = h // 2, h % 2
                        rows = slice(v * HD, (v + 1) * HD)
                        b = banks[4 + n % 2]
                        if n >= 2:
                            pe.wait_ge(p_ready, step - 1)
                        elif i:
                            pe.wait_ge(p_ready, i * NIT)
                        masked = i == 1 and t > 0
                        mm(b[:, 0:k1 - k0], qT[rows, i, g, t * P:(t + 1) * P], kT[rows, i, k0:k1], start=True,
                           stop=True, signal=None if masked else s_ready, skip_group_check=masked)
                        if masked:
                            other = slice(P, 2 * P) if t == 1 else slice(0, P)
                            mm(b[:, other], ident, c_("negabove") if t == 1 else c_("negbelow"), start=False, stop=True,
                               signal=s_ready, skip_group_check=True)
                    else:
                        if n:
                            pe.wait_ge(p_ready, 2 * NIT + n)
                        else:
                            pe.wait_ge(p_ready, 2 * NIT)
                        for m in range(2):
                            j = 2 * h + m
                            r = slice(32 * (j % 4), 32 * (j % 4) + 32)
                            mm(banks[4 + m][:, 0:k1 - k0], dqT[r, j // 4, t * P:(t + 1) * P], dkT[r, j // 4, k0:k1],
                               tile_position=(32 * (j % 4), 0), signal=s_ready if m else None)

                def weights(i, n):
                    h, t = iters(i)[n]
                    step = i * NIT + n
                    if i < 2:
                        pe.wait_ge(p_ready, step + 1)
                    else:
                        pe.wait_ge(w_ready, n + 1)
                    if step:
                        pe.wait_ge(pts_ready, step)
                    nb = len(values(i, h, t))
                    for k in range(nb):
                        turn(banks[6][:, k * P:(k + 1) * P], pr[:, n % 2, k * P:(k + 1) * P],
                             signal=pt_ready if k == nb - 1 else None)

                def weighted(i, n):
                    h, t = iters(i)[n]
                    step = i * NIT + n
                    pe.wait_ge(pts_ready, step + 1)
                    if step:
                        pe.wait_ge(o_ready, step)
                    vs = values(i, h, t)
                    for k, v in enumerate(vs):
                        mm(banks[7][:, 0:HD], pT[:, n % 2, k * P:(k + 1) * P], v, start=k == 0, stop=k == len(vs) - 1,
                           signal=pv_ready if k == len(vs) - 1 else None)

                def lift(i):
                    j = AT_LIFT[i]
                    if i < 2:
                        pe.wait_ge(o_ready, (i + 1) * NIT)
                    else:
                        pe.wait_ge(bo_ready, i - 1)
                    for c in range(2):
                        b = bank(("boT", i, c))
                        for t in range(NT):
                            turn(b[:, t * P:(t + 1) * P], bo[:, t, c * P:(c + 1) * P], signal=big if t == NT - 1 else None)
                    taken(("boT", i, 1))
                    need(j)
                    for t in range(NT):
                        for h in range(2):
                            b = bank(("up", i, t, h))
                            for c in range(2):
                                mm(b[:, :], boT[:, c, t * P:(t + 1) * P], ring[:, j % SLOTS, c, h * HALF:(h + 1) * HALF],
                                   start=c == 0, stop=c == 1, signal=big if c == 1 else None)
                    owed.append(freed[j % SLOTS])

                scores(0, 0)
                for i in range(3):
                    for n in range(NIT + 2):
                        if 1 <= n < NIT:
                            scores(i, n)
                        if 1 <= n <= NIT:
                            weights(i, n - 1)
                        if n >= 2:
                            weighted(i, n - 2)
                        if 1 <= n <= NIT:
                            gate(i + 1, (n - 1) // 2, (n - 1) % 2)
                        if i == 2 and n >= NIT:
                            rows(2, n - NIT)
                    if i < 2:
                        scores(i + 1, 0)
                        lift(i)

                pe.wait_ge(conv_out, 4)
                for t in range(NT):
                    b = bank(("uT", t))
                    for g in range(3):
                        turn(b[:, g * P:(g + 1) * P], uT[:, g, t * P:(t + 1) * P], signal=big if g == 2 else None)
                pe.wait_ge(dt_done, 1)
                b = bank(("cum",))
                for t in range(NT):
                    o = t * 16
                    mm(b[:, o:o + 4], c_("upto"), la[:, t, 0:4])
                    mm(b[:, o + 4:o + 8], c_("from"), la[:, t, 4:8])
                    mm(b[:, o + 8:o + 16], c_("ones"), la[:, t, :], signal=big if t == NT - 1 else None)
                b = bank(("h0T",))
                for d in range(2):
                    turn(b[:, d * P:(d + 1) * P], ch("ssm")[:, d * P:(d + 1) * P], signal=big if d else None)
                for h in range(2):
                    rows(3, h)

                def tri(d):
                    return c_("upto") if d == 0 else c_("from")

                def decays(t):
                    for d in range(2):
                        b = bank(("dec", t, d))
                        for h in range(4):
                            mm(b[:, h * P:(h + 1) * P], la[:, t, 4 * d + h:4 * d + h + 1].broadcast_to([P, P]), tri(d),
                               start=h == 0, stop=False, skip_group_check=True)
                        mm(b[:, :], ident, rep(c_("negbelow" if d == 0 else "negabove"), 1, 4), start=False, stop=True,
                           signal=big, skip_group_check=True)

                decays(0)
                lift(2)
                taken(("uT", 2))
                for t in range(NT):
                    for g in range(2):
                        b = bank(("GT", t, g))
                        r = slice(g * HD, (g + 1) * HD)
                        mm(b[:, 0:P], uT[r, 2, t * P:(t + 1) * P], uT[r, 3, t * P:(t + 1) * P], signal=big)
                    if t + 1 < NT:
                        decays(t + 1)
                    pe.wait_ge(mt_ready, t + 1)
                    if t == 1:
                        pe.wait_ge(st0_taken, 1)
                    elif t == 2:
                        pe.wait_ge(y_taken, 1)
                    b = banks[4]
                    if t == 0:
                        for d in range(2):
                            for g in range(2):
                                o = (2 * d + g) * HD
                                mm(b[:, o:o + HD], xde[:, d, 2 * g:2 * g + 2, :], xsB[:, t, 256 + g * HD:256 + (g + 1) * HD],
                                   signal=sty_ready if d and g else None)
                    else:
                        for g in range(2):
                            mm(b[g * HD:(g + 1) * HD, 0:P], xsB[:, t, 256 + g * HD:256 + (g + 1) * HD],
                               xde[:, t - 1, 2 * g:2 * g + 2, :], signal=sty_ready if g else None)
                    b = banks[5]
                    if t:
                        pe.wait_ge(y_taken, t)
                    for h in range(4):
                        for d in range(2):
                            mm(b[:, h * HD:(h + 1) * HD], Mt[:, 4 * d + h, :], xdt[:, d, h, :], start=d == 0, stop=d == 1,
                               signal=sty_ready if (h == 3 and d == 1) else None)
                rows(4, 0)
                pe.wait_ge(h_in, 1)
                for t in (1, 2):
                    for g in range(2):
                        b = bank(("yo", t, g))
                        r = slice(g * HD, (g + 1) * HD)
                        for d in range(2):
                            i = (0, 3) if t == 1 else (1, 2)
                            mm(b[:, d * P:(d + 1) * P], uT[r, 3, t * P:(t + 1) * P], hin[r, i[d], :],
                               signal=big if d else None)
                rows(4, 1)
                columns(3)
                lift(3)
                columns(4)

                pe.wait_ge(merged, 18)
                for k in range(KD):
                    b = bank(("mT", k))
                    for t in range(NT):
                        turn(b[:, t * P:(t + 1) * P], xn[:, t, k * P:(k + 1) * P], signal=big if t == NT - 1 else None)

                def gate_rows(out, i, g, h, signal):
                    mm(out, c_("selb")[:, g * P:(g + 1) * P], gaterow[:, i, h * HALF:(h + 1) * HALF], signal=signal)

                pe.wait_ge(bias_row1, 16 * (li + 1))
                for g in range(2):
                    for h in range(2):
                        gate_rows(bank(("gb", g, h))[:, :], 0, g, h, big)
                taken(("mT", KD - 2))
                taken(("mT", KD - 1))
                need(AT_OUT)
                need(AT_OUT + 1)
                for t in range(NT):
                    for h in range(2):
                        tokens(bank(("out", t, h))[:, :], t, AT_OUT, slice(h * HALF, (h + 1) * HALF), signal=big,
                               free=t == NT - 1 and h == 1)

                rows(5, 0)
                widths("h2T")
                taken(("h2T", KD - 2))
                taken(("h2T", KD - 1))
                b = bank(("lg",))
                for t in range(NT):
                    for k in range(KD):
                        mm(b[:, t * NE:(t + 1) * NE], hT[:, k, t * P:(t + 1) * P], wr[:, k, :], start=k == 0,
                           stop=k == KD - 1, signal=big if t == NT - 1 and k == KD - 1 else None)
                pe.wait_ge(aff_ready, 1)
                b = bank(("affT",))
                for t in range(NT):
                    turn(b[0:NE, t * P:(t + 1) * P], aff[:, t, :], signal=big if t == NT - 1 else None)
                rows(5, 1)
                pe.wait_ge(mask_ready, 1)
                b = bank(("mk",))
                for t in range(NT):
                    turn(b[:, t * NE:(t + 1) * NE], maskT[:, t * P:(t + 1) * P], signal=big if t == NT - 1 else None)
                taken(("mk",))
                b = bank(("rank",))
                mm(b[:, 0:NE], c_("upto"), msk[:, 0, :])
                mm(b[:, NE:2 * NE], c_("upto"), msk[:, 1, :])
                mm(b[:, 2 * NE:3 * NE], c_("upto"), msk[:, 2, :], stop=False)
                mm(b[:, 2 * NE:3 * NE], c_("ones"), msk[:, 1, :], start=False, signal=big)
                pe.wait_ge(bias_row2, 16 * (li + 1))
                for g in range(2):
                    for h in range(2):
                        gate_rows(bank(("gb2", g, h))[:, :], 1, g, h, big)
                pe.wait_ge(hot_ready, 1)
                for k in range(KD):
                    cols = slice(k * P, (k + 1) * P)
                    mm(bank(("xc", k))[:, 0:256], xn[:, 0, cols], Sc[:, :, :], signal=big)
                    b = bank(("xl", k))
                    mm(b[:, :], xn[:, 1, cols], Sl[:, 0, :, :], stop=False)
                    mm(b[:, :], xn[:, 2, cols], Sl[:, 1, :, :], start=False, signal=big)
                for n in range(len(BIG) - 4, len(BIG)):
                    taken(BIG[n][0])
                for i in range(6):
                    mm(banks[i][:, :], c_("zero"), cst[:, 0:512], stop=False, skip_group_check=True)

                with pe.Fori(0, NE // 2) as ep:
                    for u in range(2):
                        e = ep * 2 + u

                        def arrive(i):
                            i += 6 * u
                            pe.wait_ge(loaded[i % SLOTS], (base + (LOADS0 // SLOTS + i // SLOTS + 1) + ep * 3) * 16)

                        def up(out, i, last, free_last):
                            for k in range(KD):
                                s = (6 * u + i + k // 4) % SLOTS
                                if k % 4 == 0:
                                    arrive(i + k // 4)
                                for h in range(2):
                                    sig = None
                                    if h and k == 3:
                                        sig = freed[s]
                                    if h and k == KD - 1:
                                        sig = freed[s] if free_last else last
                                    mm(out[h * 64:(h + 1) * 64, :], xcur[:, k, :], ring[:, s, k % 4, h * HALF:(h + 1) * HALF],
                                       start=k == 0, stop=k == KD - 1, signal=sig)
                            if not free_last:
                                owed.append(freed[s])

                        pe.wait_ge(xc_ready, e + 1)
                        pe.wait_ge(sgs_ready, e)
                        up(banks[6], 0, None, True)
                        pe.wait_ge(yo_ready, e)
                        up(banks[7], 2, h3_ready, False)
                        pe.wait_ge(hid_ready, e + 1)
                        for b in range(4):
                            turn(banks[6][:, b * P:(b + 1) * P], hid[:, b, :], signal=ht_ready if b == 3 else None)
                        pe.wait_ge(hts_ready, e + 1)
                        for fh in range(2):
                            arrive(4 + fh)
                            s = (6 * u + 4 + fh) % SLOTS
                            for b in range(4):
                                for h in range(2):
                                    sig = None
                                    if b == 3 and h == 1:
                                        sig = yp_ready if fh else freed[s]
                                    mm(banks[7][h * 64:(h + 1) * 64, :], hidT[:, b, fh * 64:(fh + 1) * 64],
                                       ring[:, s, b, h * HALF:(h + 1) * HALF], start=fh == 0 and b == 0,
                                       stop=fh == 1 and b == 3, signal=sig)
                        owed.append(freed[s])
                        pe.wait_ge(w1hot, e + 1)
                        for t in range(NT):
                            turn(banks[6][:, t * P:(t + 1) * P], sgs[:, t, :], signal=sg_ready if t == NT - 1 else None)
                        pe.wait_ge(sgs_ready, e + 1)
                        pe.wait_ge(yo_ready, e + 1)
                        for t in range(NT):
                            for h in range(2):
                                r = slice(h * 64, (h + 1) * 64)
                                mm(banks[2 * t + h][:, :], sgT[r, t, :], yo[r, :], start=False, stop=False,
                                   skip_group_check=True)
                for i in range(6):
                    mm(banks[i][:, 0:32], c_("zero"), cst[:, 0:32], start=False, stop=True, skip_group_check=True,
                       signal=closed)
                assert not owed
                pe.drain().then_inc(done_pe, 1)
                pe.wait_ge(layer_go, li + 1)
                pe.sem_inc(dummy_pe, 1)

        @block.scalar
        def _(act):
            A = nc.scalar.activation
            nbig = [0]
            own = [0]

            def step(ins):
                ins.then_inc(act_step, 1)
                own[0] += 1

            def settle():
                act.wait_ge(act_step, own[0])

            def grab(name):
                assert BIG_BY[name] == "act"
                act.wait_ge(big, BIG_AT[name] + 1)
                return banks[BIG_AT[name] % 4]

            def gave(name, ins):
                nbig[0] += 1
                assert taken_by(name) == ("act", nbig[0]), name
                ins.then_inc(big_act, 1)

            def taken_dve(name):
                act.wait_ge(big_dve, taken_by(name)[1])

            roots = [0]

            def root(n):
                roots[0] += 1
                act.wait_ge(var_ready, roots[0])
                A(st[:, 1, 0:n], st[:, 0, 0:n], ACT.Sqrt).then_inc(root_ready, 1)

            def modulated(name, k, out_c, in_c, out_l, in_l, which):
                A(out_c, in_c, ACT.Identity, bias=modc[:, 2 * which, k, 0:1], scale=gs[:, which, k, 0:1])
                gave((name, k), A(out_l, in_l, ACT.Identity, bias=modc[:, 2 * which, k, 1:2], scale=gs[:, which, k, 1:2]))

            act.wait_ge(in_cond, 16)
            act.wait_ge(cond0, 1)
            A(csw[:, :, 0:2], cs[:, :, :], ACT.Silu).then_inc(cond, 1)
            act.wait_ge(in_x, 32)
            with act.Fori(0, DEPTH) as li:
                nbig[0] = own[0] = roots[0] = 0
                for t in range(NT):
                    A(xn[:, t, :], x[:, t, :], ACT.Square, accum_out=st[:, 4, t:t + 1]).then_inc(act_sq, 1)
                root(NT)

                def rows(v, h):
                    if v == 2 and h == 0:
                        act.wait_ge(kv_out, 96 * (li + 1))
                    b = grab(("row", v, h))
                    out = gaterow[:, v // 3, :] if v in (2, 5) else rsb[:, v % 2, :]
                    gave(("row", v, h), A(out[:, h * HALF:(h + 1) * HALF], b[:, :], ACT.Copy))

                for v in range(2):
                    for h in range(2):
                        rows(v, h)
                act.wait_ge(mod1, 1)

                def modulate(name, which):
                    for k in range(0, KD, 2):
                        b = grab((name, k))
                        modulated(name, k, hT[:, k, 0:P], b[:, 0:P], hT[:, k, P:T], b[:, P:T], which)

                modulate("hT", 0)
                for br in range(2):
                    for t in range(NT):
                        b = grab(("ab", t, br))
                        A(AB[:, t, br, 0:256].rearrange("p (g v d) -> p v g d", v=2, g=2),
                          b[:, 0:256].rearrange("p (v g d) -> p v g d", v=2, g=2), ACT.Copy)
                        A(AB[:, t, br, 256:384], b[:, 256:384], ACT.Copy)
                        gave(("ab", t, br), A(vab[:, t, br, :], b[:, 384:512], ACT.Copy))
                for t in range(NT):
                    act.wait_ge(big_act, taken_by(("ab", t, 1))[1])
                    if t >= 2:
                        act.wait_ge(sq_free, t - 1)
                    A(tmp[:, t % 2, :], AB[:, t, :, :].rearrange("p b n -> p (b n)"), ACT.Square).then_inc(act_sq, 1)
                for t in range(NT):
                    b = grab(("dqk", t))
                    gave(("dqk", t), A(DQ[:, t, :], b[:, :], ACT.Copy))
                    b = grab(("dv", t))
                    gave(("dv", t), A(vd[:, t, :], b[:, 0:256], ACT.Copy))
                root(36)
                for t in range(NT):
                    b = grab(("zdt", t))
                    A(sz[:, t, :], b[:, 0:256], ACT.Silu)
                    gave(("zdt", t), A(dtr[:, t, :], b[:, 256:264], ACT.Copy))
                act.wait_ge(pads, 1)
                for g in range(4):
                    b = grab(("xbc", g))
                    A(xbc[:, g, 2:2 + P], b[:, 0:P], ACT.Copy)
                    gave(("xbc", g), A(xbc[:, g, LAT0 + 2:LAT0 + 2 + 256], b[:, P:T], ACT.Copy))
                act.wait_ge(ab_ready, 1)
                for t in range(NT):
                    if t >= 2:
                        act.wait_ge(sq_free, NT + t - 1)
                    A(tmp[:, t % 2, 0:512], DQ[:, t, :], ACT.Square).then_inc(act_sq, 1)
                root(48)
                act.wait_ge(dt_abs, 1)
                step(A(dexp, dabs, ACT.Exp))
                settle()
                A(dexp, dexp, ACT.Ln, bias=1.0)
                A(expa, r_("alog"), ACT.Exp).then_inc(dt_log, 1)
                act.wait_ge(lam_dot, 1)
                A(lamx, lamd, ACT.Exp).then_inc(lam_exp, 1)

                def gate(i, s):
                    t, h = s // 2, s % 2
                    if s == 0 and i == 2:
                        taken_dve(("up", 0, NT - 1, 1))
                    elif s == 0 and i == 3:
                        act.wait_ge(merged, 6)
                    b = grab(("g", i, t, h))
                    gave(("g", i, t, h), A(G[i % 2][:, t, h * HALF:(h + 1) * HALF], b[:, :], ACT.Tanh, scale=0.5))

                for s in range(6):
                    gate(0, s)
                for g in range(4):
                    act.wait_ge(conv_sum, g + 1)
                    bias = cp[:, COLS["convb"][0] + g:COLS["convb"][0] + g + 1]
                    A(uT[:, g, 0:P], cacc[:, g, 0:P], ACT.Silu, bias=bias)
                    A(uT[:, g, P:T], cacc[:, g, LAT0:LAT0 + 256], ACT.Silu, bias=bias).then_inc(conv_out, 1)
                for t in range(NT):
                    for br in range(2):
                        b = grab(("qkT", t, br))
                        A(qT[:, br, :, t * P:(t + 1) * P], b[:, 0:256].rearrange("p (g t) -> p g t", g=2), ACT.Copy)
                        gave(("qkT", t, br), A(kT[:, br, t * P:(t + 1) * P], b[:, 256:384], ACT.Copy))
                b = grab(("ckT",))
                gave(("ckT",), A(kT[:, :, T:512], b[:, 0:256].rearrange("p (g t) -> p g t", g=2), ACT.Copy))
                for t in range(NT):
                    b = grab(("dT", t))
                    A(dqT[:, :, t * P:(t + 1) * P], b[:, 0:256].rearrange("p (g t) -> p g t", g=2), ACT.Copy)
                    gave(("dT", t), A(dkT[:, :, t * P:(t + 1) * P], b[:, 256:512].rearrange("p (g t) -> p g t", g=2), ACT.Copy))
                b = grab(("cdT",))
                gave(("cdT",), A(dkT[:, :, T:512], b[:, 0:256].rearrange("p (g t) -> p g t", g=2), ACT.Copy))

                for i in range(3):
                    its = iters(i)
                    for n in range(NIT + 1):
                        if n < NIT:
                            h, t = its[n]
                            nk = P if t == 0 else T
                            step_ = i * NIT + n
                            act.wait_ge(m_ready, step_ + 1)
                            q = 2 * (n % 4)
                            if i < 2:
                                ins = A(pr[:, n % 2, 0:nk], banks[4 + n % 2][:, 0:nk], ACT.Exp, bias=st[:, 1, q:q + 1],
                                        scale=HD ** -0.5, accum_out=st[:, 2, q:q + 1])
                                if i == 1:
                                    ins = A(st[:, 4, q:q + 1], r_("sink")[:, h:h + 1], ACT.Exp, bias=st[:, 1, q:q + 1])
                            else:
                                for m in range(2):
                                    ins = A(pr[:, n % 2, m * T:m * T + nk], banks[4 + m][:, 0:nk], ACT.Exp,
                                            bias=st[:, 1, q + m:q + m + 1], scale=32 ** -0.5,
                                            accum_out=st[:, 2, q + m:q + m + 1])
                            ins.then_inc(p_ready, 1)
                        if n >= 1:
                            h, t = its[n - 1]
                            nk = P if t == 0 else T
                            step_ = i * NIT + n - 1
                            act.wait_ge(pt_ready, step_ + 1)
                            if step_ >= 2:
                                act.wait_ge(pv_ready, step_ - 1)
                            A(pT[:, (n - 1) % 2, 0:nk], banks[6][:, 0:nk], ACT.Copy).then_inc(pts_ready, 1)
                        if n and n % 2 == 0:
                            gate(i + 1, n // 2 - 1)
                for h in range(2):
                    rows(2, h)
                for t in range(NT):
                    if t == 2:
                        root(12)
                    b = grab(("uT", t))
                    gave(("uT", t), A(xsB[:, t, :], b[:, 0:384], ACT.Copy))
                b = grab(("h0T",))
                A(hin[:, 0, :], b[:, 0:P], ACT.Copy)
                gave(("h0T",), A(hin[:, 2, :], b[:, P:2 * P], ACT.Copy))
                for h in range(2):
                    rows(3, h)
                act.wait_ge(ssd_small, 1)
                A(ex[:, :, :, :], sm[:, :, :, :], ACT.Exp).then_inc(ssd_exp, 1)
                for t in range(NT):
                    if t:
                        act.wait_ge(mt_ready, t)
                    for d in range(2):
                        b = grab(("dec", t, d))
                        for h in range(4):
                            ins = A(E[:, 4 * d + h, :], b[:, h * P:(h + 1) * P], ACT.Exp, bias=nacs[:, t, 4 * d + h:4 * d + h + 1])
                        gave(("dec", t, d), ins)
                    if t == 0:
                        act.wait_ge(sty_ready, 1)
                        A(sst[:, :, :], banks[4][:, 0:256].rearrange("p (i n) -> p i n", i=4), ACT.Copy)\
                            .then_inc(st0_taken, 1)
                for h in range(2):
                    rows(4, h)
                root(NT)
                for k in range(0, KD, 2):
                    b = grab(("mT", k))
                    gave(("mT", k), A(hT[:, k, :], b[:, 0:T], ACT.Copy, scale=0.5))
                for g in range(2):
                    for h in range(2):
                        b = grab(("gb", g, h))
                        gave(("gb", g, h), A(gbc[:, g, h * HALF:(h + 1) * HALF], b[:, :], ACT.Copy))
                for t in range(NT):
                    act.wait_ge(x_ready, t + 1)
                    A(xn[:, t, :], x[:, t, :], ACT.Square, accum_out=st[:, 4, t:t + 1]).then_inc(act_sq, 1)
                root(NT)
                rows(5, 0)
                act.wait_ge(mod1, 2)
                modulate("h2T", 1)
                act.wait_ge(ssm_out, (li + 1) * 64)
                act.wait_ge(aff_in, 1)
                A(aff[:, :, :], aff[:, :, :], ACT.Exp).then_inc(aff_exp, 1)
                b = grab(("affT",))
                gave(("affT",), A(affT, b[0:NE, 0:T], ACT.Copy))
                rows(5, 1)
                b = grab(("mk",))
                gave(("mk",), A(msk[:, :, :], b[:, 0:48].rearrange("p (t e) -> p t e", t=NT), ACT.Copy))
                for g in range(2):
                    for h in range(2):
                        b = grab(("gb2", g, h))
                        gave(("gb2", g, h), A(gbc[:, g, h * HALF:(h + 1) * HALF], b[:, :], ACT.Copy))
                XTe = XT[:, :, 0:NE * CE].rearrange("p k (e c) -> p k e c", c=CE)
                for k in range(0, KD, 2):
                    b = grab(("xc", k))
                    gave(("xc", k), A(XTe[:, k, :, 0:CAP[0]], b[:, 0:256].rearrange("p (e c) -> p e c", e=NE), ACT.Identity,
                                      bias=modc[:, 2, k, 0:1], scale=gs[:, 1, k, 0:1]))
                    b = grab(("xl", k))
                    gave(("xl", k), A(XTe[:, k, :, CAP[0]:CE], b[:, :].rearrange("p (e c) -> p e c", e=NE), ACT.Identity,
                                      bias=modc[:, 2, k, 1:2], scale=gs[:, 1, k, 1:2]))
                with act.Fori(0, NE) as e:
                    act.wait_ge(h3_ready, e + 1)
                    A(hs, banks[6][:, :], ACT.Silu).then_inc(silu_ready, 1)
                    act.wait_ge(ht_ready, e + 1)
                    A(hidT[:, :, :], banks[6][:, :].rearrange("p (b n) -> p b n", b=4), ACT.Copy).then_inc(hts_ready, 1)
                    act.wait_ge(yp_ready, e + 1)
                    A(yo, banks[7][:, :], ACT.Copy).then_inc(yo_ready, 1)
                act.drain().then_inc(done_act, 1)
                act.wait_ge(layer_go, li + 1)
                act.sem_inc(dummy_act, 1)

        @block.vector
        def _(dve):
            V = nc.vector
            nbig = [0]
            own = [0]
            norms = [0]
            sqs = [0]

            def step(ins):
                ins.then_inc(dve_step, 1)
                own[0] += 1

            def settle():
                dve.wait_ge(dve_step, own[0])

            def link(ins):
                step(ins)
                settle()

            def grab(name):
                assert BIG_BY[name] == "dve"
                dve.wait_ge(big, BIG_AT[name] + 1)
                return banks[BIG_AT[name] % 4]

            def gave(name, ins):
                nbig[0] += 1
                assert taken_by(name) == ("dve", nbig[0]), name
                ins.then_inc(big_dve, 1)

            def rsqrt(ssq, n, width):
                var, root, y, c = (st[:, i, 0:n] for i in range(4))
                V.tensor_scalar(var, ssq, 1.0 / width, EPS, ALU.mult, ALU.add).then_inc(var_ready, 1)
                norms[0] += 1
                dve.wait_ge(root_ready, norms[0])
                dve.wait_ge(var_ready, norms[0])
                link(V.reciprocal(y, root))
                link(V.tensor_tensor(c, var, y, ALU.mult))
                link(V.tensor_tensor(c, c, y, ALU.mult))
                link(V.tensor_scalar(c, c, -0.5, 1.5, ALU.mult, ALU.add))
                link(V.tensor_tensor(y, y, c, ALU.mult))
                return y

            def norm_rows():
                sqs[0] += NT
                dve.wait_ge(act_sq, sqs[0])
                y = rsqrt(st[:, 4, 0:NT], NT, D)
                for t in range(NT):
                    V.tensor_scalar(xn[:, t, :], x[:, t, :], y[:, t:t + 1], None, ALU.mult).then_inc(xn_ready, 1)

            def modulate(name, which):
                for k in range(1, KD, 2):
                    b = grab((name, k))
                    V.tensor_scalar(hT[:, k, 0:P], b[:, 0:P], gs[:, which, k, 0:1], modc[:, 2 * which, k, 0:1],
                                    ALU.mult, ALU.add)
                    gave((name, k), V.tensor_scalar(hT[:, k, P:T], b[:, P:T], gs[:, which, k, 1:2],
                                                    modc[:, 2 * which, k, 1:2], ALU.mult, ALU.add))

            def head_norm(buf, heads, width, per_tile, gq_mul, ready, rotary):
                n = NT * heads
                for t in range(NT):
                    sqs[0] += 1
                    dve.wait_ge(act_sq, sqs[0])
                    V.tensor_reduce(st[:, 5, t * heads:(t + 1) * heads] if n <= 36 else stw[:, t * heads:(t + 1) * heads],
                                    tmp[:, t % 2, 0:heads * width].rearrange("p (h n) -> p h n", h=heads), AX.X, ALU.add)\
                        .then_inc(sq_free, 1)
                    per_tile[0] += 1
                dve.wait_ge(sq_free, per_tile[0])
                y = rsqrt(st[:, 5, 0:n] if n <= 36 else stw[:, 0:n], n, width)
                for t in range(NT):
                    step(V.tensor_tensor(buf(t), buf(t), rep(y[:, t * heads:(t + 1) * heads], 2, width), ALU.mult))
                settle()
                for t in range(NT):
                    for ins in gq_mul(t):
                        step(ins)
                settle()
                for t in (1, 2):
                    rotary(t)
                return None

            taken_sq = [0]
            dve.wait_ge(in_x, 32)
            dve.wait_ge(in_cst, 16)
            with dve.Fori(0, DEPTH) as li:
                nbig[0] = own[0] = norms[0] = sqs[0] = taken_sq[0] = 0
                norm_rows()
                dve.wait_ge(params, (li + 1) * 64)

                def columns(v):
                    n = (0, 1, None, 2, 3)[v]
                    b = grab(("col", v))
                    bias = cp[:, COLS["bada"][0] + 8 * n:COLS["bada"][0] + 8 * n + 8]
                    gave(("col", v), V.tensor_tensor(modc[:, n, :, :], b[:, 0:16].rearrange("p (k g) -> p k g", g=2),
                                                     rep(bias, 2, 2), ALU.add))
                    if v in (1, 4):
                        i = v // 3
                        dve.wait_ge(big_dve, nbig[0])
                        V.scalar_tensor_tensor(gs[:, i, :, :], modc[:, 2 * i + 1, :, :], 1.0,
                                               rep(cp[:, 8 * i:8 * i + 8], 2, 2), ALU.add, ALU.mult).then_inc(mod1, 1)
                        dve.wait_ge(mod1, i + 1)

                for v in range(2):
                    columns(v)
                link(V.tensor_tensor(lamt, r_("lamq"), r_("lamk"), ALU.mult))
                step(V.tensor_scalar(nsink, r_("sink"), -1.0, None, ALU.mult))
                V.tensor_reduce(lamd, lamt.rearrange("p (i n) -> p i n", i=2), AX.X, ALU.add).then_inc(lam_dot, 1)
                modulate("hT", 0)

                def ab_gain(t):
                    q = AB[:, t, :, 0:256].rearrange("p b (h d) -> p b h d", h=4)
                    k = AB[:, t, :, 256:384].rearrange("p b (h d) -> p b h d", h=2)
                    return [V.tensor_tensor(q, q, rep(gqc, 2, 4), ALU.mult), V.tensor_tensor(k, k, rep(gkc, 2, 2), ALU.mult)]

                def turner(buf, heads, width, cosn, sinn, last, sem_):
                    def rotary(t):
                        n = width // 4
                        v = buf(t)
                        cs_ = c_(cosn)[:, (t - 1) * width:t * width]
                        sn_ = c_(sinn)[:, (t - 1) * width:t * width].rearrange("p (a h n) -> p a h n", a=2, h=2)
                        v5 = v.rearrange("p h (a c n) -> p h a c n", a=2, c=2)
                        o5 = tmp[:, 1, 0:heads * width].rearrange("p (h a c n) -> p h a c n", h=heads, a=2, c=2)
                        for c in range(2):
                            step(V.tensor_tensor(o5[:, :, :, c, :], v5[:, :, :, 1 - c, :], rep(sn_[:, :, c, :], 1, heads), ALU.mult))
                        settle()
                        link(V.tensor_tensor(v, v, rep(cs_, 1, heads), ALU.mult))
                        ins = V.tensor_tensor(v, v, tmp[:, 1, 0:heads * width].rearrange("p (h n) -> p h n", h=heads), ALU.add)
                        if t == last:
                            ins.then_inc(sem_, 1)
                            dve.wait_ge(sem_, 1)
                        else:
                            link(ins)
                    return rotary

                abuf = lambda t: AB[:, t, :, :].rearrange("p b (h d) -> p (b h) d", d=HD)
                head_norm(abuf, 12, HD, taken_sq, ab_gain, ab_ready, turner(abuf, 12, HD, "cos", "sin", 2, ab_ready))

                dve.wait_ge(big_act, taken_by(("zdt", 2))[1])
                link(V.tensor_tensor(dtr, dtr, rep(r_("dtb"), 1, NT), ALU.add))
                V.scalar_tensor_tensor(dabs, dtr, -1.0, dtr, ALU.mult, ALU.min).then_inc(dt_abs, 1)

                def d_gain(t):
                    q = DQ[:, t, 0:256].rearrange("p (h d) -> p h d", h=8)
                    k = DQ[:, t, 256:512].rearrange("p (h d) -> p h d", h=8)
                    return [V.tensor_tensor(q, q, rep(r_("gqd"), 1, 8), ALU.mult), V.tensor_tensor(k, k, rep(r_("gkd"), 1, 8), ALU.mult)]

                dbuf = lambda t: DQ[:, t, :].rearrange("p (h d) -> p h d", h=16)
                head_norm(dbuf, 16, 32, taken_sq, d_gain, d_ready, turner(dbuf, 16, 32, "cosd", "sind", 2, d_ready))

                dve.wait_ge(dt_log, 1)
                link(V.scalar_tensor_tensor(dt_, dtr, 0.0, dexp, ALU.max, ALU.add))
                V.scalar_tensor_tensor(la, dt_, -1.0, rep(expa, 1, NT), ALU.mult, ALU.mult).then_inc(dt_done, 1)
                dve.wait_ge(lam_exp, 1)
                link(V.tensor_tensor(nlam, lamx[:, 1:2], lamx[:, 0:1], ALU.subtract))
                link(V.tensor_tensor(nlam, nlam, r_("laminit"), ALU.subtract))

                dve.wait_ge(big_act, taken_by(("xbc", 3))[1])
                cw = cp[:, COLS["convw"][0]:COLS["convw"][1]].rearrange("p (g k) -> p g k", g=4)
                for k in range(5):
                    for g in range(4):
                        if k == 0:
                            step(V.tensor_scalar(cacc[:, g, :], xbc[:, g, 0:NU_CONV], cw[:, g, 0:1], None, ALU.mult))
                        else:
                            ins = V.scalar_tensor_tensor(cacc[:, g, :], xbc[:, g, k:k + NU_CONV], cw[:, g, k:k + 1],
                                                         cacc[:, g, :], ALU.mult, ALU.add)
                            if k == 4:
                                ins.then_inc(conv_sum, 1)
                            else:
                                step(ins)
                    if k < 4:
                        settle()

                def lift(i):
                    for c in range(2):
                        b = grab(("boT", i, c))
                        gave(("boT", i, c), V.tensor_copy(boT[:, c, :], b[:, 0:T]))
                    for t in range(NT):
                        for h in range(2):
                            b = grab(("up", i, t, h))
                            g = G[i % 2][:, t, h * HALF:(h + 1) * HALF]
                            m = xn[:, t, h * HALF:(h + 1) * HALF]
                            if i == 0:
                                dve.wait_ge(big_act, taken_by(("g", 0, t, h))[1])
                                gave(("up", i, t, h), V.scalar_tensor_tensor(m, g, 1.0, b[:, :], ALU.add, ALU.mult))
                            else:
                                dve.wait_ge(big_act, taken_by(("g", i, t, h))[1])
                                gave(("up", i, t, h), V.scalar_tensor_tensor(g, g, 1.0, b[:, :], ALU.add, ALU.mult))
                                dve.wait_ge(big_dve, nbig[0])
                                V.tensor_tensor(m, m, g, ALU.add).then_inc(merged, 1)

                def maximum(i, n):
                    h, t = iters(i)[n]
                    nk = P if t == 0 else T
                    q = 2 * (n % 4)
                    dve.wait_ge(s_ready, i * NIT + n + 1)
                    mx, nb = st[:, 0, q:q + 2], st[:, 1, q:q + 2]
                    if i < 2:
                        link(V.tensor_reduce(mx[:, 0:1], banks[4 + n % 2][:, 0:nk], AX.X, ALU.max))
                    else:
                        for m in range(2):
                            step(V.tensor_reduce(mx[:, m:m + 1], banks[4 + m][:, 0:nk], AX.X, ALU.max))
                        settle()
                    if i == 0:
                        ins = V.tensor_scalar(nb[:, 0:1], mx[:, 0:1], -(HD ** -0.5), None, ALU.mult)
                    elif i == 1:
                        ins = V.tensor_scalar(nb[:, 0:1], mx[:, 0:1], -(HD ** -0.5), nsink[:, h:h + 1], ALU.mult, ALU.min)
                    else:
                        ins = V.tensor_scalar(nb, mx, -(32 ** -0.5), None, ALU.mult)
                    ins.then_inc(m_ready, 1)

                maximum(0, 0)
                for i in range(3):
                    its = iters(i)
                    for n in range(NIT + 2):
                        if 1 <= n < NIT and i < 2:
                            maximum(i, n)
                        if 1 <= n <= NIT:
                            h, t = its[n - 1]
                            nk = P if t == 0 else T
                            q = 2 * ((n - 1) % 4)
                            dve.wait_ge(p_ready, i * NIT + n)
                            sums, rs = st[:, 2, q:q + 2], st[:, 3, q:q + 2]
                            if i == 1:
                                link(V.tensor_tensor(sums[:, 0:1], sums[:, 0:1], st[:, 4, q:q + 1], ALU.add))
                            if i < 2:
                                step(V.reciprocal(rs[:, 0:1], sums[:, 0:1]))
                            else:
                                link(V.reciprocal(rs, sums))
                                link(V.tensor_tensor(rs[:, 1:2], rs[:, 1:2], nlam, ALU.mult))
                                p0, p1 = pr[:, (n - 1) % 2, 0:nk], pr[:, (n - 1) % 2, T:T + nk]
                                link(V.tensor_scalar(p1, p1, rs[:, 1:2], None, ALU.mult))
                                V.scalar_tensor_tensor(p0, p0, rs[:, 0:1], p1, ALU.mult, ALU.add).then_inc(w_ready, 1)
                        if 1 <= n < NIT and i == 2:
                            maximum(i, n)
                        if n >= 2:
                            h, t = its[n - 2]
                            q = 2 * ((n - 2) % 4)
                            settle()
                            dve.wait_ge(pv_ready, i * NIT + n - 1)
                            if i == 0 and n == 2:
                                dve.wait_ge(kv_out, (li + 1) * 96)
                            out = bo[:, t, h * HD:(h + 1) * HD]
                            if i < 2:
                                V.tensor_scalar(out, banks[7][:, 0:HD], st[:, 3, q:q + 1], None, ALU.mult).then_inc(o_ready, 1)
                            else:
                                V.tensor_copy(out, banks[7][:, 0:HD]).then_inc(o_ready, 1)
                    if i == 2:
                        dve.wait_ge(o_ready, 3 * NIT)
                        sq = at(po, NT * 256).rearrange("p (t n) -> p t n", t=NT)
                        link(V.tensor_tensor(sq, bo[:, :, :], bo[:, :, :], ALU.mult))
                        link(V.tensor_reduce(st[:, 5, 0:12], sq.rearrange("p t (h n) -> p (t h) n", n=HD), AX.X, ALU.add))
                        y = rsqrt(st[:, 5, 0:12], 12, HD)
                        link(V.tensor_scalar(y, y, r_("onemlam"), None, ALU.mult))
                        b4 = bo[:, :, :].rearrange("p t (h n) -> p (t h) n", n=HD)
                        link(V.tensor_tensor(b4, b4, rep(y, 2, HD), ALU.mult))
                        V.tensor_tensor(b4, b4, rep(r_("gdout"), 1, 12), ALU.mult).then_inc(bo_ready, 1)
                    else:
                        maximum(i + 1, 0)
                        lift(i)

                b = grab(("cum",))
                cum = b[:, 0:48].rearrange("p (t i j) -> p i t j", t=NT, i=2)
                step(V.tensor_copy(sm[:, 0, :, :], cum[:, 0, :, :]))
                step(V.tensor_copy(sm[:, 2, :, :], cum[:, 1, :, :]))
                gave(("cum",), V.tensor_scalar(nacs, cum[:, 0, :, :], -1.0, None, ALU.mult))
                settle()
                V.tensor_tensor(sm[:, 1, :, :], sm[:, 2, :, :], sm[:, 0, :, :], ALU.subtract).then_inc(ssd_small, 1)
                dve.wait_ge(big_dve, nbig[0])
                lift(2)
                dve.wait_ge(ssd_exp, 1)
                ea, te, dcy = ex[:, 0, :, :], ex[:, 1, :, :], ex[:, 2, :, :]
                for t in range(NT):
                    xs = xsB[:, t, 0:256].rearrange("p (h n) -> p h n", h=4)
                    dve.wait_ge(big_act, taken_by(("uT", 2))[1])
                    for d in range(2):
                        step(V.tensor_tensor(xdt[:, d, :, :], xs, rep(dt_[:, t, 4 * d:4 * d + 4], 2, HD), ALU.mult))
                    settle()
                    step(V.tensor_tensor(xde.rearrange("p d h n -> p (d h) n"), xdt.rearrange("p d h n -> p (d h) n"),
                                         rep(te[:, t, :], 2, HD), ALU.mult))
                    step(V.tensor_tensor(bo[:, t, :].rearrange("p (h n) -> p h n", h=4), xs, rep(r_("dskip"), 2, HD), ALU.mult))
                    dve.wait_ge(big_act, taken_by(("dec", t, 1))[1])
                    E4 = E.rearrange("p (d h) l -> p d h l", d=2)
                    M4 = Mt.rearrange("p (d h) l -> p d h l", d=2)
                    for g in range(2):
                        b = grab(("GT", t, g))
                        for d in range(2):
                            ins = V.tensor_tensor(M4[:, d, 2 * g:2 * g + 2, :], E4[:, d, 2 * g:2 * g + 2, :],
                                                  rep(b[:, 0:P], 1, 2), ALU.mult)
                            if d:
                                gave(("GT", t, g), ins)
                            else:
                                step(ins)
                    settle()
                    dve.wait_ge(big_dve, nbig[0])
                    V.tensor_copy(xmark, dt_[:, 0, 0:1]).then_inc(mt_ready, 1)
                    if t:
                        dve.wait_ge(sty_ready, 2 * t + 1)
                        d, src, dst = t - 1, 2 * (t - 1), 2 * (t - 1) + 1
                        for g in range(2):
                            r = slice(g * HD, (g + 1) * HD)
                            hh = hin[r, dst, :].rearrange("p (h n) -> p h n", h=2)
                            step(V.tensor_tensor(hh, hin[r, src, :].rearrange("p (h n) -> p h n", h=2),
                                                 rep(dcy[r, t, 4 * d + 2 * g:4 * d + 2 * g + 2], 2, HD), ALU.mult))
                        settle()
                        step(V.tensor_tensor(hin[:, dst, :], hin[:, dst, :], banks[4][:, 0:P], ALU.add))
                        settle()
                    dve.wait_ge(sty_ready, 2 * t + 2)
                    V.tensor_tensor(bo[:, t, :], bo[:, t, :], banks[5][:, 0:256], ALU.add).then_inc(y_taken, 1)
                    dve.wait_ge(y_taken, t + 1)
                V.tensor_copy(xmark, dt_[:, 0, 0:1]).then_inc(h_in, 1)
                for t in (1, 2):
                    for g in range(2):
                        b = grab(("yo", t, g))
                        yt = at(po, 256).rearrange("p (d h n) -> p d h n", d=2, h=2)
                        for d in range(2):
                            ins = V.tensor_tensor(yt[:, d, :, :], b[:, d * P:(d + 1) * P].rearrange("p (h n) -> p h n", h=2),
                                                  rep(ea[:, t, 4 * d + 2 * g:4 * d + 2 * g + 2], 2, HD), ALU.mult)
                            if d:
                                gave(("yo", t, g), ins)
                            else:
                                step(ins)
                        settle()
                        dve.wait_ge(big_dve, nbig[0])
                        o = bo[:, t, g * P:(g + 1) * P].rearrange("p (h n) -> p h n", h=2)
                        for d in range(2):
                            link(V.tensor_tensor(o, o, yt[:, d, :, :], ALU.add))
                link(V.tensor_tensor(bo[:, :, :], bo[:, :, :], sz[:, :, :], ALU.mult))
                sq = at(po, NT * 256).rearrange("p (t n) -> p t n", t=NT)
                link(V.tensor_tensor(sq, bo[:, :, :], bo[:, :, :], ALU.mult))
                link(V.tensor_reduce(st[:, 5, 0:NT], sq, AX.X, ALU.add))
                y = rsqrt(st[:, 5, 0:NT], NT, 256)
                for t in range(NT):
                    ins = V.scalar_tensor_tensor(bo[:, t, :], bo[:, t, :], y[:, t:t + 1], r_("gssm"), ALU.mult, ALU.mult)
                    if t == NT - 1:
                        ins.then_inc(bo_ready, 1)
                    else:
                        step(ins)
                settle()
                columns(3)
                lift(3)
                columns(4)

                for k in range(1, KD, 2):
                    b = grab(("mT", k))
                    gave(("mT", k), V.tensor_scalar(hT[:, k, :], b[:, 0:T], 0.5, None, ALU.mult))
                dve.wait_ge(big_act, taken_by(("gb", 1, 1))[1])
                for t in range(NT):
                    for h in range(2):
                        b = grab(("out", t, h))
                        cols = slice(h * HALF, (h + 1) * HALF)
                        gave(("out", t, h), V.tensor_tensor(gtmp[:, h, :], b[:, :], gbc[:, min(t, 1), cols], ALU.mult))
                        dve.wait_ge(big_dve, nbig[0])
                        ins = V.tensor_tensor(x[:, t, cols], x[:, t, cols], gtmp[:, h, :], ALU.add)
                        if h:
                            ins.then_inc(x_ready, 1)
                        else:
                            step(ins)
                    settle()
                norm_rows()
                modulate("h2T", 1)
                dve.wait_ge(ssm_out, (li + 1) * 64)
                b = grab(("lg",))
                lg = b[:, 0:48].rearrange("p (t e) -> p t e", t=NT)
                link(V.tensor_reduce(st[:, 0, 0:NT], lg, AX.X, ALU.max))
                gave(("lg",), V.tensor_tensor(aff[:, :, :], lg, rep(st[:, 0, 0:NT], 2, NE), ALU.subtract))
                dve.wait_ge(big_dve, nbig[0])
                V.tensor_copy(xmark, dt_[:, 0, 0:1]).then_inc(aff_in, 1)
                dve.wait_ge(aff_exp, 1)
                link(V.tensor_reduce(st[:, 1, 0:NT], aff[:, :, :], AX.X, ALU.add))
                link(V.reciprocal(st[:, 2, 0:NT], st[:, 1, 0:NT]))
                V.tensor_tensor(aff[:, :, :], aff[:, :, :], rep(st[:, 2, 0:NT], 2, NE), ALU.mult).then_inc(aff_ready, 1)
                dve.wait_ge(big_act, taken_by(("affT",))[1])
                for c0, c1, rounds in ((0, P, CAP[0] // 8), (P, T, CAP[1] // 8)):
                    src = affT[:, c0:c1]
                    for _ in range(rounds):
                        link(V.max(top8, src))
                        link(V.match_replace(wrk[:, c0:c1], top8, src, -1.0))
                        src = wrk[:, c0:c1]
                V.tensor_scalar(maskT, wrk, 0.0, None, ALU.is_lt).then_inc(mask_ready, 1)
                b = grab(("rank",))
                rk = b[:, 0:48].rearrange("p (t e) -> p t e", t=NT)
                step(V.tensor_tensor(pos[:, 0, :], rk[:, 0, :], msk[:, 0, :], ALU.mult))
                gave(("rank",), V.scalar_tensor_tensor(pos[:, 1:3, :], rk[:, 1:3, :], float(CAP[0]), msk[:, 1:3, :],
                                                       ALU.add, ALU.mult))
                settle()
                dve.wait_ge(big_dve, nbig[0])
                link(V.tensor_scalar(pos[:, :, :], pos[:, :, :], -1.0, None, ALU.add))
                iota = c_("iota")
                step(V.tensor_tensor(Sc[:, :, :], rep(iota[:, 0:CAP[0]], 1, NE), rep(pos[:, 0, :], 2, CAP[0]), ALU.is_equal))
                step(V.tensor_tensor(Sl[:, 0, :, :], rep(iota[:, CAP[0]:CE], 1, NE), rep(pos[:, 1, :], 2, CAP[1]), ALU.is_equal))
                step(V.tensor_tensor(Sl[:, 1, :, :], rep(iota[:, CAP[0]:CE], 1, NE), rep(pos[:, 2, :], 2, CAP[1]), ALU.is_equal))
                settle()
                V.memset(XT[:, :, NE * CE:784], 0.0).then_inc(hot_ready, 1)
                XTe = XT[:, :, 0:NE * CE].rearrange("p k (e c) -> p k e c", c=CE)
                for k in range(1, KD, 2):
                    b = grab(("xc", k))
                    gave(("xc", k), V.tensor_scalar(XTe[:, k, :, 0:CAP[0]], b[:, 0:256].rearrange("p (e c) -> p e c", e=NE),
                                                    gs[:, 1, k, 0:1], modc[:, 2, k, 0:1], ALU.mult, ALU.add))
                    b = grab(("xl", k))
                    gave(("xl", k), V.tensor_scalar(XTe[:, k, :, CAP[0]:CE], b[:, :].rearrange("p (e c) -> p e c", e=NE),
                                                    gs[:, 1, k, 1:2], modc[:, 2, k, 1:2], ALU.mult, ALU.add))
                dve.wait_ge(big_dve, nbig[0])
                dve.wait_ge(big_act, taken_by(("xl", KD - 2))[1])
                dve.wait_ge(hot_ready, 1)

                with dve.Fori(0, NE) as e:
                    dve.wait_ge(h3_ready, e)
                    V.tensor_copy(xcur[:, :, :], XT[:, :, bass.ds(e * CE, 64)]).then_inc(xc_ready, 1)
                    dve.wait_ge(sg_ready, e)
                    for t in range(NT):
                        ins = V.tensor_scalar(sgs[:, t, :], iota, pos[:, t, bass.ds(e, 1)], aff[:, t, bass.ds(e, 1)],
                                              ALU.is_equal, ALU.mult)
                    ins.then_inc(w1hot, 1)
                    dve.wait_ge(silu_ready, e + 1)
                    V.tensor_tensor(hid.rearrange("p b n -> p (b n)"), hs, banks[7][:, :], ALU.mult).then_inc(hid_ready, 1)
                    dve.wait_ge(sg_ready, e + 1)
                    V.tensor_copy(sgT.rearrange("p t c -> p (t c)"), banks[6][:, 0:T]).then_inc(sgs_ready, 1)
                for t in range(NT):
                    for h in range(2):
                        dve.wait_ge(closed, 2 * t + h + 1)
                        cols = slice(h * HALF, (h + 1) * HALF)
                        link(V.tensor_tensor(gtmp[:, h, :], banks[2 * t + h][:, :], gbc[:, min(t, 1), cols], ALU.mult))
                        step(V.tensor_tensor(x[:, t, cols], x[:, t, cols], gtmp[:, h, :], ALU.add))
                    settle()
                dve.drain().then_inc(done_dve, 1)
                dve.wait_ge(layer_go, li + 1)
                dve.sem_inc(dummy_dve, 1)
            dve.drain().then_inc(x_final, 1)


_OUTS = [((1, 128, 1024), "float32"), ((1, 256, 1024), "float32"),
         ((1, 2, 128, 2, 64), "float32"), ((1, 2, 128, 2, 64), "float32"),
         ((1, 2, 128, 2, 64), "float32"), ((1, 2, 128, 2, 64), "float32"),
         ((1, 2, 2, 4, 64, 64), "float32"),
         ((1, 2, 128, 4, 2, 32), "float32"), ((1, 2, 128, 4, 64), "float32")]


def constants():
    import numpy as np
    c = np.zeros((P, NCST), np.float32)

    def put(name, a):
        c[:, CST[name][0]:CST[name][1]] = a

    i = np.arange(P)
    put("ident", np.eye(P))
    put("upto", i[:, None] <= i[None, :])
    put("from", i[:, None] >= i[None, :])
    put("negbelow", np.where(i[None, :] < i[:, None], -1e30, 0.0))
    put("negabove", np.where(i[None, :] > i[:, None], -1e30, 0.0))
    put("ones", 1.0)
    put("sel", (i[:, None] % 32) == np.arange(2)[None, :])
    put("selb", np.repeat(((i[:, None] % 32) == np.arange(2)[None, :]) | (i[:, None] == 2), P, axis=1))
    put("iota", np.tile(np.arange(64), 2)[None, :])
    for width, cn, sn in ((64, "cos", "sin"), (32, "cosd", "sind")):
        n = width // 4
        inv = np.float32(10000.0) ** (-np.arange(n, dtype=np.float32) / np.float32(n))
        inv = inv.astype(np.float32)
        tok = np.arange(256)
        ang = np.stack([(tok // 64)[:, None].astype(np.float32) * inv, (tok % 64)[:, None].astype(np.float32) * inv], 1)
        cos, sin = np.cos(ang), np.sin(ang)
        full_c = np.stack([cos, cos], 2).reshape(2, P, width)
        full_s = np.stack([-sin, sin], 2).reshape(2, P, width)
        put(cn, full_c.transpose(1, 0, 2).reshape(P, 2 * width))
        put(sn, full_s.transpose(1, 0, 2).reshape(P, 2 * width))
    return c


def kernel(**inputs):
    import math

    import numpy as _np
    import concourse.bacc as _bacc
    from concourse.bass_utils import run_bass_kernel_spmd as _run

    n = {k: _np.asarray(v) for k, v in inputs.items()}
    f32 = _np.float32
    init = [0.8 - 0.6 * math.exp(-0.3 * i) for i in range(DEPTH)]
    rows = [n["g_qa"], n["g_qb"], n["g_ka"], n["g_kb"], n["g_qd"], n["g_kd"], n["g_dout"], n["lam_q1"], n["lam_q2"],
            n["lam_k1"], n["lam_k2"], n["sink_b"], n["a_log"].reshape(DEPTH, 8), n["dt_bias"].reshape(DEPTH, 8),
            n["d_skip"], n["g_ssm"], _np.array(init, f32)[:, None], (1 - _np.array(init))[:, None].astype(f32)]
    cols = [n["g_norm1"].reshape(DEPTH, KD, P).transpose(0, 2, 1), n["g_norm2"].reshape(DEPTH, KD, P).transpose(0, 2, 1),
            n["conv_w"].reshape(DEPTH, 5, 4, P).transpose(0, 3, 2, 1).reshape(DEPTH, P, 20),
            n["conv_b"].reshape(DEPTH, 4, P).transpose(0, 2, 1),
            n["b_ada"].reshape(DEPTH, 6, KD, P)[:, [0, 1, 3, 4]].reshape(DEPTH, 4 * KD, P).transpose(0, 2, 1)]
    ssm = n["state_ssm"][0].reshape(DEPTH, 2, 2, 2, 64, 64).transpose(0, 3, 4, 1, 2, 5).reshape(DEPTH, P, 256)
    cache = [n["cache_" + k][0].reshape(DEPTH, P, -1) for k in ("a_k", "b_k", "a_v", "b_v", "d_k", "d_v")] + [ssm]
    cvec = _np.stack([n["c_ctx"], n["c"][0]], axis=-1).reshape(KD, P, 2).transpose(1, 0, 2)
    arrays = {
        "x_prompt": n["x_prompt"], "x_sample": n["x_sample"], "cvecT": cvec, "rowp": _np.concatenate(rows, axis=1),
        "colp": _np.concatenate(cols, axis=2), "caches": _np.concatenate(cache, axis=2), "b_ada": n["b_ada"],
        "w_ada": n["w_ada"], "w_in": n["w_in"], "w_br": n["w_br"], "w_out": n["w_out"], "w_router": n["w_router"],
        "w_e1": n["w_e1"], "w_e3": n["w_e3"], "w_e2": n["w_e2"], "consts": constants(),
    }
    nc = _bacc.Bacc("TRN2", target_bir_lowering=False, num_devices=1)
    sent, args = {}, []
    for name, a in arrays.items():
        sent[f"in_{name}"] = _np.ascontiguousarray(a)
        args.append(nc.dram_tensor(f"in_{name}", a.shape, mybir.dt.from_np(a.dtype), kind="ExternalInput").ap())
    for i, (shape, dtype) in enumerate(_OUTS):
        args.append(nc.dram_tensor(f"out_{i}", shape, mybir.dt.from_np(_np.dtype(dtype)), kind="ExternalOutput").ap())
    trunk_kernel(nc, *args)
    r = _run(nc, [sent], core_ids=[0])
    return tuple(r.results[0][f"out_{i}"] for i in range(len(_OUTS)))
```

```python
from contextlib import ExitStack

import concourse.bass as bass
from concourse import mybir

P = 128
D = 1024
KD = D // P
NT = 3
T = NT * P
DEPTH = 2
HD = 64
NE = 16
CAP = (16, 32)
CE = CAP[0] + CAP[1]
STAGES = ((0, 4), (4, 10), (10, 16))
EPS = 1e-6
HALF = 512
SLOTS = 4
AT_ADA = (0, 2, 20, 22, 25, 30)
AT_AB, AT_D, AT_C, AT_OUT = 4, 6, 8, 28
AT_GATE = (10, 12, 15, 18)
AT_LIFT = (14, 17, 24, 27)
LOADS0 = 32
SLOTS_E = 6
PER = [LOADS0 // SLOTS + NE - 1] * 2 + [LOADS0 // SLOTS + NE] * 2 + [NE] * 2 + [1] * 2
XTN = 6 * CE + 16
BRANCH = (0, 1, 3, 2)
COL_A, COL_C, COL_D, COL_G = 0, 1024, 1792, 2568
NC_ = 768
ND_ = 776
NDT = 8
PADW = 392
NU_CONV = PADW - 4
LAT0 = 132

F32 = mybir.dt.float32
ACT = mybir.ActivationFunctionType
ALU = mybir.AluOpType
AX = mybir.AxisListType

ROW = {}
_at = 0
for _name, _n in (("gq", 128), ("gk", 128), ("gqd", 32), ("gkd", 32), ("gdout", 64), ("lamq", 64), ("lamk", 64),
                  ("sink", 4), ("alog", 8), ("dtb", 8), ("dskip", 4), ("gssm", 256), ("laminit", 1), ("onemlam", 1)):
    ROW[_name] = (_at, _at + _n)
    _at += _n
NROW = _at
COLS = {"gn1": (0, 8), "gn2": (8, 16), "convw": (16, 36), "convb": (36, 40), "bada": (40, 72)}
NCOL = 72
CACHE = {"ak": (0, 128), "bk": (128, 256), "av": (256, 384), "bv": (384, 512), "dk": (512, 768), "dv": (768, 1024),
         "ssm": (1024, 1280)}
NCACHE = 1280
CST = {}
_at = 0
for _name, _n in (("ident", 128), ("sel", 2), ("upto", 128), ("from", 128), ("negbelow", 128), ("negabove", 128), ("ones", 128),
                  ("selb", 256), ("iota", 128), ("cos", 128), ("sin", 128),
                  ("cosd", 64), ("sind", 64), ("zero", 128)):
    CST[_name] = (_at, _at + _n)
    _at += _n
NCST = _at
NCST0 = CST["sel"][1]




def big_results():
    out = []
    for v in range(2):
        out += [(("row", v, h), "act") for h in range(2)]
    out += [(("col", v), "dve") for v in range(2)]
    out += [(("hT", k), "dve" if k % 2 else "act") for k in range(KD)]
    out += [(("ab", t, b), "act") for b in range(2) for t in range(NT)]
    for t in range(NT):
        out += [(("dqk", t), "act"), (("dv", t), "act")]
    out += [(("z", t), "act") for t in range(NT)]
    out += [(("xbc", g), "act") for g in range(4)]
    out += [(("g", 0, s // 2, s % 2), "act") for s in range(3)]
    for t in range(NT):
        out += [(("qkT", t, b), "act") for b in range(2)] + [(("g", 0, (t + 3) // 2, (t + 3) % 2), "act")]
    out += [(("ckT",), "act")] + [(("dT", t), "act") for t in range(NT)] + [(("cdT",), "act")]
    for i in range(4):
        if i < 3:
            out += [(("g", i + 1, t, h), "act") for t in range(NT) for h in range(2)]
        if i == 2:
            out += [(("row", 2, h), "act") for h in range(2)]
            out += [(("uT", t), "act") for t in range(NT)]
            out += [(("cum",), "dve"), (("h0T",), "act")]
            out += [(("row", 3, h), "act") for h in range(2)]
            out += [(("dec", 0, d), "act") for d in range(2)]
        if i == 3:
            for t in range(NT):
                out += [(("GT", t, 0), "dve"), (("GT", t, 1), "dve")]
                if t + 1 < NT:
                    out += [(("dec", t + 1, d), "act") for d in range(2)]
            out.append((("row", 4, 0), "act"))
            out += [(("yo", t, g), "dve") for t in (1, 2) for g in range(2)]
            out += [(("row", 4, 1), "act"), (("col", 3), "dve")]
        out += [(("boT", i, k), "dve") for k in range(2)]
        out += [(("up", i, t, h), "dve") for t in range(NT) for h in range(2)]
    out.append((("col", 4), "dve"))
    out += [(("mT", k), "dve" if k % 2 else "act") for k in range(KD)]
    out += [(("gb", g, h), "act") for g in range(2) for h in range(2)]
    out += [(("out", t, h), "dve") for t in range(NT) for h in range(2)]
    out += [(("row", 5, h), "act") for h in range(2)]
    out += [(("h2T", k), "dve" if k % 2 else "act") for k in range(KD)]
    out += [(("lg",), "dve"), (("affT",), "act")]
    out += [(("gb2", g, h), "act") for g in range(2) for h in range(2)]
    out += [(("mk",), "act"), (("rank",), "dve")]
    return out


BIG = big_results()
BIG_AT = {name: n for n, (name, _) in enumerate(BIG)}
BIG_BY = dict(BIG)


def taken_by(name):
    n = BIG_AT[name]
    by = BIG[n][1]
    return by, sum(1 for _, e in BIG[:n + 1] if e == by)


def trunk_kernel(nc, x_prompt, x_sample, cvecT, rowp, colp, caches, b_ada, w_ada, w_in, w_br, w_out, w_router,
                 w_e1, w_e3, w_e2, consts, y_prompt, y_sample, o_ak, o_av, o_bk, o_bv, o_ssm, o_dk, o_dv):
    with ExitStack() as ctx:
        def sb(name, shape):
            return ctx.enter_context(nc.sbuf_tensor(name, shape, F32))

        def sem(name):
            return ctx.enter_context(nc.semaphore(name))

        ring = sb("ring", [P, SLOTS, 4, D])
        x = sb("x", [P, NT, D])
        xn = sb("xn", [P, NT, D])
        hT = sb("hT", [P, KD, T])
        cst = sb("cst", [P, NCST])
        gaterow = sb("gaterow", [P, 2, D])
        rp = sb("rp", [P, NROW])
        cp = sb("cp", [P, NCOL])
        ca = sb("ca", [P, NCACHE])
        wr = sb("wr", [P, KD, NE])
        cs = sb("cs", [P, KD, 2])
        csw = sb("csw", [P, KD, 32])
        modc = sb("modc", [P, 4, KD, 2])
        gs = sb("gs", [P, 2, KD, 2])
        st = sb("st", [P, 6, 48])
        stw = sb("stw", [P, 48])
        dsm = sb("dsm", [P, 88])
        expa, lamd, lamx, nlam, nsink = dsm[:, 0:8], dsm[:, 8:10], dsm[:, 10:12], dsm[:, 12:13], dsm[:, 13:17]
        xmark = dsm[:, 17:18]
        amark = dsm[:, 18:19]
        lamt = dsm[:, 20:84]
        used = [0]
        SCR = 20520
        scr = sb("scr", [P, SCR])

        def at(off, n):
            assert off + n <= SCR
            return scr[:, off:off + n]

        def take(n):
            used[0] += n
            return at(used[0] - n, n)

        G = [take(NT * D).rearrange("p (t n) -> p t n", t=NT) for _ in range(2)]
        abo = used[0]
        AB = take(2304).rearrange("p (t b n) -> p t b n", t=NT, b=2)
        qko = used[0]
        qT = take(2 * 2 * T).rearrange("p (b g t) -> p b g t", b=2, g=2)
        kT = take(2 * 512).rearrange("p (b t) -> p b t", b=2)
        dqT = take(2 * T).rearrange("p (c t) -> p c t", c=2)
        dkT = take(2 * 512).rearrange("p (c t) -> p c t", c=2)
        vab = take(NT * 256).rearrange("p (t b n) -> p t b n", t=NT, b=2)
        vd = take(NT * 256).rearrange("p (t n) -> p t n", t=NT)
        qkend = used[0]
        sz = take(NT * 256).rearrange("p (t n) -> p t n", t=NT)
        xbc = take(4 * PADW).rearrange("p (g n) -> p g n", g=4)
        uT = xbc[:, :, 0:T]
        bof = used[0]
        bo = take(NT * 256).rearrange("p (t n) -> p t n", t=NT)
        boT = take(2 * T).rearrange("p (c t) -> p c t", c=2)
        DQ = at(bof, NT * 512).rearrange("p (t n) -> p t n", t=NT)
        po = used[0]
        pr = take(2 * 768).rearrange("p (i n) -> p i n", i=2)
        pT = take(2 * T).rearrange("p (i n) -> p i n", i=2)
        tmp = at(po, 2 * 768).rearrange("p (i n) -> p i n", i=2)
        cacc = at(po, 4 * NU_CONV).rearrange("p (i n) -> p i n", i=4)
        so = [qko]

        def over(n):
            so[0] += n
            assert so[0] <= qkend
            return at(so[0] - n, n)

        xsB = over(NT * 384).rearrange("p (t n) -> p t n", t=NT)
        E = over(8 * P).rearrange("p (j l) -> p j l", j=8)
        Mt = over(8 * P).rearrange("p (j l) -> p j l", j=8)
        xdt = over(1024).rearrange("p (i d h n) -> p i d h n", i=2, d=2, h=4)
        xde = over(512).rearrange("p (d h n) -> p d h n", d=2, h=4)
        hin = over(512).rearrange("p (i n) -> p i n", i=4)
        sst = over(256).rearrange("p (i n) -> p i n", i=4)
        sm = over(72).rearrange("p (i t j) -> p i t j", i=3, t=NT)
        ex = over(72).rearrange("p (i t j) -> p i t j", i=3, t=NT)
        nacs = over(24).rearrange("p (t j) -> p t j", t=NT)
        dtk = sb("dtk", [P, 5, 24])
        dtr, dt_, la = (dtk[:, i, :].rearrange("p (t j) -> p t j", t=NT) for i in range(3))
        dabs = dtk[:, 3, :].rearrange("p (t j) -> p t j", t=NT)
        dexp = dtk[:, 4, :].rearrange("p (t j) -> p t j", t=NT)
        rsb = at(abo, 2 * D).rearrange("p (i n) -> p i n", i=2)
        gbc = at(0, 2 * D).rearrange("p (g n) -> p g n", g=2)
        gtmp = at(2 * D, D).rearrange("p (i n) -> p i n", i=2)
        gsq = at(3 * D, D)
        eo = [0]

        def exp_take(n):
            eo[0] += n
            return at(eo[0] - n, n)

        eo[0] = 3 * D
        XT = exp_take(KD * XTN).rearrange("p (k c) -> p k c", k=KD)
        Sc = exp_take(256).rearrange("p (e c) -> p e c", e=NE)
        Sl = exp_take(2 * 512).rearrange("p (i e c) -> p i e c", i=2, e=NE)
        xcur = exp_take(KD * 64).rearrange("p (k c) -> p k c", k=KD)
        sgs = exp_take(T).rearrange("p (t c) -> p t c", t=NT)
        sgT = exp_take(T).rearrange("p (t c) -> p t c", t=NT)
        ro = eo[0]
        hs = exp_take(HALF)
        hid = exp_take(HALF).rearrange("p (b n) -> p b n", b=4)
        hidT = exp_take(HALF).rearrange("p (b n) -> p b n", b=4)
        yo = exp_take(HALF)
        aff = exp_take(48).rearrange("p (t e) -> p t e", t=NT)
        pos = exp_take(48).rearrange("p (t e) -> p t e", t=NT)
        msk = exp_take(48).rearrange("p (t e) -> p t e", t=NT)
        affT = scr[0:NE, ro:ro + T]
        wrk = scr[0:NE, ro + T:ro + 2 * T]
        top8 = scr[0:NE, ro + 2 * T:ro + 2 * T + 16]
        maskT = scr[0:NE, ro + 2 * T + 16:ro + 3 * T + 16]
        spare = [at(eo[0], D), at(eo[0] + D, D)]
        more = at(SCR - 2 * 4 * D, 2 * 4 * D).rearrange("p (s k n) -> p s k n", s=2, k=4)
        assert eo[0] + 2 * D <= SCR - 2 * 4 * D
        idle = [hT[:, 0:8, :].rearrange("p k t -> p (k t)")[:, i * D:(i + 1) * D] for i in range(3)] + \
            [at(2 * D, D), gaterow[:, 0, :], gaterow[:, 1, :]] + spare

        def chunk(s, k):
            if s < SLOTS:
                return ring[:, s, k, :]
            return more[:, s - SLOTS, k, :] if s < SLOTS_E else idle[4 * (s - SLOTS_E) + k]


        banks = [ctx.enter_context(nc.psum_tensor(f"bank{i}", [P, 512], F32)) for i in range(8)]

        def c_(name):
            return cst[:, CST[name][0]:CST[name][1]]

        def r_(name):
            return rp[:, ROW[name][0]:ROW[name][1]]

        def ch(name):
            return ca[:, CACHE[name][0]:CACHE[name][1]]

        ident = c_("ident")
        gqc = r_("gq").rearrange("p (b n) -> p b n", b=2)
        gkc = r_("gk").rearrange("p (b n) -> p b n", b=2)

        def rep(ap, axis, n):
            a = ap.unsqueeze(axis)
            shape = list(a.shape)
            shape[axis] = n
            return a.broadcast_to(shape)

        loaded = [sem(f"loaded{i}") for i in range(SLOTS_E + 2)]
        freed = [sem(f"freed{i}") for i in range(SLOTS_E)]
        in_x = sem("in_x")
        in_cst0 = sem("in_cst0")
        in_cst = sem("in_cst")
        in_cond = sem("in_cond")
        cond0 = sem("cond_zero")
        cond = sem("cond_ready")
        done_pe, done_act, done_dve, done_pool = (sem(f"done_{e}") for e in ("pe", "act", "dve", "pool"))
        layer_go = sem("layer_go")
        dummy, dummy_pe, dummy_act, dummy_dve, dummy_sp = (sem(f"passed_{e}") for e in ("pool", "pe", "act", "dve", "sp"))
        y_out = sem("y_out")
        params_c = sem("params_c")
        params = sem("params")
        kv_out = sem("kv_out")
        ssm_out = sem("ssm_out")
        bias_row1, bias_row2 = sem("bias_row1"), sem("bias_row2")
        x_final = sem("x_final")
        layer_sems = []

        def lsem(name):
            layer_sems.append(sem(name))
            return layer_sems[-1]

        pads = lsem("pads")
        big = lsem("big_ready")
        big_act = lsem("big_taken_act")
        big_dve = lsem("big_taken_dve")
        big_of = {"act": big_act, "dve": big_dve}
        mod1 = lsem("mod_ready")
        act_sq = lsem("squares_ready")
        sq_free = lsem("squares_used")
        var_ready = lsem("variance_ready")
        root_ready = lsem("root_ready")
        xn_ready = lsem("xn_ready")
        ab_ready = lsem("ab_ready")
        d_ready = lsem("d_ready")
        dt_abs = lsem("dt_abs")
        dt_log = lsem("dt_log")
        dt_done = lsem("dt_done")
        lam_dot = lsem("lam_dot")
        lam_exp = lsem("lam_exp")
        conv_sum = lsem("conv_sum")
        conv_out = lsem("conv_out")
        s_ready = lsem("scores_ready")
        m_ready = lsem("max_ready")
        aff_in = lsem("aff_in")
        aff_exp = lsem("aff_exp")
        w1hot = lsem("expert_hot")
        p_ready = lsem("probs_ready")
        w_ready = lsem("diffprobs_ready")
        pt_ready = lsem("probsT_ready")
        pts_ready = lsem("probsT_sbuf")
        pv_ready = lsem("pv_ready")
        o_ready = lsem("o_taken")
        bo_ready = lsem("branch_ready")
        merged = lsem("merged")
        ssd_small = lsem("ssd_small")
        ssd_exp = lsem("ssd_exp")
        mt_ready = lsem("mt_ready")
        h_in = lsem("h_in")
        x_ready = lsem("x_ready")
        aff_ready = lsem("aff_ready")
        mask_ready = lsem("mask_ready")
        mk_ready = lsem("mk_ready")
        hot_ready = lsem("hot_ready")
        xc_ready = lsem("xcur_ready")
        h3_ready = lsem("h3_ready")
        silu_ready = lsem("silu_ready")
        hid_ready = lsem("hid_ready")
        ht_ready = lsem("hidT_ready")
        hts_ready = lsem("hidT_sbuf")
        yp_ready = lsem("yo_psum")
        sg_ready = lsem("sgT_ready")
        sgs_ready = lsem("sgT_sbuf")
        yo_ready = lsem("yo_sbuf")
        sty_ready = lsem("tile_products")
        st0_taken = lsem("states_taken")
        y_taken = lsem("tile_taken")
        u_ready = lsem("gated_outputs")
        sc_ready = lsem("prompt_hot")
        gath = lsem("gathered")
        gath_act = lsem("gath_taken_act")
        gath_dve = lsem("gath_taken_dve")
        closed = lsem("sums_closed")
        act_step = lsem("act_step")
        dve_step = lsem("dve_step")
        numbers = sorted(s.num for s in layer_sems)
        assert numbers == list(range(numbers[0], numbers[0] + len(numbers)))

        def iters(i):
            return [(h, t) for h in range(4) for t in range(NT)]

        NIT = 12

        block = ctx.enter_context(nc.Block())

        @block.sync
        def _(sp):
            sp.dma_start(cs[:, :, :], cvecT).then_inc(in_cond, 16)

            def load(n, s, src, cols, chunks=4):
                if not (isinstance(n, int) and n == 0):
                    sp.wait_ge(freed[s], n)
                sp.dma_start((ring[:, s] if s < SLOTS else more[:, s - SLOTS])[:, 0:chunks, 0:cols],
                             src.rearrange("(k p) n -> p k n", p=P)).then_inc(loaded[s], 16)

            def mixer_weights(li, first, last):
                plan = {}
                for h in range(2):
                    rows = slice(h * HALF, (h + 1) * HALF)
                    for v in range(6):
                        plan[AT_ADA[v] + h] = (w_ada[li, rows, v * D:(v + 1) * D], D, 4)
                    for j, c0, n in ((AT_AB, COL_A, D), (AT_D, COL_D, ND_), (AT_C, COL_C, NC_)):
                        plan[j + h] = (w_in[li, rows, c0:c0 + n], n, 4)
                    for i, br in enumerate(BRANCH):
                        plan[AT_GATE[i] + h] = (w_in[li, rows, COL_G + br * D:COL_G + (br + 1) * D], D, 4)
                    plan[AT_OUT + h] = (w_out[li, rows, :], D, 4)
                for i, br in enumerate(BRANCH):
                    plan[AT_LIFT[i]] = (w_br[li, br, :, :], D, 2)
                assert sorted(plan) == list(range(LOADS0))
                for j in range(first, last):
                    src, cols, chunks = plan[j]
                    load(li * PER[j % SLOTS] + j // SLOTS, j % SLOTS, src, cols, chunks)

            def expert_weights(li):
                def half(s, e):
                    if s < 2:
                        before = LOADS0 // SLOTS + (0 if isinstance(e, int) and e == 0 else e - 1)
                    else:
                        before = LOADS0 // SLOTS + e if s < SLOTS else e
                    if s >= SLOTS and isinstance(e, int) and e == 0:
                        before, base = 0, 0
                    else:
                        base = li * PER[s]
                    load(base + before, s, (w_e1, w_e3, w_e2)[s // 2][li, e, (s % 2) * HALF:(s % 2 + 1) * HALF, :], D)

                sp.wait_ge(ssm_out, (li + 1) * 64)
                sp.sem_inc(dummy_sp, 1)
                sp.wait_ge(big, BIG_AT[("up", 3, NT - 1, 1)] + 1)
                for s in (4, 5, 0, 1, 2, 3):
                    half(s, 0)
                sp.wait_ge(big, BIG_AT[("gb2", 1, 1)] + 1)
                for s in range(2):
                    for k in range(4):
                        r = s * HALF + k * P
                        sp.dma_start(chunk(SLOTS_E + s, k), w_e1[li, 1, r:r + P, :]).then_inc(loaded[SLOTS_E + s], 16)
                for e, slots in ((2, (0, 1)), (1, (2, 3, 4, 5)), (2, (2, 3, 4, 5))):
                    for s in slots:
                        half(s, e)
                with sp.Fori(3, NE) as e:
                    for s in range(SLOTS_E):
                        half(s, e)

            def layer_end(li):
                for s in (done_pe, done_act, done_dve, done_pool):
                    sp.wait_ge(s, li + 1)
                sp.sem_inc(dummy_sp, 1)
                sp.sem_clear(range(numbers[0], numbers[-1] + 1))
                sp.sem_inc(layer_go, 1)

            mixer_weights(0, 0, 2)
            sp.dma_start(x[:, 0, :], x_prompt.rearrange("a s d -> (a s) d")).then_inc(in_x, 16)
            sp.dma_start(x[:, 1:3, :], x_sample.rearrange("a (t p) d -> p (a t) d", p=P)).then_inc(in_x, 16)
            sp.dma_start(cst[:, 0:NCST0], consts[:, 0:NCST0]).then_inc(in_cst0, 16)
            mixer_weights(0, 2, SLOTS)
            with sp.Fori(0, DEPTH - 1) as li:
                mixer_weights(li, SLOTS, LOADS0)
                expert_weights(li)
                mixer_weights(li + 1, 0, SLOTS)
                layer_end(li)
            mixer_weights(DEPTH - 1, SLOTS, LOADS0)
            expert_weights(DEPTH - 1)
            sample = y_sample.rearrange("a (t p) d -> (a t) p d", p=P)
            for t in range(NT):
                sp.wait_ge(x_final, NT * (DEPTH - 1) + t + 1)
                sp.dma_start(y_prompt.rearrange("a s d -> (a s) d") if t == 0 else sample[t - 1],
                             x[:, t, :]).then_inc(y_out, 16)
            layer_end(DEPTH - 1)
            sp.wait_ge(y_out, 16 * NT)

        @block.gpsimd
        def _(pool):
            def parameters(li, first=False):
                pool.dma_start(cp[:, :], colp[li, :, :]).then_inc(params_c, 16)
                if first:
                    pool.wait_ge(loaded[(AT_AB + 1) % SLOTS], 16 * ((AT_AB + 1) // SLOTS + 1))
                    pool.dma_start(cst[:, NCST0:NCST], consts[:, NCST0:NCST]).then_inc(in_cst, 16)
                pool.dma_start(rp[:, :], rowp[li, :].partition_broadcast(P)).then_inc(params, 16)
                pool.dma_start(ca[:, :], caches[li, :, :]).then_inc(params, 16)
                pool.dma_start(wr[:, :, :], w_router[li, :, :].rearrange("(k p) e -> p k e", p=P)).then_inc(params, 16)

            def mixers(li):
                pool.memset(xbc[:, :, :], 0.0).then_inc(pads, 1)
                pool.wait_ge(ab_ready, 1)
                pool.dma_start(o_ak[0, li].rearrange("s h d -> s (h d)"), AB[:, 0, 0, 256:384]).then_inc(kv_out, 16)
                pool.dma_start(o_bk[0, li].rearrange("s h d -> s (h d)"), AB[:, 0, 1, 256:384]).then_inc(kv_out, 16)
                pool.wait_ge(big_act, taken_by(("ab", 0, 1))[1])
                pool.dma_start(o_av[0, li].rearrange("s h d -> s (h d)"), vab[:, 0, 0, :]).then_inc(kv_out, 16)
                pool.dma_start(o_bv[0, li].rearrange("s h d -> s (h d)"), vab[:, 0, 1, :]).then_inc(kv_out, 16)
                pool.wait_ge(d_ready, 1)
                pool.dma_start(o_dk[0, li].rearrange("s h m d -> s (h m d)"), DQ[:, 0, 256:512]).then_inc(kv_out, 16)
                pool.wait_ge(big_act, taken_by(("dv", 0))[1])
                pool.dma_start(o_dv[0, li].rearrange("s h d -> s (h d)"), vd[:, 0, :]).then_inc(kv_out, 16)

                def bias_row(i, v):
                    pool.wait_ge(big_act, taken_by(("row", v, 1))[1])
                    pool.dma_start(gaterow[2:3, i, :], b_ada[li, v * D:(v + 1) * D].unsqueeze(0)).then_inc((bias_row1, bias_row2)[i], 16)

                bias_row(0, 2)
                pool.wait_ge(st0_taken, 1)
                for d in range(2):
                    for g in range(2):
                        pool.dma_start(o_ssm[0, li, d, 2 * g:2 * g + 2].rearrange("h p n -> (h p) n"),
                                       sst[:, 2 * d + g, :]).then_inc(ssm_out, 16)
                bias_row(1, 5)
                pool.wait_ge(kv_out, (li + 1) * 96)
                pool.sem_inc(dummy, 1)
                pool.wait_ge(ssm_out, (li + 1) * 64)
                pool.sem_inc(dummy, 1)
                pool.wait_ge(bias_row2, (li + 1) * 16)
                pool.sem_inc(dummy, 1)

            def layer_end(li):
                pool.drain().then_inc(done_pool, 1)
                pool.wait_ge(layer_go, li + 1)
                pool.sem_inc(dummy, 1)

            pool.memset(csw[:, :, :], 0.0).then_inc(cond0, 1)
            parameters(0, first=True)
            with pool.Fori(0, DEPTH - 1) as li:
                mixers(li)
                pool.wait_ge(big_dve, taken_by(("lg",))[1])
                parameters(li + 1)
                layer_end(li)
            mixers(DEPTH - 1)
            layer_end(DEPTH - 1)

        @block.tensor
        def _(pe):
            owed = []

            def mm(out, lhsT, rhs, start=True, stop=True, signal=None, **kw):
                ins = pe.matmul(out, lhsT, rhs, start=start, stop=stop, **kw)
                if signal is not None:
                    ins.then_inc(signal, 1)
                elif owed:
                    ins.then_inc(owed.pop(0), 1)
                return ins

            def turn(out, in_, signal=None):
                k = in_.shape[0]
                ins = pe.transpose(out, in_, ident[0:k, 0:k])
                if signal is not None:
                    ins.then_inc(signal, 1)
                elif owed:
                    ins.then_inc(owed.pop(0), 1)
                return ins

            count = [0]

            def bank(name):
                n = count[0]
                assert BIG[n][0] == name, (BIG[n], name)
                count[0] += 1
                if n >= 4:
                    by, value = taken_by(BIG[n - 4][0])
                    pe.wait_ge(big_of[by], value)
                return banks[n % 4]

            def taken(name):
                by, value = taken_by(name)
                pe.wait_ge(big_of[by], value)

            pe.wait_ge(cond, 1)
            with pe.Fori(0, DEPTH) as li:
                count[0] = 0

                def need(j):
                    pe.wait_ge(loaded[j % SLOTS], (li * PER[j % SLOTS] + (j // SLOTS + 1)) * 16)

                def rows(v, h):
                    j = AT_ADA[v]
                    if h == 0:
                        need(j)
                        need(j + 1)
                    b = bank(("row", v, h))
                    cols = slice(h * HALF, (h + 1) * HALF)
                    for k in range(KD):
                        q = 32 * (k % 4)
                        sig = big if k == KD - 1 else freed[j % SLOTS] if h and k == 3 else None
                        mm(b[q:q + 32, :], csw[:, k, :], ring[:, (j + k // 4) % SLOTS, k % 4, cols],
                           start=k < 4, stop=k >= 4, signal=sig)
                    if h:
                        owed.append(freed[(j + 1) % SLOTS])

                def columns(v):
                    taken(("row", v, 1))
                    b = bank(("col", v))
                    for k in range(KD):
                        mm(b[:, 2 * k:2 * k + 2], rsb[:, v % 2, k * P:(k + 1) * P], c_("sel"),
                           signal=big if k == KD - 1 else None)

                for v in range(2):
                    j = AT_ADA[v]
                    bs = [bank(("row", v, h)) for h in range(2)]
                    for c in range(2):
                        need(j + c)
                        for h in range(2):
                            for k in range(4 * c, 4 * c + 4):
                                q = 32 * (k % 4)
                                sig = big if k == KD - 1 else freed[j % SLOTS] if h and k == 3 else None
                                mm(bs[h][q:q + 32, :], csw[:, k, :],
                                   ring[:, (j + c) % SLOTS, k % 4, h * HALF:(h + 1) * HALF],
                                   start=c == 0, stop=c == 1, signal=sig)
                    owed.append(freed[(j + 1) % SLOTS])
                pe.wait_ge(in_cst0, 16)
                for v in range(2):
                    columns(v)

                def widths(name):
                    for k in range(KD):
                        if k == 0:
                            pe.wait_ge(xn_ready, NT * (1 if name == "hT" else 2))
                        b = bank((name, k))
                        for t in range(NT):
                            turn(b[:, t * P:(t + 1) * P], xn[:, t, k * P:(k + 1) * P],
                                 signal=big if t == NT - 1 else None)

                def tokens(out, t, j, cols, signal=None, free=False, ks=range(KD)):
                    for k in ks:
                        sig = None
                        if free and k == 3:
                            sig = freed[j % SLOTS]
                        if k == KD - 1:
                            sig = signal
                        mm(out, hT[:, k, t * P:(t + 1) * P], ring[:, (j + k // 4) % SLOTS, k % 4, cols],
                           start=k == 0, stop=k == KD - 1, signal=sig)
                    if free and KD - 1 in ks:
                        owed.append(freed[(j + 1) % SLOTS])

                widths("hT")
                taken(("hT", KD - 2))
                taken(("hT", KD - 1))
                need(AT_AB)
                need(AT_AB + 1)
                for br in range(2):
                    for t in range(NT):
                        tokens(bank(("ab", t, br))[:, :], t, AT_AB, slice(br * 512, br * 512 + 512), signal=big,
                               free=(br == 1 and t == NT - 1))
                need(AT_D)
                need(AT_D + 1)
                for t in range(NT):
                    tokens(bank(("dqk", t))[:, :], t, AT_D, slice(0, 512), signal=big)
                    tokens(bank(("dv", t))[:, 0:ND_ - 512], t, AT_D, slice(512, ND_), signal=big, free=t == NT - 1)
                need(AT_C)
                need(AT_C + 1)
                for t in range(NT):
                    tokens(bank(("z", t))[:, 0:256], t, AT_C, slice(0, 256), signal=big)
                for g in range(4):
                    b = bank(("xbc", g))
                    for k in range(KD):
                        sig = None
                        if g == 3 and k == 3:
                            sig = freed[AT_C % SLOTS]
                        if k == KD - 1:
                            sig = big
                        mm(b[:, 0:T], ring[:, (AT_C + k // 4) % SLOTS, k % 4, 256 + g * P:256 + (g + 1) * P], hT[:, k, :],
                           start=k == 0, stop=k == KD - 1, signal=sig)
                owed.append(freed[(AT_C + 1) % SLOTS])

                gate_bank = [None]

                def gate(i, s, part):
                    j = AT_GATE[i]
                    if s == 0:
                        need(j + part)
                    t, h = s // 2, s % 2
                    if part == 0:
                        gate_bank[0] = bank(("g", i, t, h))
                    tokens(gate_bank[0][:, :], t, j, slice(h * HALF, (h + 1) * HALF), signal=big, free=s == 5,
                           ks=range(4 * part, 4 * part + 4))

                def gate0(s):
                    for part in range(2):
                        gate(0, s, part)

                for s in range(3):
                    gate0(s)

                pe.wait_ge(in_cst, 16)
                pe.wait_ge(params, (li + 1) * 48)
                pe.wait_ge(ab_ready, 1)
                for t in range(NT):
                    for br in range(2):
                        b = bank(("qkT", t, br))
                        for g in range(2):
                            turn(b[:, g * P:(g + 1) * P], AB[:, t, br, g * P:(g + 1) * P])
                        turn(b[:, 256:384], AB[:, t, br, 256:384], signal=big)
                    gate0(3 + t)
                b = bank(("ckT",))
                turn(b[:, 0:P], ch("ak"))
                turn(b[:, P:2 * P], ch("bk"), signal=big)
                pe.wait_ge(d_ready, 1)
                for t in range(NT):
                    b = bank(("dT", t))
                    for c in range(4):
                        turn(b[:, c * P:(c + 1) * P], DQ[:, t, c * P:(c + 1) * P], signal=big if c == 3 else None)
                b = bank(("cdT",))
                turn(b[:, 0:P], ch("dk")[:, 0:P])
                turn(b[:, P:2 * P], ch("dk")[:, P:2 * P], signal=big)
                taken(("cdT",))

                def keys(t):
                    return (0, P) if t == 0 else (P, 512)

                def values(i, h, t):
                    cols = slice((h // 2) * HD, (h // 2) * HD + HD) if i < 2 else slice(h * HD, h * HD + HD)
                    own = [0] if t == 0 else [1, 2]
                    out = [vab[:, s, i, cols] if i < 2 else vd[:, s, cols] for s in own]
                    if t:
                        out.append(ch(("av", "bv", "dv")[i])[:, cols])
                    return out

                def scores(i, n):
                    h, t = iters(i)[n]
                    k0, k1 = keys(t)
                    step = i * NIT + n
                    if i < 2:
                        v, g = h // 2, h % 2
                        rows = slice(v * HD, (v + 1) * HD)
                        b = banks[4 + n % 2]
                        if n >= 2:
                            pe.wait_ge(p_ready, step - 1)
                        elif i:
                            pe.wait_ge(p_ready, i * NIT)
                        masked = i == 1 and t > 0
                        mm(b[:, 0:k1 - k0], qT[rows, i, g, t * P:(t + 1) * P], kT[rows, i, k0:k1], start=True,
                           stop=True, signal=None if masked else s_ready, skip_group_check=masked)
                        if masked:
                            other = slice(P, 2 * P) if t == 1 else slice(0, P)
                            mm(b[:, other], ident, c_("negabove") if t == 1 else c_("negbelow"), start=False, stop=True,
                               signal=s_ready, skip_group_check=True)
                    else:
                        if n:
                            pe.wait_ge(p_ready, 2 * NIT + n)
                        else:
                            pe.wait_ge(p_ready, 2 * NIT)
                        for m in range(2):
                            j = 2 * h + m
                            r = slice(32 * (j % 4), 32 * (j % 4) + 32)
                            mm(banks[4 + m][:, 0:k1 - k0], dqT[r, j // 4, t * P:(t + 1) * P], dkT[r, j // 4, k0:k1],
                               tile_position=(32 * (j % 4), 0), signal=s_ready if m else None)

                def weights(i, n):
                    h, t = iters(i)[n]
                    step = i * NIT + n
                    if i < 2:
                        pe.wait_ge(p_ready, step + 1)
                    else:
                        pe.wait_ge(w_ready, n + 1)
                    if step:
                        pe.wait_ge(pts_ready, step)
                    nb = len(values(i, h, t))
                    for k in range(nb):
                        turn(banks[6][:, k * P:(k + 1) * P], pr[:, n % 2, k * P:(k + 1) * P],
                             signal=pt_ready if k == nb - 1 else None)

                def weighted(i, n):
                    h, t = iters(i)[n]
                    step = i * NIT + n
                    pe.wait_ge(pts_ready, step + 1)
                    if step:
                        pe.wait_ge(o_ready, step)
                    vs = values(i, h, t)
                    for k, v in enumerate(vs):
                        mm(banks[7][:, 0:HD], pT[:, n % 2, k * P:(k + 1) * P], v, start=k == 0, stop=k == len(vs) - 1,
                           signal=pv_ready if k == len(vs) - 1 else None)

                def lift(i):
                    j = AT_LIFT[i]
                    if i < 2:
                        pe.wait_ge(o_ready, (i + 1) * NIT)
                    else:
                        pe.wait_ge(bo_ready, i - 1)
                    for c in range(2):
                        b = bank(("boT", i, c))
                        for t in range(NT):
                            turn(b[:, t * P:(t + 1) * P], bo[:, t, c * P:(c + 1) * P], signal=big if t == NT - 1 else None)
                    taken(("boT", i, 1))
                    need(j)
                    for t in range(NT):
                        for h in range(2):
                            b = bank(("up", i, t, h))
                            for c in range(2):
                                mm(b[:, :], boT[:, c, t * P:(t + 1) * P], ring[:, j % SLOTS, c, h * HALF:(h + 1) * HALF],
                                   start=c == 0, stop=c == 1, signal=big if c == 1 else None)
                    owed.append(freed[j % SLOTS])

                scores(0, 0)
                for i in range(3):
                    for n in range(NIT + 2):
                        if 1 <= n < NIT:
                            scores(i, n)
                        if 1 <= n <= NIT:
                            weights(i, n - 1)
                        if n >= 2:
                            weighted(i, n - 2)
                        if 1 <= n <= NIT:
                            gate(i + 1, (n - 1) // 2, (n - 1) % 2)
                        if i == 2 and n >= NIT:
                            rows(2, n - NIT)
                    if i < 2:
                        scores(i + 1, 0)
                        lift(i)

                pe.wait_ge(conv_out, 4)
                for t in range(NT):
                    b = bank(("uT", t))
                    for g in range(3):
                        turn(b[:, g * P:(g + 1) * P], uT[:, g, t * P:(t + 1) * P], signal=big if g == 2 else None)
                pe.wait_ge(dt_done, 1)
                b = bank(("cum",))
                for t in range(NT):
                    o = t * 16
                    mm(b[:, o:o + 4], c_("upto"), la[:, t, 0:4])
                    mm(b[:, o + 4:o + 8], c_("from"), la[:, t, 4:8])
                    mm(b[:, o + 8:o + 16], c_("ones"), la[:, t, :], signal=big if t == NT - 1 else None)
                b = bank(("h0T",))
                for d in range(2):
                    turn(b[:, d * P:(d + 1) * P], ch("ssm")[:, d * P:(d + 1) * P], signal=big if d else None)
                for h in range(2):
                    rows(3, h)

                def tri(d):
                    return c_("upto") if d == 0 else c_("from")

                def decays(t):
                    for d in range(2):
                        b = bank(("dec", t, d))
                        for h in range(4):
                            mm(b[:, h * P:(h + 1) * P], la[:, t, 4 * d + h:4 * d + h + 1].broadcast_to([P, P]), tri(d),
                               start=h == 0, stop=False, skip_group_check=True)
                        mm(b[:, :], ident, rep(c_("negbelow" if d == 0 else "negabove"), 1, 4), start=False, stop=True,
                           signal=big, skip_group_check=True)

                decays(0)
                lift(2)
                taken(("uT", 2))
                for t in range(NT):
                    for g in range(2):
                        b = bank(("GT", t, g))
                        r = slice(g * HD, (g + 1) * HD)
                        mm(b[:, 0:P], uT[r, 2, t * P:(t + 1) * P], uT[r, 3, t * P:(t + 1) * P], signal=big)
                    if t + 1 < NT:
                        decays(t + 1)
                    pe.wait_ge(mt_ready, t + 1)
                    if t == 1:
                        pe.wait_ge(st0_taken, 1)
                    elif t == 2:
                        pe.wait_ge(y_taken, 1)
                    b = banks[4]
                    if t == 0:
                        for d in range(2):
                            for g in range(2):
                                o = (2 * d + g) * HD
                                mm(b[:, o:o + HD], xde[:, d, 2 * g:2 * g + 2, :], xsB[:, t, 256 + g * HD:256 + (g + 1) * HD],
                                   signal=sty_ready if d and g else None)
                    else:
                        for g in range(2):
                            mm(b[g * HD:(g + 1) * HD, 0:P], xsB[:, t, 256 + g * HD:256 + (g + 1) * HD],
                               xde[:, t - 1, 2 * g:2 * g + 2, :], signal=sty_ready if g else None)
                    b = banks[5]
                    if t:
                        pe.wait_ge(y_taken, t)
                    for h in range(4):
                        for d in range(2):
                            mm(b[:, h * HD:(h + 1) * HD], Mt[:, 4 * d + h, :], xdt[:, t % 2, d, h, :], start=d == 0, stop=d == 1,
                               signal=sty_ready if (h == 3 and d == 1) else None)
                rows(4, 0)
                pe.wait_ge(h_in, 1)
                for t in (1, 2):
                    for g in range(2):
                        b = bank(("yo", t, g))
                        r = slice(g * HD, (g + 1) * HD)
                        for d in range(2):
                            i = (0, 3) if t == 1 else (1, 2)
                            mm(b[:, d * P:(d + 1) * P], uT[r, 3, t * P:(t + 1) * P], hin[r, i[d], :],
                               signal=big if d else None)
                rows(4, 1)
                columns(3)
                lift(3)
                columns(4)

                pe.wait_ge(merged, 18)
                for k in range(KD):
                    b = bank(("mT", k))
                    for t in range(NT):
                        turn(b[:, t * P:(t + 1) * P], xn[:, t, k * P:(k + 1) * P], signal=big if t == NT - 1 else None)

                def gate_rows(out, i, g, h, signal):
                    mm(out, c_("selb")[:, g * P:(g + 1) * P], gaterow[:, i, h * HALF:(h + 1) * HALF], signal=signal)

                pe.wait_ge(bias_row1, 16 * (li + 1))
                for g in range(2):
                    for h in range(2):
                        gate_rows(bank(("gb", g, h))[:, :], 0, g, h, big)
                taken(("mT", KD - 2))
                taken(("mT", KD - 1))
                need(AT_OUT)
                need(AT_OUT + 1)
                for t in range(NT):
                    for h in range(2):
                        tokens(bank(("out", t, h))[:, :], t, AT_OUT, slice(h * HALF, (h + 1) * HALF), signal=big,
                               free=t == NT - 1 and h == 1)

                for h in range(2):
                    rows(5, h)
                widths("h2T")
                taken(("h2T", KD - 2))
                taken(("h2T", KD - 1))
                b = bank(("lg",))
                for t in range(NT):
                    for k in range(KD):
                        mm(b[:, t * NE:(t + 1) * NE], hT[:, k, t * P:(t + 1) * P], wr[:, k, :], start=k == 0,
                           stop=k == KD - 1, signal=big if t == NT - 1 and k == KD - 1 else None)
                pe.wait_ge(aff_ready, 1)
                b = bank(("affT",))
                for t in range(NT):
                    turn(b[0:NE, t * P:(t + 1) * P], aff[:, t, :], signal=big if t == NT - 1 else None)
                pe.wait_ge(bias_row2, 16 * (li + 1))
                for g in range(2):
                    for h in range(2):
                        gate_rows(bank(("gb2", g, h))[:, :], 1, g, h, big)
                pe.wait_ge(mask_ready, 1)
                b = bank(("mk",))
                for t in range(NT):
                    turn(b[:, t * NE:(t + 1) * NE], maskT[:, t * P:(t + 1) * P], signal=big if t == NT - 1 else None)
                taken(("mk",))
                b = bank(("rank",))
                mm(b[:, 0:NE], c_("upto"), msk[:, 0, :], signal=h3_ready)
                mm(b[:, NE:2 * NE], c_("upto"), msk[:, 1, :], signal=sg_ready)
                mm(b[:, 2 * NE:3 * NE], c_("upto"), msk[:, 2, :], stop=False)
                mm(b[:, 2 * NE:3 * NE], c_("ones"), msk[:, 1, :], start=False, signal=big)
                for n in range(len(BIG) - 4, len(BIG)):
                    taken(BIG[n][0])

                def gather(e0, e1, turn_):
                    n = e1 - e0
                    for k in range(KD):
                        cols = slice(k * P, (k + 1) * P)
                        b = banks[6 + k % 2]
                        c = (KD * turn_ + k) // 2
                        if turn_ and k < 2:
                            pe.wait_ge((sgs_ready, yo_ready)[k], e0 + 1)
                        if k >= 2:
                            pe.wait_ge((gath_act, gath_dve)[k % 2], c)
                        if k == 0:
                            pe.wait_ge(sc_ready, 1)
                        mm(b[:, 0:16 * n], xn[:, 0, cols], Sc[:, e0:e1, :])
                        if k == 0:
                            pe.wait_ge(hot_ready, 1)
                        mm(b[:, 16 * n:48 * n], xn[:, 1, cols], Sl[:, 0, e0:e1, :], stop=False)
                        mm(b[:, 16 * n:48 * n], xn[:, 2, cols], Sl[:, 1, e0:e1, :], start=False, signal=gath)

                def scatter(h, tiles=range(NT), signal=None, first=False):
                    r = slice(h * 64, (h + 1) * 64)
                    for t in tiles:
                        mm(banks[2 * t + h][:, :], sgT[r, t, :], yo[r, :], start=first, stop=signal is not None,
                           skip_group_check=True, signal=signal)

                def one_expert(e):
                    def arrive(s):
                        if s >= SLOTS_E:
                            pe.wait_ge(loaded[s], (li + 1) * 64)
                        elif s < 2:
                            n = 1 if isinstance(e, int) and e == 0 else e
                            pe.wait_ge(loaded[s], (li * PER[s] + LOADS0 // SLOTS + n) * 16)
                        else:
                            before = LOADS0 // SLOTS if s < SLOTS else 0
                            pe.wait_ge(loaded[s], (li * PER[s] + before + e + 1) * 16)

                    def up(out, s0, last, free_last):
                        for k in range(KD):
                            s = s0 + k // 4
                            if k % 4 == 0:
                                arrive(s)
                            for h in range(2):
                                sig = None
                                if h and k == 3 and s < SLOTS_E:
                                    sig = freed[s]
                                if h and k == KD - 1 and s < SLOTS_E:
                                    sig = freed[s] if free_last else last
                                mm(out[h * 64:(h + 1) * 64, :], xcur[:, k, :], chunk(s, k % 4)[:, h * HALF:(h + 1) * HALF],
                                   start=k == 0, stop=k == KD - 1, signal=sig)
                        if not free_last:
                            owed.append(freed[s])

                    pe.wait_ge(xc_ready, e + 1)
                    pe.wait_ge(sgs_ready, e + 1)
                    up(banks[6], SLOTS_E if isinstance(e, int) and e == 1 else 0, None, True)
                    pe.wait_ge(yo_ready, e + 1)
                    up(banks[7], 2, h3_ready, False)
                    first = isinstance(e, int) and e == 1
                    if not (isinstance(e, int) and e == 0):
                        scatter(0, first=first)
                    pe.wait_ge(hid_ready, e + 1)
                    for b in range(4):
                        turn(banks[6][:, b * P:(b + 1) * P], hid[:, b, :], signal=ht_ready if b == 3 else None)
                    if not (isinstance(e, int) and e == 0):
                        scatter(1, first=first)
                    pe.wait_ge(w1hot, e + 1)
                    pe.wait_ge(hts_ready, e + 1)
                    for t in range(NT):
                        turn(banks[6][:, t * P:(t + 1) * P], sgs[:, t, :], signal=sg_ready if t == NT - 1 else None)
                    for fh in range(2):
                        arrive(4 + fh)
                        s = 4 + fh
                        for b in range(4):
                            for h in range(2):
                                sig = None
                                if b == 3 and h == 1:
                                    sig = yp_ready if fh else freed[s]
                                mm(banks[7][h * 64:(h + 1) * 64, :], hidT[:, b, fh * 64:(fh + 1) * 64],
                                   chunk(s, b)[:, h * HALF:(h + 1) * HALF], start=fh == 0 and b == 0,
                                   stop=fh == 1 and b == 3, signal=sig)
                    owed.append(freed[s])
                    mm(banks[0][:, 0:8], c_("zero"), c_("zero")[:, 0:8], start=False, stop=False, skip_group_check=True)

                for turn_, (e0, e1) in enumerate(STAGES):
                    gather(e0, e1, turn_)
                    pe.wait_ge(gath_act, KD // 2 * (turn_ + 1))
                    if e0 == 0:
                        one_expert(0)
                        one_expert(1)
                        e0 = 2
                    with pe.Fori(e0, e1) as e:
                        one_expert(e)
                pe.wait_ge(sgs_ready, NE + 1)
                pe.wait_ge(yo_ready, NE + 1)
                for t in range(NT):
                    for h in range(2):
                        scatter(h, (t,), closed)
                assert not owed
                pe.drain().then_inc(done_pe, 1)
                pe.wait_ge(layer_go, li + 1)
                pe.sem_inc(dummy_pe, 1)

        @block.scalar
        def _(act):
            A = nc.scalar.activation
            nbig = [0]
            own = [0]

            def step(ins):
                ins.then_inc(act_step, 1)
                own[0] += 1

            def settle():
                act.wait_ge(act_step, own[0])

            def grab(name):
                assert BIG_BY[name] == "act"
                act.wait_ge(big, BIG_AT[name] + 1)
                return banks[BIG_AT[name] % 4]

            def gave(name, ins):
                nbig[0] += 1
                assert taken_by(name) == ("act", nbig[0]), name
                ins.then_inc(big_act, 1)

            def taken_dve(name):
                act.wait_ge(big_dve, taken_by(name)[1])

            def ahead(func):
                settle()
                step(A(amark, c_("ident")[:, 0:1], func))

            roots = [0]

            def root(n):
                roots[0] += 1
                act.wait_ge(var_ready, roots[0])
                A(st[:, 1, 0:n], st[:, 0, 0:n], ACT.Sqrt).then_inc(root_ready, 1)

            def modulated(name, k, out_c, in_c, out_l, in_l, which):
                A(out_c, in_c, ACT.Identity, bias=modc[:, 2 * which, k, 0:1], scale=gs[:, which, k, 0:1])
                gave((name, k), A(out_l, in_l, ACT.Identity, bias=modc[:, 2 * which, k, 1:2], scale=gs[:, which, k, 1:2]))

            act.wait_ge(in_cond, 16)
            act.wait_ge(cond0, 1)
            A(csw[:, :, 0:2], cs[:, :, :], ACT.Silu).then_inc(cond, 1)
            act.wait_ge(in_x, 32)
            with act.Fori(0, DEPTH) as li:
                nbig[0] = own[0] = roots[0] = 0
                for t in range(NT):
                    A(xn[:, t, :], x[:, t, :], ACT.Square, accum_out=st[:, 4, t:t + 1]).then_inc(act_sq, 1)
                root(NT)

                def rows(v, h):
                    if v == 2 and h == 0:
                        act.wait_ge(kv_out, 96 * (li + 1))
                    b = grab(("row", v, h))
                    out = gaterow[:, v // 3, :] if v in (2, 5) else rsb[:, v % 2, :]
                    gave(("row", v, h), A(out[:, h * HALF:(h + 1) * HALF], b[:, :], ACT.Copy))

                for v in range(2):
                    for h in range(2):
                        rows(v, h)
                act.wait_ge(mod1, 1)

                def modulate(name, which):
                    for k in range(0, KD, 2):
                        b = grab((name, k))
                        modulated(name, k, hT[:, k, 0:P], b[:, 0:P], hT[:, k, P:T], b[:, P:T], which)

                modulate("hT", 0)
                for br in range(2):
                    for t in range(NT):
                        b = grab(("ab", t, br))
                        A(AB[:, t, br, 0:256].rearrange("p (g v d) -> p v g d", v=2, g=2),
                          b[:, 0:256].rearrange("p (v g d) -> p v g d", v=2, g=2), ACT.Copy)
                        A(AB[:, t, br, 256:384], b[:, 256:384], ACT.Copy)
                        gave(("ab", t, br), A(vab[:, t, br, :], b[:, 384:512], ACT.Copy))
                for t in range(NT):
                    act.wait_ge(big_act, taken_by(("ab", t, 1))[1])
                    if t >= 2:
                        act.wait_ge(sq_free, t - 1)
                    A(tmp[:, t % 2, :], AB[:, t, :, :].rearrange("p b n -> p (b n)"), ACT.Square).then_inc(act_sq, 1)
                for t in range(NT):
                    b = grab(("dqk", t))
                    A(dtr[:, t, :], b[:, 0:NDT], ACT.Copy)
                    gave(("dqk", t), A(DQ[:, t, 0:512 - NDT], b[:, NDT:512], ACT.Copy))
                    b = grab(("dv", t))
                    A(DQ[:, t, 512 - NDT:512], b[:, 0:NDT], ACT.Copy)
                    gave(("dv", t), A(vd[:, t, :], b[:, NDT:NDT + 256], ACT.Copy))
                root(36)
                for t in range(NT):
                    b = grab(("z", t))
                    gave(("z", t), A(sz[:, t, :], b[:, 0:256], ACT.Silu))
                act.wait_ge(pads, 1)
                for g in range(4):
                    b = grab(("xbc", g))
                    A(xbc[:, g, 2:2 + P], b[:, 0:P], ACT.Copy)
                    gave(("xbc", g), A(xbc[:, g, LAT0 + 2:LAT0 + 2 + 256], b[:, P:T], ACT.Copy))
                act.wait_ge(ab_ready, 1)
                for t in range(NT):
                    if t >= 2:
                        act.wait_ge(sq_free, NT + t - 1)
                    A(tmp[:, t % 2, 0:512], DQ[:, t, :], ACT.Square).then_inc(act_sq, 1)
                root(48)
                act.wait_ge(dt_abs, 1)
                step(A(dexp, dabs, ACT.Exp))
                settle()
                A(dexp, dexp, ACT.Ln, bias=1.0)
                A(expa, r_("alog"), ACT.Exp).then_inc(dt_log, 1)
                act.wait_ge(lam_dot, 1)
                A(lamx, lamd, ACT.Exp).then_inc(lam_exp, 1)

                def gate(i, s):
                    t, h = s // 2, s % 2
                    if s == 0 and i == 2:
                        taken_dve(("up", 0, NT - 1, 1))
                    elif s == 0 and i == 3:
                        act.wait_ge(merged, 6)
                    b = grab(("g", i, t, h))
                    gave(("g", i, t, h), A(G[i % 2][:, t, h * HALF:(h + 1) * HALF], b[:, :], ACT.Tanh, scale=0.5))

                def convolved(g):
                    act.wait_ge(conv_sum, g + 1)
                    bias = cp[:, COLS["convb"][0] + g:COLS["convb"][0] + g + 1]
                    A(uT[:, g, 0:P], cacc[:, g, 0:P], ACT.Silu, bias=bias)
                    A(uT[:, g, P:T], cacc[:, g, LAT0:LAT0 + 256], ACT.Silu, bias=bias).then_inc(conv_out, 1)

                for s in range(3):
                    gate(0, s)
                for t in range(NT):
                    for br in range(2):
                        b = grab(("qkT", t, br))
                        A(qT[:, br, :, t * P:(t + 1) * P], b[:, 0:256].rearrange("p (g t) -> p g t", g=2), ACT.Copy)
                        gave(("qkT", t, br), A(kT[:, br, t * P:(t + 1) * P], b[:, 256:384], ACT.Copy))
                    gate(0, 3 + t)
                    if t == 1:
                        for g in range(4):
                            convolved(g)
                b = grab(("ckT",))
                gave(("ckT",), A(kT[:, :, T:512], b[:, 0:256].rearrange("p (g t) -> p g t", g=2), ACT.Copy))
                for t in range(NT):
                    b = grab(("dT", t))
                    A(dqT[:, :, t * P:(t + 1) * P], b[:, 0:256].rearrange("p (g t) -> p g t", g=2), ACT.Copy)
                    gave(("dT", t), A(dkT[:, :, t * P:(t + 1) * P], b[:, 256:512].rearrange("p (g t) -> p g t", g=2), ACT.Copy))
                b = grab(("cdT",))
                gave(("cdT",), A(dkT[:, :, T:512], b[:, 0:256].rearrange("p (g t) -> p g t", g=2), ACT.Copy))

                def squared(n):
                    h, t = iters(2)[n]
                    act.wait_ge(o_ready, 2 * NIT + n + 1)
                    act.wait_ge(act_sq, 3 * NT + n)
                    A(lamt, bo[:, t, h * HD:(h + 1) * HD], ACT.Square,
                      accum_out=st[:, 5, 4 * t + h:4 * t + h + 1]).then_inc(act_sq, 1)

                for i in range(3):
                    its = iters(i)
                    for n in range(NIT + 1):
                        if n < NIT:
                            h, t = its[n]
                            nk = P if t == 0 else T
                            step_ = i * NIT + n
                            act.wait_ge(m_ready, step_ + 1)
                            q = 2 * (n % 4)
                            if i < 2:
                                ins = A(pr[:, n % 2, 0:nk], banks[4 + n % 2][:, 0:nk], ACT.Exp, bias=st[:, 1, q:q + 1],
                                        scale=HD ** -0.5, accum_out=st[:, 2, q:q + 1])
                                if i == 1:
                                    ins = A(st[:, 4, q:q + 1], r_("sink")[:, h:h + 1], ACT.Exp, bias=st[:, 1, q:q + 1])
                            else:
                                for m in range(2):
                                    ins = A(pr[:, n % 2, m * T:m * T + nk], banks[4 + m][:, 0:nk], ACT.Exp,
                                            bias=st[:, 1, q + m:q + m + 1], scale=32 ** -0.5,
                                            accum_out=st[:, 2, q + m:q + m + 1])
                            ins.then_inc(p_ready, 1)
                        if n >= 1:
                            h, t = its[n - 1]
                            nk = P if t == 0 else T
                            step_ = i * NIT + n - 1
                            act.wait_ge(pt_ready, step_ + 1)
                            if step_ >= 2:
                                act.wait_ge(pv_ready, step_ - 1)
                            A(pT[:, (n - 1) % 2, 0:nk], banks[6][:, 0:nk], ACT.Copy).then_inc(pts_ready, 1)
                        if n and n % 2 == 0:
                            gate(i + 1, n // 2 - 1)
                        if i == 2 and n == NIT:
                            ahead(ACT.Sqrt)
                        if i == 2 and n >= 2:
                            squared(n - 2)
                squared(NIT - 1)
                for h in range(2):
                    rows(2, h)
                for t in range(NT):
                    if t == 2:
                        root(12)
                    b = grab(("uT", t))
                    gave(("uT", t), A(xsB[:, t, :], b[:, 0:384], ACT.Copy))
                b = grab(("h0T",))
                A(hin[:, 0, :], b[:, 0:P], ACT.Copy)
                gave(("h0T",), A(hin[:, 2, :], b[:, P:2 * P], ACT.Copy))
                for h in range(2):
                    rows(3, h)
                act.wait_ge(ssd_small, 1)
                A(ex[:, :, :, :], sm[:, :, :, :], ACT.Exp).then_inc(ssd_exp, 1)
                for t in range(NT):
                    if t:
                        act.wait_ge(mt_ready, t)
                    for d in range(2):
                        b = grab(("dec", t, d))
                        for h in range(4):
                            ins = A(E[:, 4 * d + h, :], b[:, h * P:(h + 1) * P], ACT.Exp, bias=nacs[:, t, 4 * d + h:4 * d + h + 1])
                        gave(("dec", t, d), ins)
                    if t == 0:
                        act.wait_ge(sty_ready, 1)
                        A(sst[:, :, :], banks[4][:, 0:256].rearrange("p (i n) -> p i n", i=4), ACT.Copy)\
                            .then_inc(st0_taken, 1)
                for h in range(2):
                    rows(4, h)
                for t in range(NT):
                    act.wait_ge(u_ready, t + 1)
                    A(at(po + 1024 + 256 * t, 256), bo[:, t, :], ACT.Square, accum_out=st[:, 5, t:t + 1]).then_inc(act_sq, 1)
                root(NT)
                for k in range(0, KD, 2):
                    b = grab(("mT", k))
                    gave(("mT", k), A(hT[:, k, :], b[:, 0:T], ACT.Copy, scale=0.5))
                for g in range(2):
                    for h in range(2):
                        b = grab(("gb", g, h))
                        gave(("gb", g, h), A(gbc[:, g, h * HALF:(h + 1) * HALF], b[:, :], ACT.Copy))
                for t in range(NT):
                    act.wait_ge(x_ready, t + 1)
                    act.wait_ge(act_sq, 4 * NT + NIT + t)
                    A(gsq, x[:, t, :], ACT.Square, accum_out=st[:, 4, t:t + 1]).then_inc(act_sq, 1)
                    if t:
                        root(2 if t == 1 else 1)
                for h in range(2):
                    rows(5, h)
                act.wait_ge(mod1, 2)
                ahead(ACT.Exp)
                modulate("h2T", 1)
                act.wait_ge(ssm_out, (li + 1) * 64)
                act.wait_ge(aff_in, 1)
                A(aff[:, :, :], aff[:, :, :], ACT.Exp).then_inc(aff_exp, 1)
                b = grab(("affT",))
                gave(("affT",), A(affT, b[0:NE, 0:T], ACT.Copy))
                for g in range(2):
                    for h in range(2):
                        b = grab(("gb2", g, h))
                        gave(("gb2", g, h), A(gbc[:, g, h * HALF:(h + 1) * HALF], b[:, :], ACT.Copy))
                ahead(ACT.Silu)
                b = grab(("mk",))
                gave(("mk",), A(msk[:, :, :], b[:, 0:48].rearrange("p (t e) -> p t e", t=NT), ACT.Copy))
                XTe = XT[:, :, 0:6 * CE].rearrange("p k (e c) -> p k e c", c=CE)

                def gathered(e0, e1, turn_):
                    n = e1 - e0
                    if e0:
                        act.wait_ge(xc_ready, e0)
                    for k in range(0, KD, 2):
                        act.wait_ge(gath, KD * turn_ + k + 1)
                        A(XTe[:, k, 0:n, 0:CAP[0]], banks[6][:, 0:16 * n].rearrange("p (e c) -> p e c", e=n),
                          ACT.Identity, bias=modc[:, 2, k, 0:1], scale=gs[:, 1, k, 0:1])
                        A(XTe[:, k, 0:n, CAP[0]:CE], banks[6][:, 16 * n:48 * n].rearrange("p (e c) -> p e c", e=n),
                          ACT.Identity, bias=modc[:, 2, k, 1:2], scale=gs[:, 1, k, 1:2]).then_inc(gath_act, 1)

                def one_expert(e):
                    act.wait_ge(h3_ready, e + 2)
                    A(hs, banks[6][:, :], ACT.Silu).then_inc(silu_ready, 1)
                    act.wait_ge(ht_ready, e + 1)
                    A(hidT[:, :, :], banks[6][:, :].rearrange("p (b n) -> p b n", b=4), ACT.Copy).then_inc(hts_ready, 1)
                    act.wait_ge(yp_ready, e + 1)
                    A(yo, banks[7][:, :], ACT.Copy).then_inc(yo_ready, 1)

                A(yo, cst[:, 0:HALF], ACT.Copy, scale=0.0).then_inc(yo_ready, 1)
                for turn_, (e0, e1) in enumerate(STAGES):
                    gathered(e0, e1, turn_)
                    with act.Fori(e0, e1) as e:
                        one_expert(e)
                act.drain().then_inc(done_act, 1)
                act.wait_ge(layer_go, li + 1)
                act.sem_inc(dummy_act, 1)

        @block.vector
        def _(dve):
            V = nc.vector
            nbig = [0]
            own = [0]
            norms = [0]
            sqs = [0]

            def step(ins):
                ins.then_inc(dve_step, 1)
                own[0] += 1

            def settle():
                dve.wait_ge(dve_step, own[0])

            def link(ins):
                step(ins)
                settle()

            def grab(name):
                assert BIG_BY[name] == "dve"
                dve.wait_ge(big, BIG_AT[name] + 1)
                return banks[BIG_AT[name] % 4]

            def gave(name, ins):
                nbig[0] += 1
                assert taken_by(name) == ("dve", nbig[0]), name
                ins.then_inc(big_dve, 1)

            def rsqrt(ssq, n, width):
                var, root, y, c = (st[:, i, 0:n] for i in range(4))
                V.tensor_scalar(var, ssq, 1.0 / width, EPS, ALU.mult, ALU.add).then_inc(var_ready, 1)
                norms[0] += 1
                dve.wait_ge(root_ready, norms[0])
                dve.wait_ge(var_ready, norms[0])
                link(V.reciprocal(y, root))
                link(V.tensor_tensor(c, var, y, ALU.mult))
                link(V.tensor_tensor(c, c, y, ALU.mult))
                link(V.tensor_scalar(c, c, -0.5, 1.5, ALU.mult, ALU.add))
                link(V.tensor_tensor(y, y, c, ALU.mult))
                return y

            def norm_rows(t0, t1):
                sqs[0] += t1 - t0
                dve.wait_ge(act_sq, sqs[0])
                y = rsqrt(st[:, 4, t0:t1], t1 - t0, D)
                for t in range(t0, t1):
                    y = st[:, 2, t - t0:t - t0 + 1]
                    V.tensor_scalar(xn[:, t, :], x[:, t, :], y, None, ALU.mult).then_inc(xn_ready, 1)

            def modulate(name, which):
                for k in range(1, KD, 2):
                    b = grab((name, k))
                    V.tensor_scalar(hT[:, k, 0:P], b[:, 0:P], gs[:, which, k, 0:1], modc[:, 2 * which, k, 0:1],
                                    ALU.mult, ALU.add)
                    gave((name, k), V.tensor_scalar(hT[:, k, P:T], b[:, P:T], gs[:, which, k, 1:2],
                                                    modc[:, 2 * which, k, 1:2], ALU.mult, ALU.add))

            def head_norm(buf, heads, width, per_tile, gq_mul, ready, rotary):
                n = NT * heads
                for t in range(NT):
                    sqs[0] += 1
                    dve.wait_ge(act_sq, sqs[0])
                    V.tensor_reduce(st[:, 5, t * heads:(t + 1) * heads] if n <= 36 else stw[:, t * heads:(t + 1) * heads],
                                    tmp[:, t % 2, 0:heads * width].rearrange("p (h n) -> p h n", h=heads), AX.X, ALU.add)\
                        .then_inc(sq_free, 1)
                    per_tile[0] += 1
                dve.wait_ge(sq_free, per_tile[0])
                y = rsqrt(st[:, 5, 0:n] if n <= 36 else stw[:, 0:n], n, width)
                for t in range(NT):
                    step(V.tensor_tensor(buf(t), buf(t), rep(y[:, t * heads:(t + 1) * heads], 2, width), ALU.mult))
                settle()
                for t in range(NT):
                    for ins in gq_mul(t):
                        step(ins)
                settle()
                for t in (1, 2):
                    rotary(t)
                return None

            taken_sq = [0]
            dve.wait_ge(in_x, 32)
            with dve.Fori(0, DEPTH) as li:
                nbig[0] = own[0] = norms[0] = sqs[0] = taken_sq[0] = 0
                norm_rows(0, NT)
                dve.wait_ge(params_c, (li + 1) * 16)

                def columns(v):
                    n = (0, 1, None, 2, 3)[v]
                    b = grab(("col", v))
                    bias = cp[:, COLS["bada"][0] + 8 * n:COLS["bada"][0] + 8 * n + 8]
                    gave(("col", v), V.tensor_tensor(modc[:, n, :, :], b[:, 0:16].rearrange("p (k g) -> p k g", g=2),
                                                     rep(bias, 2, 2), ALU.add))
                    if v in (1, 4):
                        i = v // 3
                        dve.wait_ge(big_dve, nbig[0])
                        V.scalar_tensor_tensor(gs[:, i, :, :], modc[:, 2 * i + 1, :, :], 1.0,
                                               rep(cp[:, 8 * i:8 * i + 8], 2, 2), ALU.add, ALU.mult).then_inc(mod1, 1)
                        dve.wait_ge(mod1, i + 1)

                for v in range(2):
                    columns(v)
                modulate("hT", 0)
                dve.wait_ge(params, (li + 1) * 48)
                dve.wait_ge(in_cst, 16)
                link(V.tensor_tensor(lamt, r_("lamq"), r_("lamk"), ALU.mult))
                step(V.tensor_scalar(nsink, r_("sink"), -1.0, None, ALU.mult))
                V.tensor_reduce(lamd, lamt.rearrange("p (i n) -> p i n", i=2), AX.X, ALU.add).then_inc(lam_dot, 1)

                def ab_gain(t):
                    q = AB[:, t, :, 0:256].rearrange("p b (h d) -> p b h d", h=4)
                    k = AB[:, t, :, 256:384].rearrange("p b (h d) -> p b h d", h=2)
                    return [V.tensor_tensor(q, q, rep(gqc, 2, 4), ALU.mult), V.tensor_tensor(k, k, rep(gkc, 2, 2), ALU.mult)]

                def turner(buf, heads, width, cosn, sinn, last, sem_):
                    def rotary(t):
                        n = width // 4
                        v = buf(t)
                        cs_ = c_(cosn)[:, (t - 1) * width:t * width]
                        sn_ = c_(sinn)[:, (t - 1) * width:t * width].rearrange("p (a h n) -> p a h n", a=2, h=2)
                        v5 = v.rearrange("p h (a c n) -> p h a c n", a=2, c=2)
                        o5 = tmp[:, 1, 0:heads * width].rearrange("p (h a c n) -> p h a c n", h=heads, a=2, c=2)
                        for c in range(2):
                            step(V.tensor_tensor(o5[:, :, :, c, :], v5[:, :, :, 1 - c, :], rep(sn_[:, :, c, :], 1, heads), ALU.mult))
                        settle()
                        link(V.tensor_tensor(v, v, rep(cs_, 1, heads), ALU.mult))
                        ins = V.tensor_tensor(v, v, tmp[:, 1, 0:heads * width].rearrange("p (h n) -> p h n", h=heads), ALU.add)
                        if t == last:
                            ins.then_inc(sem_, 1)
                            dve.wait_ge(sem_, 1)
                        else:
                            link(ins)
                    return rotary

                abuf = lambda t: AB[:, t, :, :].rearrange("p b (h d) -> p (b h) d", d=HD)
                head_norm(abuf, 12, HD, taken_sq, ab_gain, ab_ready, turner(abuf, 12, HD, "cos", "sin", 2, ab_ready))

                dve.wait_ge(big_act, taken_by(("dqk", 2))[1])
                link(V.tensor_tensor(dtr, dtr, rep(r_("dtb"), 1, NT), ALU.add))
                V.scalar_tensor_tensor(dabs, dtr, -1.0, dtr, ALU.mult, ALU.min).then_inc(dt_abs, 1)

                def d_gain(t):
                    q = DQ[:, t, 0:256].rearrange("p (h d) -> p h d", h=8)
                    k = DQ[:, t, 256:512].rearrange("p (h d) -> p h d", h=8)
                    return [V.tensor_tensor(q, q, rep(r_("gqd"), 1, 8), ALU.mult), V.tensor_tensor(k, k, rep(r_("gkd"), 1, 8), ALU.mult)]

                dbuf = lambda t: DQ[:, t, :].rearrange("p (h d) -> p h d", h=16)
                head_norm(dbuf, 16, 32, taken_sq, d_gain, d_ready, turner(dbuf, 16, 32, "cosd", "sind", 2, d_ready))

                dve.wait_ge(dt_log, 1)
                link(V.scalar_tensor_tensor(dt_, dtr, 0.0, dexp, ALU.max, ALU.add))
                V.scalar_tensor_tensor(la, dt_, -1.0, rep(expa, 1, NT), ALU.mult, ALU.mult).then_inc(dt_done, 1)
                dve.wait_ge(lam_exp, 1)
                link(V.tensor_tensor(nlam, lamx[:, 1:2], lamx[:, 0:1], ALU.subtract))
                link(V.tensor_tensor(nlam, nlam, r_("laminit"), ALU.subtract))

                dve.wait_ge(big_act, taken_by(("xbc", 3))[1])
                cw = cp[:, COLS["convw"][0]:COLS["convw"][1]].rearrange("p (g k) -> p g k", g=4)
                for k in range(5):
                    for g in range(4):
                        if k == 0:
                            step(V.tensor_scalar(cacc[:, g, :], xbc[:, g, 0:NU_CONV], cw[:, g, 0:1], None, ALU.mult))
                        else:
                            ins = V.scalar_tensor_tensor(cacc[:, g, :], xbc[:, g, k:k + NU_CONV], cw[:, g, k:k + 1],
                                                         cacc[:, g, :], ALU.mult, ALU.add)
                            if k == 4:
                                ins.then_inc(conv_sum, 1)
                            else:
                                step(ins)
                    if k < 4:
                        settle()

                def lift(i, then=None):
                    for c in range(2):
                        b = grab(("boT", i, c))
                        gave(("boT", i, c), V.tensor_copy(boT[:, c, :], b[:, 0:T]))
                    if then:
                        then()
                    for t in range(NT):
                        for h in range(2):
                            b = grab(("up", i, t, h))
                            g = G[i % 2][:, t, h * HALF:(h + 1) * HALF]
                            m = xn[:, t, h * HALF:(h + 1) * HALF]
                            if i == 0:
                                dve.wait_ge(big_act, taken_by(("g", 0, t, h))[1])
                                gave(("up", i, t, h), V.scalar_tensor_tensor(m, g, 1.0, b[:, :], ALU.add, ALU.mult))
                            else:
                                dve.wait_ge(big_act, taken_by(("g", i, t, h))[1])
                                gave(("up", i, t, h), V.scalar_tensor_tensor(g, g, 1.0, b[:, :], ALU.add, ALU.mult))
                                dve.wait_ge(big_dve, nbig[0])
                                V.tensor_tensor(m, m, g, ALU.add).then_inc(merged, 1)

                def maximum(i, n):
                    h, t = iters(i)[n]
                    nk = P if t == 0 else T
                    q = 2 * (n % 4)
                    dve.wait_ge(s_ready, i * NIT + n + 1)
                    mx, nb = st[:, 0, q:q + 2], st[:, 1, q:q + 2]
                    if i < 2:
                        link(V.tensor_reduce(mx[:, 0:1], banks[4 + n % 2][:, 0:nk], AX.X, ALU.max))
                    else:
                        for m in range(2):
                            step(V.tensor_reduce(mx[:, m:m + 1], banks[4 + m][:, 0:nk], AX.X, ALU.max))
                        settle()
                    if i == 0:
                        ins = V.tensor_scalar(nb[:, 0:1], mx[:, 0:1], -(HD ** -0.5), None, ALU.mult)
                    elif i == 1:
                        ins = V.tensor_scalar(nb[:, 0:1], mx[:, 0:1], -(HD ** -0.5), nsink[:, h:h + 1], ALU.mult, ALU.min)
                    else:
                        ins = V.tensor_scalar(nb, mx, -(32 ** -0.5), None, ALU.mult)
                    ins.then_inc(m_ready, 1)

                maximum(0, 0)
                for i in range(3):
                    its = iters(i)
                    for n in range(NIT + 2):
                        if 1 <= n < NIT and i < 2:
                            maximum(i, n)
                        if 1 <= n <= NIT:
                            h, t = its[n - 1]
                            nk = P if t == 0 else T
                            q = 2 * ((n - 1) % 4)
                            dve.wait_ge(p_ready, i * NIT + n)
                            sums, rs = st[:, 2, q:q + 2], st[:, 3, q:q + 2]
                            if i == 1:
                                link(V.tensor_tensor(sums[:, 0:1], sums[:, 0:1], st[:, 4, q:q + 1], ALU.add))
                            if i < 2:
                                step(V.reciprocal(rs[:, 0:1], sums[:, 0:1]))
                            else:
                                link(V.reciprocal(rs, sums))
                                link(V.tensor_tensor(rs[:, 1:2], rs[:, 1:2], nlam, ALU.mult))
                                p0, p1 = pr[:, (n - 1) % 2, 0:nk], pr[:, (n - 1) % 2, T:T + nk]
                                link(V.tensor_scalar(p1, p1, rs[:, 1:2], None, ALU.mult))
                                V.scalar_tensor_tensor(p0, p0, rs[:, 0:1], p1, ALU.mult, ALU.add).then_inc(w_ready, 1)
                        if 1 <= n < NIT and i == 2:
                            maximum(i, n)
                        if n >= 2:
                            h, t = its[n - 2]
                            q = 2 * ((n - 2) % 4)
                            settle()
                            dve.wait_ge(pv_ready, i * NIT + n - 1)
                            if i == 0 and n == 2:
                                dve.wait_ge(kv_out, (li + 1) * 96)
                            out = bo[:, t, h * HD:(h + 1) * HD]
                            if i < 2:
                                V.tensor_scalar(out, banks[7][:, 0:HD], st[:, 3, q:q + 1], None, ALU.mult).then_inc(o_ready, 1)
                            else:
                                V.tensor_copy(out, banks[7][:, 0:HD]).then_inc(o_ready, 1)
                    if i == 2:
                        dve.wait_ge(o_ready, 3 * NIT)
                        sqs[0] += NIT
                        dve.wait_ge(act_sq, sqs[0])
                        y = rsqrt(st[:, 5, 0:12], 12, HD)
                        link(V.tensor_scalar(y, y, r_("onemlam"), None, ALU.mult))
                        b4 = bo[:, :, :].rearrange("p t (h n) -> p (t h) n", n=HD)
                        link(V.tensor_tensor(b4, b4, rep(y, 2, HD), ALU.mult))
                        V.tensor_tensor(b4, b4, rep(r_("gdout"), 1, 12), ALU.mult).then_inc(bo_ready, 1)
                    else:
                        maximum(i + 1, 0)
                        lift(i)

                b = grab(("cum",))
                cum = b[:, 0:48].rearrange("p (t i j) -> p i t j", t=NT, i=2)
                step(V.tensor_copy(sm[:, 0, :, :], cum[:, 0, :, :]))
                step(V.tensor_copy(sm[:, 2, :, :], cum[:, 1, :, :]))
                gave(("cum",), V.tensor_scalar(nacs, cum[:, 0, :, :], -1.0, None, ALU.mult))
                settle()
                V.tensor_tensor(sm[:, 1, :, :], sm[:, 2, :, :], sm[:, 0, :, :], ALU.subtract).then_inc(ssd_small, 1)
                dve.wait_ge(big_dve, nbig[0])
                ea, te, dcy = ex[:, 0, :, :], ex[:, 1, :, :], ex[:, 2, :, :]

                def channels(t):
                    return xsB[:, t, 0:256].rearrange("p (h n) -> p h n", h=4)

                def ssd_inputs(t):
                    for d in range(2):
                        step(V.tensor_tensor(xdt[:, t % 2, d, :, :], channels(t), rep(dt_[:, t, 4 * d:4 * d + 4], 2, HD),
                                             ALU.mult))

                def ssd_decayed(t):
                    settle()
                    step(V.tensor_tensor(xde.rearrange("p d h n -> p (d h) n"),
                                         xdt[:, t % 2].rearrange("p d h n -> p (d h) n"), rep(te[:, t, :], 2, HD), ALU.mult))

                def skips():
                    for t in range(NT):
                        step(V.tensor_tensor(bo[:, t, :].rearrange("p (h n) -> p h n", h=4), channels(t),
                                             rep(r_("dskip"), 2, HD), ALU.mult))

                dve.wait_ge(big_act, taken_by(("uT", 2))[1])
                dve.wait_ge(ssd_exp, 1)
                ssd_inputs(0)
                ssd_decayed(0)
                lift(2, skips)
                for t in range(NT):
                    if t:
                        ssd_decayed(t)
                    dve.wait_ge(big_act, taken_by(("dec", t, 1))[1])
                    E4 = E.rearrange("p (d h) l -> p d h l", d=2)
                    M4 = Mt.rearrange("p (d h) l -> p d h l", d=2)
                    for g in range(2):
                        b = grab(("GT", t, g))
                        gave(("GT", t, g), V.tensor_tensor(M4[:, :, 2 * g:2 * g + 2, :], E4[:, :, 2 * g:2 * g + 2, :],
                                                           rep(rep(b[:, 0:P], 1, 2), 1, 2), ALU.mult))
                    settle()
                    dve.wait_ge(big_dve, nbig[0])
                    V.tensor_copy(xmark, dt_[:, 0, 0:1]).then_inc(mt_ready, 1)
                    if t + 1 < NT:
                        ssd_inputs(t + 1)
                    if t:
                        dve.wait_ge(sty_ready, 2 * t + 1)
                        d, src, dst = t - 1, 2 * (t - 1), 2 * (t - 1) + 1
                        for g in range(2):
                            r = slice(g * HD, (g + 1) * HD)
                            hh = hin[r, dst, :].rearrange("p (h n) -> p h n", h=2)
                            step(V.tensor_tensor(hh, hin[r, src, :].rearrange("p (h n) -> p h n", h=2),
                                                 rep(dcy[r, t, 4 * d + 2 * g:4 * d + 2 * g + 2], 2, HD), ALU.mult))
                        settle()
                        step(V.tensor_tensor(hin[:, dst, :], hin[:, dst, :], banks[4][:, 0:P], ALU.add))
                        settle()
                    dve.wait_ge(sty_ready, 2 * t + 2)
                    V.tensor_tensor(bo[:, t, :], bo[:, t, :], banks[5][:, 0:256], ALU.add).then_inc(y_taken, 1)
                    dve.wait_ge(y_taken, t + 1)
                V.tensor_copy(xmark, dt_[:, 0, 0:1]).then_inc(h_in, 1)
                for t in range(NT):
                    if t:
                        yt = at(po + 512 * (t - 1), 512)
                        for g in range(2):
                            b = grab(("yo", t, g))
                            gave(("yo", t, g), V.tensor_tensor(
                                yt.rearrange("p (d g h n) -> p g d h n", d=2, g=2, h=2)[:, g],
                                b[:, 0:256].rearrange("p (d h n) -> p d h n", d=2, h=2),
                                rep(ea[:, t, :].rearrange("p (d g h) -> p g d h", d=2, g=2)[:, g], 3, HD), ALU.mult))
                        dve.wait_ge(big_dve, nbig[0])
                        for d in range(2):
                            link(V.tensor_tensor(bo[:, t, :], bo[:, t, :], yt[:, d * 256:(d + 1) * 256], ALU.add))
                    V.tensor_tensor(bo[:, t, :], bo[:, t, :], sz[:, t, :], ALU.mult).then_inc(u_ready, 1)
                sqs[0] += NT
                dve.wait_ge(act_sq, sqs[0])
                dve.wait_ge(u_ready, NT)
                y = rsqrt(st[:, 5, 0:NT], NT, 256)
                for t in range(NT):
                    ins = V.scalar_tensor_tensor(bo[:, t, :], bo[:, t, :], y[:, t:t + 1], r_("gssm"), ALU.mult, ALU.mult)
                    if t == NT - 1:
                        ins.then_inc(bo_ready, 1)
                    else:
                        step(ins)
                settle()
                columns(3)
                lift(3)
                columns(4)

                for k in range(1, KD, 2):
                    b = grab(("mT", k))
                    gave(("mT", k), V.tensor_scalar(hT[:, k, :], b[:, 0:T], 0.5, None, ALU.mult))
                dve.wait_ge(big_act, taken_by(("gb", 1, 1))[1])
                for t in range(NT):
                    for h in range(2):
                        b = grab(("out", t, h))
                        cols = slice(h * HALF, (h + 1) * HALF)
                        gave(("out", t, h), V.tensor_tensor(gtmp[:, h, :], b[:, :], gbc[:, min(t, 1), cols], ALU.mult))
                        dve.wait_ge(big_dve, nbig[0])
                        ins = V.tensor_tensor(x[:, t, cols], x[:, t, cols], gtmp[:, h, :], ALU.add)
                        if h:
                            ins.then_inc(x_ready, 1)
                        else:
                            step(ins)
                    settle()
                    if t == 1:
                        norm_rows(0, 2)
                norm_rows(2, 3)
                modulate("h2T", 1)
                dve.wait_ge(ssm_out, (li + 1) * 64)
                b = grab(("lg",))
                lg = b[:, 0:48].rearrange("p (t e) -> p t e", t=NT)
                link(V.tensor_reduce(st[:, 0, 0:NT], lg, AX.X, ALU.max))
                gave(("lg",), V.tensor_tensor(aff[:, :, :], lg, rep(st[:, 0, 0:NT], 2, NE), ALU.subtract))
                dve.wait_ge(big_dve, nbig[0])
                V.tensor_copy(xmark, dt_[:, 0, 0:1]).then_inc(aff_in, 1)
                dve.wait_ge(aff_exp, 1)
                link(V.tensor_reduce(st[:, 1, 0:NT], aff[:, :, :], AX.X, ALU.add))
                link(V.reciprocal(st[:, 2, 0:NT], st[:, 1, 0:NT]))
                V.tensor_tensor(aff[:, :, :], aff[:, :, :], rep(st[:, 2, 0:NT], 2, NE), ALU.mult).then_inc(aff_ready, 1)
                dve.wait_ge(big_act, taken_by(("affT",))[1])
                for n in range(CAP[1] // 8):
                    groups = [(0, 0, P)] * (n < CAP[0] // 8) + [(1, P, T)]
                    src = affT if n == 0 else wrk
                    for i, c0, c1 in groups:
                        step(V.max(top8[:, 8 * i:8 * i + 8], src[:, c0:c1]))
                    settle()
                    for i, c0, c1 in groups:
                        step(V.match_replace(wrk[:, c0:c1], top8[:, 8 * i:8 * i + 8], src[:, c0:c1], -1.0))
                    settle()
                V.tensor_scalar(maskT, wrk, 0.0, None, ALU.is_lt).then_inc(mask_ready, 1)
                for n in {e1 - e0 for e0, e1 in STAGES}:
                    step(V.memset(XT[:, :, n * CE:n * CE + 16], 0.0))
                V.memset(sgT[:, :, :], 0.0).then_inc(sgs_ready, 1)
                b = grab(("rank",))
                rk = b[:, 0:48].rearrange("p (t e) -> p t e", t=NT)
                step(V.tensor_tensor(pos[:, 0, :], rk[:, 0, :], msk[:, 0, :], ALU.mult))
                gave(("rank",), V.scalar_tensor_tensor(pos[:, 1:3, :], rk[:, 1:3, :], float(CAP[0]), msk[:, 1:3, :],
                                                       ALU.add, ALU.mult))
                settle()
                dve.wait_ge(big_dve, nbig[0])
                link(V.tensor_scalar(pos[:, :, :], pos[:, :, :], -1.0, None, ALU.add))
                iota = c_("iota")
                V.tensor_tensor(Sc[:, :, :], rep(iota[:, 0:CAP[0]], 1, NE), rep(pos[:, 0, :], 2, CAP[0]), ALU.is_equal)\
                    .then_inc(sc_ready, 1)
                step(V.tensor_tensor(Sl[:, 0, :, :], rep(iota[:, CAP[0]:CE], 1, NE), rep(pos[:, 1, :], 2, CAP[1]), ALU.is_equal))
                settle()
                V.tensor_tensor(Sl[:, 1, :, :], rep(iota[:, CAP[0]:CE], 1, NE), rep(pos[:, 2, :], 2, CAP[1]), ALU.is_equal)\
                    .then_inc(hot_ready, 1)
                XTe = XT[:, :, 0:6 * CE].rearrange("p k (e c) -> p k e c", c=CE)

                def gathered(e0, e1, turn_):
                    n = e1 - e0
                    if e0:
                        dve.wait_ge(xc_ready, e0)
                    for k in range(1, KD, 2):
                        dve.wait_ge(gath, KD * turn_ + k + 1)
                        step(V.tensor_scalar(XTe[:, k, 0:n, 0:CAP[0]],
                                             banks[7][:, 0:16 * n].rearrange("p (e c) -> p e c", e=n),
                                             gs[:, 1, k, 0:1], modc[:, 2, k, 0:1], ALU.mult, ALU.add))
                        V.tensor_scalar(XTe[:, k, 0:n, CAP[0]:CE],
                                        banks[7][:, 16 * n:48 * n].rearrange("p (e c) -> p e c", e=n),
                                        gs[:, 1, k, 1:2], modc[:, 2, k, 1:2], ALU.mult, ALU.add).then_inc(gath_dve, 1)
                    settle()
                    dve.wait_ge(gath_dve, KD // 2 * (turn_ + 1))
                    dve.wait_ge(gath_act, KD // 2 * (turn_ + 1))

                def one_expert(e, e0):
                    dve.wait_ge(h3_ready, e + 1)
                    V.tensor_copy(xcur[:, :, :], XT[:, :, bass.ds((e - e0) * CE, 64)]).then_inc(xc_ready, 1)
                    dve.wait_ge(sg_ready, e + 1)
                    for t in range(NT):
                        ins = V.tensor_scalar(sgs[:, t, :], iota, pos[:, t, bass.ds(e, 1)], aff[:, t, bass.ds(e, 1)],
                                              ALU.is_equal, ALU.mult)
                    ins.then_inc(w1hot, 1)
                    dve.wait_ge(silu_ready, e + 1)
                    V.tensor_tensor(hid.rearrange("p b n -> p (b n)"), hs, banks[7][:, :], ALU.mult).then_inc(hid_ready, 1)
                    dve.wait_ge(sg_ready, e + 2)
                    V.tensor_copy(sgT.rearrange("p t c -> p (t c)"), banks[6][:, 0:T]).then_inc(sgs_ready, 1)

                for turn_, (e0, e1) in enumerate(STAGES):
                    gathered(e0, e1, turn_)
                    with dve.Fori(e0, e1) as e:
                        one_expert(e, e0)
                for t in range(NT):
                    for h in range(2):
                        dve.wait_ge(closed, 2 * t + h + 1)
                        cols = slice(h * HALF, (h + 1) * HALF)
                        link(V.tensor_tensor(gtmp[:, h, :], banks[2 * t + h][:, :], gbc[:, min(t, 1), cols], ALU.mult))
                        ins = V.tensor_tensor(x[:, t, cols], x[:, t, cols], gtmp[:, h, :], ALU.add)
                        if h:
                            ins.then_inc(x_final, 1)
                        else:
                            link(ins)
                dve.wait_ge(x_final, NT * (li + 1))
                dve.sem_inc(dummy_dve, 1)
                dve.drain().then_inc(done_dve, 1)
                dve.wait_ge(layer_go, li + 1)
                dve.sem_inc(dummy_dve, 1)


_OUTS = [((1, 128, 1024), "float32"), ((1, 256, 1024), "float32"),
         ((1, 2, 128, 2, 64), "float32"), ((1, 2, 128, 2, 64), "float32"),
         ((1, 2, 128, 2, 64), "float32"), ((1, 2, 128, 2, 64), "float32"),
         ((1, 2, 2, 4, 64, 64), "float32"),
         ((1, 2, 128, 4, 2, 32), "float32"), ((1, 2, 128, 4, 64), "float32")]


def constants():
    import numpy as np
    c = np.zeros((P, NCST), np.float32)

    def put(name, a):
        c[:, CST[name][0]:CST[name][1]] = a

    i = np.arange(P)
    put("ident", np.eye(P))
    put("upto", i[:, None] <= i[None, :])
    put("from", i[:, None] >= i[None, :])
    put("negbelow", np.where(i[None, :] < i[:, None], -1e30, 0.0))
    put("negabove", np.where(i[None, :] > i[:, None], -1e30, 0.0))
    put("ones", 1.0)
    put("sel", (i[:, None] % 32) == np.arange(2)[None, :])
    put("selb", np.repeat(((i[:, None] % 32) == np.arange(2)[None, :]) | (i[:, None] == 2), P, axis=1))
    put("iota", np.tile(np.arange(64), 2)[None, :])
    for width, cn, sn in ((64, "cos", "sin"), (32, "cosd", "sind")):
        n = width // 4
        inv = np.float32(10000.0) ** (-np.arange(n, dtype=np.float32) / np.float32(n))
        inv = inv.astype(np.float32)
        tok = np.arange(256)
        ang = np.stack([(tok // 64)[:, None].astype(np.float32) * inv, (tok % 64)[:, None].astype(np.float32) * inv], 1)
        cos, sin = np.cos(ang), np.sin(ang)
        full_c = np.stack([cos, cos], 2).reshape(2, P, width)
        full_s = np.stack([-sin, sin], 2).reshape(2, P, width)
        put(cn, full_c.transpose(1, 0, 2).reshape(P, 2 * width))
        put(sn, full_s.transpose(1, 0, 2).reshape(P, 2 * width))
    return c


def kernel(**inputs):
    import math

    import numpy as _np
    import concourse.bacc as _bacc
    from concourse.bass_utils import run_bass_kernel_spmd as _run

    n = {k: _np.asarray(v) for k, v in inputs.items()}
    f32 = _np.float32
    init = [0.8 - 0.6 * math.exp(-0.3 * i) for i in range(DEPTH)]
    rows = [n["g_qa"], n["g_qb"], n["g_ka"], n["g_kb"], n["g_qd"], n["g_kd"], n["g_dout"], n["lam_q1"], n["lam_q2"],
            n["lam_k1"], n["lam_k2"], n["sink_b"], n["a_log"].reshape(DEPTH, 8), n["dt_bias"].reshape(DEPTH, 8),
            n["d_skip"], n["g_ssm"], _np.array(init, f32)[:, None], (1 - _np.array(init))[:, None].astype(f32)]
    cols = [n["g_norm1"].reshape(DEPTH, KD, P).transpose(0, 2, 1), n["g_norm2"].reshape(DEPTH, KD, P).transpose(0, 2, 1),
            n["conv_w"].reshape(DEPTH, 5, 4, P).transpose(0, 3, 2, 1).reshape(DEPTH, P, 20),
            n["conv_b"].reshape(DEPTH, 4, P).transpose(0, 2, 1),
            n["b_ada"].reshape(DEPTH, 6, KD, P)[:, [0, 1, 3, 4]].reshape(DEPTH, 4 * KD, P).transpose(0, 2, 1)]
    ssm = n["state_ssm"][0].reshape(DEPTH, 2, 2, 2, 64, 64).transpose(0, 3, 4, 1, 2, 5).reshape(DEPTH, P, 256)
    cache = [n["cache_" + k][0].reshape(DEPTH, P, -1) for k in ("a_k", "b_k", "a_v", "b_v", "d_k", "d_v")] + [ssm]
    cvec = _np.stack([n["c_ctx"], n["c"][0]], axis=-1).reshape(KD, P, 2).transpose(1, 0, 2)
    arrays = {
        "x_prompt": n["x_prompt"], "x_sample": n["x_sample"], "cvecT": cvec, "rowp": _np.concatenate(rows, axis=1),
        "colp": _np.concatenate(cols, axis=2), "caches": _np.concatenate(cache, axis=2), "b_ada": n["b_ada"],
        "w_ada": n["w_ada"], "w_in": n["w_in"], "w_br": n["w_br"], "w_out": n["w_out"], "w_router": n["w_router"],
        "w_e1": n["w_e1"], "w_e3": n["w_e3"], "w_e2": n["w_e2"], "consts": constants(),
    }
    nc = _bacc.Bacc("TRN2", target_bir_lowering=False, num_devices=1)
    sent, args = {}, []
    for name, a in arrays.items():
        sent[f"in_{name}"] = _np.ascontiguousarray(a)
        args.append(nc.dram_tensor(f"in_{name}", a.shape, mybir.dt.from_np(a.dtype), kind="ExternalInput").ap())
    for i, (shape, dtype) in enumerate(_OUTS):
        args.append(nc.dram_tensor(f"out_{i}", shape, mybir.dt.from_np(_np.dtype(dtype)), kind="ExternalOutput").ap())
    trunk_kernel(nc, *args)
    r = _run(nc, [sent], core_ids=[0])
    return tuple(r.results[0][f"out_{i}"] for i in range(len(_OUTS)))
```
